# Optimizing a Trainium2 kernel written in Bass

```python
import math
import jax, jax.numpy as jnp
from jax import lax
import numpy as np

D_MODEL = 1024
BATCH = 1
SEQ = 1024
DEPTH = 2
DEC_BATCH = 8
DEC_SEQ = 8
PAST_LEN = 256
PAGE_SIZE = 128

N_A = DEPTH // 2
N_B = DEPTH - N_A
RET_HEADS = 8
RET_DK = D_MODEL // RET_HEADS
RET_DV = 2 * RET_DK
RET_QK_W = RET_HEADS * RET_DK
RET_V_W = RET_HEADS * RET_DV
RET_IN_W = 2 * RET_QK_W + 2 * RET_V_W
RET_CHUNK = 128
ROPE_BASE = 10000.0
SB_HEADS = 16
SB_DH = D_MODEL // SB_HEADS
SB_W = SB_HEADS * SB_DH
SB_IN_W = 2 * SB_W
SB_QBLOCK = 128
SB_BIAS_INIT = -6.0
EPS = 1e-6

kernel_name = "yoco_retention_stickbreaking_step"

F32 = jnp.float32

def rmsnorm(x, g):
    xf = x.astype(F32)
    return xf * lax.rsqrt(jnp.mean(xf * xf, axis=-1, keepdims=True) + EPS) * g.astype(F32)

def modulate(x, c, g, w, b):
    m = jax.nn.silu(c) @ w + b
    shift, scale, gate = jnp.split(m.astype(F32), 3, axis=-1)
    h = rmsnorm(x, g) * (1.0 + scale[:, None, :]) + shift[:, None, :]
    return h, gate[:, None, :]

def rotary(x, pos):
    half = x.shape[-1] // 2
    inv_freq = ROPE_BASE ** (-jnp.arange(half, dtype=F32) / half)
    ang = pos.astype(F32)[:, None] * inv_freq[None, :]
    cos = jnp.cos(ang)[None, :, None, :]
    sin = jnp.sin(ang)[None, :, None, :]
    x1, x2 = x[..., :half], x[..., half:]
    return jnp.concatenate([x1 * cos - x2 * sin, x1 * sin + x2 * cos], axis=-1)

def retention(q, k, v, s0):
    B, L, H, dk = q.shape
    dv = v.shape[-1]
    C = math.gcd(L, RET_CHUNK)
    n = L // C
    log_gamma = jnp.log1p(-jnp.exp2(-5.0 - jnp.arange(H, dtype=F32)))
    idx = jnp.arange(C, dtype=F32)
    diff = idx[:, None] - idx[None, :]
    decay_mask = jnp.where(diff[None] >= 0, jnp.exp(log_gamma[:, None, None] * jnp.maximum(diff, 0.0)[None]), 0.0)
    q_dec = jnp.exp(log_gamma[None, :] * (idx[:, None] + 1.0))[None, :, :, None]
    k_dec = jnp.exp(log_gamma[None, :] * (C - 1.0 - idx[:, None]))[None, :, :, None]
    chunk_dec = jnp.exp(log_gamma * C)[None, :, None, None]

    def chunks(t):
        return jnp.moveaxis(t.reshape(B, n, C, H, t.shape[-1]), 1, 0)

    def body(S, xs):
        qc, kc, vc = xs
        scores = jnp.einsum('bihd,bjhd->bhij', qc, kc) * decay_mask[None]
        intra = jnp.einsum('bhij,bjhe->bihe', scores, vc)
        cross = jnp.einsum('bihd,bhde->bihe', qc * q_dec, S)
        S_new = S * chunk_dec + jnp.einsum('bjhd,bjhe->bhde', kc * k_dec, vc)
        return S_new, intra + cross

    s_final, outs = lax.scan(body, s0, (chunks(q), chunks(k), chunks(v)))
    return jnp.moveaxis(outs, 0, 1).reshape(B, L, H, dv), s_final

def stick_breaking(q, k, v, q_pos, k_pos, bias):
    B, L, H, d = q.shape
    Qb = math.gcd(L, SB_QBLOCK)
    nb = L // Qb
    qb = jnp.moveaxis(q.reshape(B, nb, Qb, H, d), 1, 0)
    pb = q_pos.reshape(nb, Qb)
    scale = d ** -0.5
    bias_f = bias.astype(F32)[None, :, None, None]

    def block(args):
        qi, pi = args
        z = jnp.einsum('bqhd,bkhd->bhqk', qi, k).astype(F32) * scale + bias_f
        mask = (k_pos[None, :] < pi[:, None])[None, None]
        log_keep = jnp.where(mask, jax.nn.log_sigmoid(-z), 0.0)
        tail = lax.cumsum(log_keep, axis=3, reverse=True)
        tail_excl = jnp.concatenate([tail[..., 1:], jnp.zeros_like(tail[..., :1])], axis=-1)
        w = jnp.where(mask, jnp.exp(jax.nn.log_sigmoid(z) + tail_excl), 0.0)
        return jnp.einsum('bhqk,bkhd->bqhd', w, v)

    o = lax.map(block, (qb, pb))
    return jnp.moveaxis(o, 0, 1).reshape(B, L, H, d)

def retention_layer(h, pos, s0, w_in, norm_g, w_out):
    B, L, _ = h.shape
    proj = h @ w_in
    q, k, v, g = jnp.split(proj, [RET_QK_W, 2 * RET_QK_W, 2 * RET_QK_W + RET_V_W], axis=-1)
    q = rotary(q.reshape(B, L, RET_HEADS, RET_DK), pos)
    k = rotary(k.reshape(B, L, RET_HEADS, RET_DK) * (RET_DK ** -0.5), pos)
    v = v.reshape(B, L, RET_HEADS, RET_DV)
    o, s_new = retention(q, k, v, s0)
    o = rmsnorm(o, norm_g.reshape(RET_HEADS, RET_DV)).reshape(B, L, RET_V_W)
    return (jax.nn.silu(g) * o) @ w_out, s_new

def shared_kv(x, kv_norm_g, w_kv, sb_k_g):
    B, L, _ = x.shape
    kv = rmsnorm(x, kv_norm_g) @ w_kv
    k, v = jnp.split(kv, 2, axis=-1)
    k = rmsnorm(k.reshape(B, L, SB_HEADS, SB_DH), sb_k_g)
    return k, v.reshape(B, L, SB_HEADS, SB_DH)

def sb_layer(h, pos, k_all, v_all, k_pos, w_in, q_g, bias, w_out):
    B, L, _ = h.shape
    q, g = jnp.split(h @ w_in, 2, axis=-1)
    q = rmsnorm(q.reshape(B, L, SB_HEADS, SB_DH), q_g)
    o = stick_breaking(q, k_all, v_all, pos, k_pos, bias).reshape(B, L, SB_W)
    return (jax.nn.silu(g) * o) @ w_out

def trunk(x, c, pos, ret_state, past_k, past_v,
          ada_w, ada_b, norm_g, ret_w_in, ret_norm_g, ret_w_out,
          kv_norm_g, w_kv, sb_q_g, sb_k_g, sb_w_in, sb_w_out, sb_bias):
    x = x.astype(F32)
    c = c.astype(F32)
    B = x.shape[0]
    new_states = []
    for l in range(N_A):
        h, gate = modulate(x, c, norm_g[l], ada_w[l], ada_b[l])
        if ret_state is None:
            s0 = jnp.zeros((B, RET_HEADS, RET_DK, RET_DV), F32)
        else:
            s0 = ret_state[l].astype(F32)
        y, s_new = retention_layer(h, pos, s0, ret_w_in[l], ret_norm_g[l], ret_w_out[l])
        x = x + gate * y
        new_states.append(s_new)
    k_new, v_new = shared_kv(x, kv_norm_g, w_kv, sb_k_g)
    if past_k is None:
        k_all, v_all, k_pos = k_new, v_new, pos
    else:
        past_len = past_k.shape[1]
        k_all = jnp.concatenate([past_k.astype(F32), k_new], axis=1)
        v_all = jnp.concatenate([past_v.astype(F32), v_new], axis=1)
        k_pos = jnp.concatenate([jnp.arange(past_len, dtype=jnp.int32), pos])
    for j in range(N_B):
        l = N_A + j
        h, gate = modulate(x, c, norm_g[l], ada_w[l], ada_b[l])
        y = sb_layer(h, pos, k_all, v_all, k_pos, sb_w_in[j], sb_q_g[j], sb_bias[j], sb_w_out[j])
        x = x + gate * y
    return x, jnp.stack(new_states), k_new, v_new

def setup_inputs(seed: int = 0) -> dict:
    key = jax.random.key(seed)
    ks = jax.random.split(key, 24)
    n_pages = PAST_LEN // PAGE_SIZE
    n_used = DEC_BATCH * n_pages
    n_pool = n_used + max(n_used // 4, 1)
    nrm = jax.random.normal
    page_table = jax.random.permutation(ks[0], n_pool)[:n_used].reshape(DEC_BATCH, n_pages).astype(jnp.int32)
    return {
        "x_prompt": nrm(ks[1], (BATCH, SEQ, D_MODEL), F32),
        "x_sample": nrm(ks[2], (DEC_BATCH, DEC_SEQ, D_MODEL), F32),
        "state_ret": 0.1 * nrm(ks[3], (N_A, DEC_BATCH, RET_HEADS, RET_DK, RET_DV), F32),
        "cache_k": nrm(ks[4], (n_pool, PAGE_SIZE, SB_HEADS, SB_DH), F32),
        "cache_v": nrm(ks[5], (n_pool, PAGE_SIZE, SB_HEADS, SB_DH), F32),
        "page_table": page_table,
        "c_prompt": nrm(ks[6], (BATCH, D_MODEL), F32),
        "c_sample": nrm(ks[7], (DEC_BATCH, D_MODEL), F32),
        "ada_w": nrm(ks[8], (DEPTH, D_MODEL, 3 * D_MODEL), F32) * D_MODEL ** -0.5,
        "ada_b": 0.01 * nrm(ks[9], (DEPTH, 3 * D_MODEL), F32),
        "norm_g": 1.0 + 0.05 * nrm(ks[10], (DEPTH, D_MODEL), F32),
        "ret_w_in": nrm(ks[11], (N_A, D_MODEL, RET_IN_W), F32) * D_MODEL ** -0.5,
        "ret_norm_g": 1.0 + 0.05 * nrm(ks[12], (N_A, RET_V_W), F32),
        "ret_w_out": nrm(ks[13], (N_A, RET_V_W, D_MODEL), F32) * RET_V_W ** -0.5,
        "kv_norm_g": 1.0 + 0.05 * nrm(ks[14], (D_MODEL,), F32),
        "w_kv": nrm(ks[15], (D_MODEL, 2 * SB_W), F32) * D_MODEL ** -0.5,
        "sb_q_g": 1.0 + 0.05 * nrm(ks[16], (N_B, SB_DH), F32),
        "sb_k_g": 1.0 + 0.05 * nrm(ks[17], (SB_DH,), F32),
        "sb_w_in": nrm(ks[18], (N_B, D_MODEL, SB_IN_W), F32) * D_MODEL ** -0.5,
        "sb_w_out": nrm(ks[19], (N_B, SB_W, D_MODEL), F32) * SB_W ** -0.5,
        "sb_bias": SB_BIAS_INIT + 0.5 * nrm(ks[20], (N_B, SB_HEADS), F32),
    }

def reference(x_prompt, x_sample, state_ret, cache_k, cache_v, page_table, c_prompt, c_sample,
              ada_w, ada_b, norm_g, ret_w_in, ret_norm_g, ret_w_out,
              kv_norm_g, w_kv, sb_q_g, sb_k_g, sb_w_in, sb_w_out, sb_bias):
    weights = (ada_w, ada_b, norm_g, ret_w_in, ret_norm_g, ret_w_out,
               kv_norm_g, w_kv, sb_q_g, sb_k_g, sb_w_in, sb_w_out, sb_bias)
    L_p = x_prompt.shape[1]
    pos_p = jnp.arange(L_p, dtype=jnp.int32)
    y_p, st_p, k_p, v_p = trunk(x_prompt, c_prompt, pos_p, None, None, None, *weights)
    db, n_pages = page_table.shape
    past_len = n_pages * PAGE_SIZE
    past_k = cache_k[page_table].reshape(db, past_len, SB_HEADS, SB_DH)
    past_v = cache_v[page_table].reshape(db, past_len, SB_HEADS, SB_DH)
    L_s = x_sample.shape[1]
    pos_s = past_len + jnp.arange(L_s, dtype=jnp.int32)
    y_s, st_s, k_s, v_s = trunk(x_sample, c_sample, pos_s, state_ret, past_k, past_v, *weights)
    return (y_p.astype(x_prompt.dtype), y_s.astype(x_sample.dtype), st_p, st_s, k_p, v_p, k_s, v_s)


_drawn_inputs = setup_inputs


def setup_inputs(seed=0):
    import zlib

    import numpy as np

    out = dict(_drawn_inputs(seed))
    spreads = {}
    factors = {'ret_norm_g': 2.675, 'sb_q_g': 42.999, 'sb_bias': 5.026}
    for name, (base, spread) in spreads.items():
        noise = np.random.default_rng([zlib.crc32(name.encode()), seed]).standard_normal(out[name].shape)
        drawn = base * np.exp(spread * noise) if base else spread * noise
        out[name] = __import__('jax').numpy.asarray(drawn.astype(out[name].dtype))
    for name, factor in factors.items():
        out[name] = (out[name] * factor).astype(out[name].dtype)
    return out
```

```python
import math
from contextlib import ExitStack

import concourse.bass as bass
from concourse import mybir
from concourse.alu_op_type import AluOpType as ALU

ACT = mybir.ActivationFunctionType
AX = mybir.AxisListType
F32 = mybir.dt.float32
F32R = mybir.dt.float32r
I32 = mybir.dt.int32

P = 128
D = 1024
KD = D // P
SEQ = 1024
NPT = SEQ // P
NT = NPT + 1
DB, DS = 8, 8
NS = DB * DS
NC = 1 + DB
PAST = 256
PAGE = 128
NPG = PAST // PAGE
H = 8
DK, DV = 128, 256
AH = 16
DH = 64
NB = 512
EPS = 1e-6
FAR = -2.0 ** 30


def semaphores(nc, ctx, prefix):
    made = []

    def sem(name):
        made.append(nc.alloc_semaphore(f"{prefix}_{name}"))
        return made[-1]

    def give_back():
        nc.clear_and_free_semaphores(made)
        nc.all_engine_barrier()

    ctx.callback(give_back)
    return sem


def rows(t):
    return P if t < NPT else NS


class Count:

    def __init__(self):
        self.base, self.n, self.turn, self.per = 0, 0, None, 0

    def up(self, k=1):
        self.n += k
        return k

    def now(self):
        if self.turn is None:
            return self.base + self.n
        return self.turn * self.per + (self.base + self.n)

    def enter(self, turn, per):
        self.base, self.n, self.turn, self.per = self.base + self.n, 0, turn, per

    def leave(self, turns):
        assert self.n == self.per, (self.n, self.per)
        self.base, self.n, self.turn = self.base + turns * self.per, 0, None


def build_program(nc, t_in, t_out):
    ctx = ExitStack()
    with ctx:
        persist = Persistent(nc, ctx, t_in)
        modulation(nc, t_in, persist)
        retention_layer(nc, t_in, t_out, persist)
        x = ctx.enter_context(nc.sbuf_tensor("x", [P, NT, D], F32))
        outward(nc, persist, "ro", persist.retained, t_in["ret_w_out"][0], H * DV // P, True, 0, x, Finish(load=reload_x(t_in)))
        shared_kv_and_queries(nc, t_in, t_out, persist, x)
        attention_layer(nc, t_in, t_out, persist)
        outward(nc, persist, "ao", persist.attended, t_in["sb_w_out"][0], KD, False, 1, x, Finish(store=store_y(t_out)))


class Persistent:

    def __init__(self, nc, ctx, t_in):
        def sb(name, shape, dt=F32):
            return ctx.enter_context(nc.sbuf_tensor(name, shape, dt))

        self.ident = sb("ident", [P, P])
        self.selector = sb("selector", [NC, P + NS])
        self.gain = sb("gain", [P, 3, KD, NC])
        self.shift = sb("shift", [P, 3, KD, NC])
        self.gate = sb("gate", [NC, 2, D])
        self.ret_g = sb("ret_g", [P, 2 * KD])
        self.k_gain = sb("k_gain", [P, DH])
        self.q_gain = sb("q_gain", [P, DH])
        self.eps = sb("eps", [P, 1])
        self.retained = nc.dram_tensor("retained", (NT * P, H * DV), F32, kind="Internal").ap()
        self.q_rows = nc.dram_tensor("q_rows", (NT * P, D), F32, kind="Internal").ap()
        self.g_rows = nc.dram_tensor("g_rows", (NT * P, D), F32, kind="Internal").ap()
        self.attended = nc.dram_tensor("attended", (NT * P, D), F32, kind="Internal").ap()


def modulation(nc, t_in, ps):
    ctx = ExitStack()
    with ctx:
        def sb(name, shape, dt=F32):
            return ctx.enter_context(nc.sbuf_tensor(name, shape, dt))

        sem = semaphores(nc, ctx, "mod")

        NCH = 3 * D // NB
        cond = sb("cond", [NC, D])
        cond_act = sb("cond_act", [NC, D])
        cond_t = sb("cond_t", [P, KD, NC])
        vec_rows = sb("vec_rows", [5 * KD, P])
        vec_t = sb("vec_t", [P, 5 * KD])
        ada_bias = sb("ada_bias", [NC, 2, 3 * D])
        mod = sb("mod", [NC, 2, 3 * D])
        w = sb("ada_w_sb", [P, 2, KD, NB])
        acc = ctx.enter_context(nc.psum_tensor("mod_acc", [P, 2, NB], F32))
        tr = ctx.enter_context(nc.psum_tensor("mod_tr", [P, NB], F32))
        tr2 = ctx.enter_context(nc.psum_tensor("mod_tr2", [P, NB], F32))
        loaded_pool = sem("loaded_pool")
        loaded, w_loaded, act_done = sem("loaded"), [sem("ada_w0"), sem("ada_w1")], sem("mod_act")
        pe_c, pe_acc, pe_tr = sem("pe_cond_t"), sem("pe_mod_acc"), sem("pe_mod_tr")
        dve_c, dve_acc, dve_own = sem("dve_cond_t"), sem("dve_mod_acc"), sem("dve_mod_own")
        block = ctx.enter_context(nc.Block())

        @block.sync
        def _(sp):
            sp.dma_start(cond[0:1, :], t_in["c_prompt"]).then_inc(loaded, 16)
            sp.dma_start(cond[1:NC, :], t_in["c_sample"]).then_inc(loaded, 16)
            sp.dma_start(ps.ident[:], t_in["ident"]).then_inc(loaded, 16)
            sp.dma_start(vec_rows[0:2 * KD, :], t_in["norm_g"].rearrange("l (k p) -> (l k) p", p=P)).then_inc(loaded, 16)
            sp.dma_start(vec_rows[2 * KD:3 * KD, :], t_in["kv_norm_g"].rearrange("(k p) -> k p", p=P)).then_inc(loaded, 16)
            sp.dma_start(vec_rows[3 * KD:5 * KD, :], t_in["ret_norm_g"].rearrange("l (k p) -> (l k) p", p=P)).then_inc(loaded, 16)
            for la in range(2):
                with sp.Fori(0, NCH // 2) as j:
                    for b in range(2):
                        if la == 0:
                            sp.wait_ge(dve_acc, j * 2 + (b + 1))
                        else:
                            sp.wait_ge(dve_acc, j * 2 + (NCH + b + 1))
                        sp.dma_start(w[:, b, :, :], t_in["ada_w"][la].rearrange("(k p) n -> p k n", p=P)[
                            :, :, bass.ds(j * (2 * NB) + b * NB, NB)]).then_inc(w_loaded[b], 16)

        @block.gpsimd
        def _(pool):
            pool.dma_start(ada_bias[:], t_in["ada_b"].rearrange("(o l) n -> o l n", o=1).to_broadcast([NC, 2, 3 * D])).then_inc(loaded_pool, 16)
            pool.dma_start(ps.selector[:], t_in["selector"]).then_inc(loaded_pool, 16)
            pool.dma_start(ps.k_gain[:], t_in["sb_k_g"].rearrange("(o n) -> o n", o=1).to_broadcast([P, DH])).then_inc(loaded_pool, 16)
            pool.dma_start(ps.q_gain[:], t_in["sb_q_g"].to_broadcast([P, DH])).then_inc(loaded_pool, 16)


        @block.scalar
        def _(act):
            act.wait_ge(loaded, 96)
            nc.scalar.activation(cond_act[:], cond[:], ACT.Silu).then_inc(act_done, 1)

        @block.tensor
        def _(pe):
            pe.wait_ge(loaded, 96)
            pe.wait_ge(act_done, 1)
            for k in range(KD):
                last = nc.tensor.transpose(tr[:, k * NC:(k + 1) * NC], cond_act[:, k * P:(k + 1) * P], ps.ident[0:NC, 0:NC])
            last.then_inc(pe_c, 1)
            nc.tensor.transpose(tr2[:, 0:5 * KD], vec_rows[:], ps.ident[0:5 * KD, 0:5 * KD]).then_inc(pe_c, 1)
            pe.wait_ge(dve_c, 1)
            for la in range(2):
                with pe.Fori(0, NCH // 2) as j:
                    for b in range(2):
                        pe.wait_ge(w_loaded[b], (j + (la * (NCH // 2) + 1)) * 16)
                        pe.wait_ge(dve_acc, j * 2 + (la * NCH + b + 1))
                        for k in range(KD):
                            last = nc.tensor.matmul(acc[0:NC, b, :], cond_t[:, k, :], w[:, b, k, :],
                                                    start=k == 0, stop=k == KD - 1)
                        last.then_inc(pe_acc, 1)
            pe.wait_ge(dve_acc, 2 * NCH + 2)
            for la in range(2):
                for k in range(2 * KD):
                    at = (la * 2 * KD + k) * NC
                    last = nc.tensor.transpose(tr[:, at:at + NC], mod[:, la, k * P:(k + 1) * P], ps.ident[0:NC, 0:NC])
            last.then_inc(pe_tr, 1)

        @block.vector
        def _(dve):
            dve.sem_inc(dve_acc, 2)
            dve.wait_ge(loaded_pool, 64)
            dve.wait_ge(pe_c, 1)
            nc.vector.tensor_copy(cond_t[:].rearrange("p k c -> p (k c)"), tr[:, 0:KD * NC]).then_inc(dve_c, 1)
            dve.wait_ge(pe_c, 2)
            nc.vector.tensor_copy(vec_t[:], tr2[:, 0:5 * KD]).then_inc(dve_own, 1)
            for la in range(2):
                with dve.Fori(0, NCH // 2) as j:
                    for b in range(2):
                        dve.wait_ge(pe_acc, j * 2 + (la * NCH + b + 1))
                        cols = bass.ds(j * (2 * NB) + b * NB, NB)
                        nc.vector.tensor_tensor(mod[:, la, cols], acc[0:NC, b, :], ada_bias[:, la, cols], ALU.add).then_inc(dve_acc, 1)
            dve.wait_ge(dve_own, 1)
            dve.wait_ge(dve_acc, 2 * NCH + 2)
            nc.vector.tensor_copy(ps.gate[:], mod[:, :, 2 * D:3 * D])
            nc.vector.tensor_copy(ps.ret_g[:], vec_t[:, 3 * KD:5 * KD])
            nc.vector.memset(ps.shift[:, 1, :, :], 0.0)
            nc.vector.tensor_copy(ps.gain[:, 1, :, :], vec_t[:, 2 * KD:3 * KD].unsqueeze(2).to_broadcast([P, KD, NC]))
            dve.wait_ge(pe_tr, 1)
            m = tr[:, 0:4 * KD * NC].rearrange("p (l s k c) -> p l s k c", l=2, s=2, k=KD)
            for la in range(2):
                nc.vector.tensor_copy(ps.shift[:, 2 * la, :, :], m[:, la, 0])
                nc.vector.scalar_tensor_tensor(ps.gain[:, 2 * la, :, :], m[:, la, 1], 1.0,
                                               vec_t[:, la * KD:(la + 1) * KD].unsqueeze(2).to_broadcast([P, KD, NC]),
                                               ALU.add, ALU.mult)


def normed_transposed(nc, ps, x, hi, lo, which, tag, load=None):
    ctx = ExitStack()
    with ctx:
        def sb(name, shape, dt=F32):
            return ctx.enter_context(nc.sbuf_tensor(f"{tag}_{name}", shape, dt))

        sem = semaphores(nc, ctx, tag)

        xn = sb("xn", [P, NT, D])
        squares = sb("squares", [P, D])
        ss = sb("ss", [P, NT])
        root = sb("root", [P, NT])
        rstd = sb("rstd", [P, NT])
        full = sb("full", [P, 2, NB])
        part = sb("part", [P, NS])
        tr = ctx.enter_context(nc.psum_tensor(f"{tag}_tr", [P, 4, NB], F32))
        x_loaded = [sem(f"x_loaded{t}") for t in range(NT)] if load is not None else []
        cleared, squared, rooted, own, scaled = sem("cleared"), sem("squared"), sem("rooted"), sem("own"), sem("scaled")
        turned, full_ready, hi_ready, lo_ready = sem("turned"), sem("full_ready"), sem("hi_ready"), sem("lo_ready")
        block = ctx.enter_context(nc.Block())
        units = [(g, k) for g in range(3) for k in range(KD)]

        if load is not None:
            @block.sync
            def _(sp):
                load(sp, x_loaded)

        @block.scalar
        def _(act):
            act.wait_ge(cleared, 1)
            for t in range(NT):
                if load is not None:
                    act.wait_ge(x_loaded[t], 16)
                if t:
                    act.wait_ge(squared, t)
                nc.scalar.activation(squares[0:rows(t), :], x[0:rows(t), t, :], ACT.Square,
                                     accum_out=ss[0:rows(t), t:t + 1]).then_inc(squared, 1)
            act.wait_ge(squared, NT)
            nc.scalar.activation(root[:], ss[:], ACT.Sqrt, scale=1.0 / D, bias=ps.eps[:]).then_inc(rooted, 1)
            for u, (g, k) in enumerate(units):
                act.wait_ge(full_ready, u + 1)
                c0, n = g * NB, NB if g < 2 else NS
                nc.scalar.copy(hi[:, k, c0:c0 + n], full[:, u % 2, 0:n]).then_inc(hi_ready, 1)

        @block.vector
        def _(dve):
            nc.vector.memset(ss[:], 1.0).then_inc(cleared, 1)
            dve.wait_ge(rooted, 1)
            nc.vector.reciprocal(rstd[:], root[:]).then_inc(own, 1)
            dve.wait_ge(own, 1)
            for t in range(NT):
                nc.vector.tensor_scalar(xn[0:rows(t), t, :], x[0:rows(t), t, :], rstd[0:rows(t), t:t + 1], None,
                                        ALU.mult).then_inc(scaled, 1)

            def take(u):
                g, k = units[u]
                dve.wait_ge(turned, u + 1)
                if u >= 2:
                    dve.wait_ge(lo_ready, u - 1)
                if g < 2:
                    nc.vector.tensor_scalar(full[:, u % 2, :], tr[:, u % 4, :], ps.gain[:, which, k, 0:1],
                                            ps.shift[:, which, k, 0:1], ALU.mult, ALU.add).then_inc(full_ready, 1)
                else:
                    gain = ps.gain[:, which, k, 1:NC].unsqueeze(2).to_broadcast([P, DB, DS])
                    shift = ps.shift[:, which, k, 1:NC].unsqueeze(2).to_broadcast([P, DB, DS])
                    if u > 16:
                        dve.wait_ge(full_ready, u)
                    nc.vector.tensor_tensor(part[:].rearrange("p (b i) -> p b i", b=DB),
                                            tr[:, u % 4, 0:NS].rearrange("p (b i) -> p b i", b=DB), gain,
                                            ALU.mult).then_inc(own, 1)
                    dve.wait_ge(own, 2 + u - 16)
                    nc.vector.tensor_tensor(full[:, u % 2, 0:NS].rearrange("p (b i) -> p b i", b=DB),
                                            part[:].rearrange("p (b i) -> p b i", b=DB), shift,
                                            ALU.add).then_inc(full_ready, 1)

            def rest(u):
                g, k = units[u]
                dve.wait_ge(hi_ready, u + 1)
                c0, n = g * NB, NB if g < 2 else NS
                nc.vector.tensor_tensor(lo[:, k, c0:c0 + n], full[:, u % 2, 0:n], hi[:, k, c0:c0 + n].bitcast(F32),
                                        ALU.subtract).then_inc(lo_ready, 1)

            for u in range(len(units)):
                take(u)
                if u:
                    rest(u - 1)
            rest(len(units) - 1)

        @block.tensor
        def _(pe):
            for u, (g, k) in enumerate(units):
                tiles = range(4 * g, 4 * g + 4) if g < 2 else [NPT]
                pe.wait_ge(scaled, tiles[-1] + 1)
                if u >= 4:
                    pe.wait_ge(full_ready, u - 3)
                for n, t in enumerate(tiles):
                    r = rows(t)
                    last = nc.tensor.transpose(tr[:, u % 4, n * P:n * P + r], xn[0:r, t, k * P:(k + 1) * P], ps.ident[0:r, 0:r])
                last.then_inc(turned, 1)


def load_x(t_in, x):
    def load(sp, x_loaded):
        for t in range(NT):
            src = t_in["x_prompt"][0, t * P:(t + 1) * P, :] if t < NPT else t_in["x_sample"].rearrange("b i d -> (b i) d")
            sp.dma_start(x[0:rows(t), t, :], src).then_inc(x_loaded[t], 16)
    return load


def retention_layer(nc, t_in, t_out, ps):
    ctx = ExitStack()
    with ctx:
        with nc.Block() as block:
            @block.vector
            def _(dve):
                nc.vector.memset(ps.eps[:], EPS)
        hi = ctx.enter_context(nc.sbuf_tensor("ret_h_hi", [P, KD, SEQ + NS], F32R))
        lo = ctx.enter_context(nc.sbuf_tensor("ret_h_lo", [P, KD, SEQ + NS], F32R))
        with nc.sbuf_tensor("ret_x", [P, NT, D], F32) as x:
            normed_transposed(nc, ps, x, hi, lo, 0, "rn", load_x(t_in, x))
        retention_heads(nc, t_in, t_out, ps, hi, lo)


def retention_heads(nc, t_in, t_out, ps, h_hi, h_lo):
    ctx = ExitStack()
    with ctx:
        def sb(name, shape, dt=F32):
            return ctx.enter_context(nc.sbuf_tensor(f"rt_{name}", shape, dt))

        sem = semaphores(nc, ctx, "rt")

        R = 3
        CR = 10
        QKV = 2 * DK + DV
        cos = sb("cos", [P, NT, DK])
        sin = sb("sin", [P, NT, DK])
        tables = sb("tables", [P, 2, 3, H])
        causal = sb("causal", [P, P + NS])
        own_rows = sb("own_rows", [NS, DB])
        w_hi = sb("w_hi", [P, KD, QKV], F32R)
        w_lo, w_raw = overlaid(nc, ctx, "rt_w_lo", "rt_w_raw", [P, KD, QKV])
        g_hi = sb("g_hi", [P, KD, DV], F32R)
        g_lo, g_raw = overlaid(nc, ctx, "rt_g_lo", "rt_g_raw", [P, KD, DV])
        raw = sb("raw", [P, R, 2, DK])
        by_cos = sb("by_cos", [P, 2, DK])
        by_sin = sb("by_sin", [P, 2, DK])
        rot = sb("rot", [P, R, 2, DK])
        v = sb("v", [P, R, DV])
        qk_t = sb("qk_t", [P, R, 2, P])
        probs = sb("probs", [P, R, P])
        state = sb("state", [P, DV])
        state_sum = sb("state_sum", [P, DV])
        old = sb("old", [P, DB, DV])
        new = sb("new", [P, DB, DV])
        q_diag = sb("q_diag", [P, DB, NS])
        k_own = sb("k_own", [NS, DB, DK])
        o = sb("o", [P, NT, DV])
        g = sb("g", [P, NT, DV])
        squares = sb("squares", [P, DV])
        ss = sb("ss", [P, NT])
        root = sb("root", [P, NT])
        rstd = sb("rstd", [P, NT])

        def bank(name, n=1):
            return ctx.enter_context(nc.psum_tensor(f"rt_{name}", [P, n, NB], F32))

        acc, acc_g = bank("acc", 2), bank("acc_g", 2)
        tr, sc, out, st = bank("tr"), bank("sc"), bank("out"), bank("st")

        consts = sem("consts")
        w_loaded, g_loaded, old_loaded = sem("w_loaded"), sem("g_loaded"), sem("old_loaded")
        w_hi_s, w_lo_s, g_hi_s, g_lo_s = sem("w_hi"), sem("w_lo"), sem("g_hi"), sem("g_lo")
        projected, projected_g = sem("projected"), sem("projected_g")
        taken, taken_g, rotated, turned = sem("taken"), sem("taken_g"), sem("rotated"), sem("turned")
        turned_out, scored, masked, attended = sem("turned_out"), sem("scored"), sem("masked"), sem("attended")
        o_taken, state_ready, new_ready = sem("o_taken"), sem("state_ready"), sem("new_ready")
        rooted, gated, stored, cleared = sem("rooted"), sem("gated"), sem("stored"), sem("cleared")
        state_free, new_free, o_free, own = sem("state_free"), sem("new_free"), sem("o_free"), sem("own")
        k_own_s, storing = sem("k_own_s"), sem("storing")
        block = ctx.enter_context(nc.Block())

        def after(h, t):
            return h * NT + (CR + t + 1)

        def freed(h, t, ring):
            if t >= ring:
                return h * NT + (CR + t - ring + 1)
            last = max(u for u in range(NT) if u % ring == t % ring)
            return h * NT + (CR - NT + last + 1)

        w_in = t_in["ret_w_in"][0].rearrange("(k p) n -> p k n", p=P)

        @block.sync
        def _(sp):
            sp.dma_start(cos[:], t_in["rope_cos"]).then_inc(consts, 16)
            sp.dma_start(sin[:], t_in["rope_sin"]).then_inc(consts, 16)
            sp.dma_start(tables[:], t_in["decays"]).then_inc(consts, 16)
            sp.dma_start(causal[:], t_in["causal"]).then_inc(consts, 16)
            sp.dma_start(own_rows[:], t_in["own_rows"]).then_inc(consts, 16)
            with sp.Fori(0, H) as h:
                sp.wait_ge(projected, h * NT + CR)
                sp.dma_start(w_raw[:, :, 0:DK], w_in[:, :, bass.ds(h * DK, DK)]).then_inc(w_loaded, 16)
                sp.dma_start(w_raw[:, :, DK:2 * DK], w_in[:, :, bass.ds(h * DK + H * DK, DK)]).then_inc(w_loaded, 16)
                sp.dma_start(w_raw[:, :, 2 * DK:QKV], w_in[:, :, bass.ds(h * DV + 2 * H * DK, DV)]).then_inc(w_loaded, 16)
                sp.wait_ge(new_ready, h + CR)
                sp.dma_start(old[:], t_in["state_ret"][0].rearrange("b h k e -> h k b e")[bass.ds(h, 1)].rearrange(
                    "o k b e -> (o k) b e")).then_inc(old_loaded, 16)
                sp.wait_ge(projected_g, h * NT + CR)
                sp.dma_start(g_raw[:], w_in[:, :, bass.ds(h * DV + 2 * H * DK + H * DV, DV)]).then_inc(g_loaded, 16)

        @block.gpsimd
        def _(pool):
            nc.gpsimd.memset(q_diag[:], 0.0).then_inc(cleared, 1)
            for s in (state_free, new_free, o_free):
                pool.sem_inc(s, 1)
            with pool.Fori(0, H) as h:
                pool.wait_ge(state_ready, after(h, NPT - 1))
                pool.sem_inc(storing, 1)
                pool.dma_start(t_out["st_prompt"][0, 0][bass.ds(h, 1)].rearrange("o k e -> (o k) e"), state[:]).then_inc(stored, 16)
                pool.wait_ge(stored, h * 64 + 16)
                pool.sem_inc(state_free, 1)
                pool.wait_ge(new_ready, h + (CR + 1))
                pool.sem_inc(storing, 1)
                pool.dma_start(t_out["st_sample"][0].rearrange("b h k e -> h k b e")[bass.ds(h, 1)].rearrange(
                    "o k b e -> (o k) b e"), new[:]).then_inc(stored, 16)
                pool.wait_ge(stored, h * 64 + 32)
                pool.sem_inc(new_free, 1)
                pool.wait_ge(gated, (h + 1) * NT)
                pool.sem_inc(storing, 1)
                pool.dma_start(ps.retained[0:SEQ, bass.ds(h * DV, DV)].rearrange("(t p) e -> p t e", p=P), o[:, 0:NPT, :]).then_inc(stored, 16)
                pool.dma_start(ps.retained[SEQ:SEQ + NS, bass.ds(h * DV, DV)], o[0:NS, NPT, :]).then_inc(stored, 16)
                pool.wait_ge(stored, h * 64 + 64)
                pool.sem_inc(o_free, 1)

        @block.tensor
        def _(pe):
            pe.sem_inc(projected, CR)
            pe.sem_inc(projected_g, CR)
            pe.sem_inc(attended, CR)
            pe.wait_ge(consts, 80)

            def turn(h, t):
                pe.wait_ge(rotated, after(h, t))
                pe.wait_ge(turned_out, freed(h, t, 1))
                for n in range(2):
                    last = nc.tensor.transpose(tr[:, 0, n * P:(n + 1) * P], rot[:, t % R, n, :], ps.ident[:])
                last.then_inc(turned, 1)

            def score(h, t):
                r = rows(t)
                pe.wait_ge(turned_out, after(h, t))
                pe.wait_ge(masked, freed(h, t, 1))
                nc.tensor.matmul(sc[0:r, 0, 0:r], qk_t[:, t % R, 1, 0:r], qk_t[:, t % R, 0, 0:r],
                                 start=True, stop=True).then_inc(scored, 1)

            def attend(h, t):
                r = rows(t)
                pe.wait_ge(masked, after(h, t))
                pe.wait_ge(o_taken, freed(h, t, 1))
                if t == NPT:
                    pe.wait_ge(old_loaded, (h + 1) * 16)
                    pe.wait_ge(k_own_s, h + 1)
                    for b in range(DB):
                        nc.tensor.matmul(out[0:r, 0, 0:DV], q_diag[:, b, :], old[:, b, :], start=b == 0, stop=False)
                elif t > 0:
                    pe.wait_ge(state_ready, after(h, t - 1))
                    nc.tensor.matmul(out[0:r, 0, 0:DV], qk_t[:, t % R, 0, :], state[:], start=True, stop=False)
                last = nc.tensor.matmul(out[0:r, 0, 0:DV], probs[0:r, t % R, 0:r], v[0:r, t % R, :], start=t == 0, stop=True)
                if t < NPT:
                    pe.wait_ge(state_ready, freed(h, t, 1) if t else h * NT + CR)
                    last = nc.tensor.matmul(st[:, 0, 0:DV], rot[0:r, t % R, 1, :], v[0:r, t % R, :], start=True, stop=True)
                else:
                    pe.wait_ge(state_ready, after(h, NPT - 1))
                    pe.wait_ge(taken, after(h, NPT))
                    for b in range(DB):
                        dst = (acc[:, 0], acc[:, 1], st[:, 0], tr[:, 0])[b // 2]
                        last = nc.tensor.matmul(dst[:, (b % 2) * DV:(b % 2 + 1) * DV], k_own[:, b, :], v[0:NS, t % R, :],
                                                start=b % 2 == 0, stop=True, skip_group_check=True)
                last.then_inc(attended, 1)

            def project(dst, whi, wlo, t, n):
                r = rows(t)
                for k in range(KD):
                    cols = slice(t * P, t * P + r)
                    nc.tensor.matmul(dst[0:r, 0:n], h_hi[:, k, cols], whi[:, k, :], start=k == 0, stop=False)
                    nc.tensor.matmul(dst[0:r, 0:n], h_hi[:, k, cols], wlo[:, k, :], start=False, stop=False)
                    last = nc.tensor.matmul(dst[0:r, 0:n], h_lo[:, k, cols], whi[:, k, :], start=False, stop=k == KD - 1)
                return last

            def later_steps(h, s):
                if 0 <= s - 3 < NT:
                    attend(h, s - 3)
                if 0 <= s - 2 < NT:
                    score(h, s - 2)
                if 0 <= s - 1 < NT:
                    turn(h, s - 1)

            with pe.Fori(0, H) as h:
                pe.wait_ge(new_ready, h + CR)
                pe.wait_ge(w_lo_s, (h + 1) * 4)
                for t in range(NT):
                    later_steps(h, t)
                    pe.wait_ge(taken, freed(h, t, 2))
                    project(acc[:, t % 2], w_hi, w_lo, t, QKV).then_inc(projected, 1)
                pe.wait_ge(g_lo_s, (h + 1) * 2)
                for t in range(NT):
                    later_steps(h, NT + t)
                    pe.wait_ge(taken_g, freed(h, t, 2))
                    project(acc_g[:, t % 2], g_hi, g_lo, t, DV).then_inc(projected_g, 1)

        @block.scalar
        def _(act):
            act.sem_inc(taken, CR)
            act.sem_inc(taken_g, CR)
            act.sem_inc(turned_out, CR)
            act.sem_inc(o_taken, CR)
            act.wait_ge(consts, 80)
            act.wait_ge(cleared, 2)

            def take(h, t):
                r, kind = rows(t), 0 if t < NPT else 1
                act.wait_ge(projected, after(h, t))
                act.wait_ge(rotated, freed(h, t, R))
                act.wait_ge(attended, freed(h, t, R))
                nc.scalar.copy(v[0:r, t % R, :], acc[0:r, t % 2, 2 * DK:QKV])
                for n in range(2):
                    last = nc.scalar.activation(raw[0:r, t % R, n, :], acc[0:r, t % 2, n * DK:(n + 1) * DK], ACT.Copy,
                                                scale=tables[0:r, kind, n, bass.ds(h, 1)])
                last.then_inc(taken, 1)

            def turn_out(h, t):
                r = rows(t)
                act.wait_ge(turned, h * NT + (t + 1))
                act.wait_ge(attended, freed(h, t, R))
                if t == NPT:
                    nc.scalar.copy(diagonal(q_diag, DB, NS, DS), tr[:, 0, 0:NS].rearrange("p (b i) -> p b i", i=DS))
                src = tr[:, 0, 0:2 * P].rearrange("p (n c) -> p n c", n=2)[:, :, 0:r]
                nc.scalar.copy(qk_t[:, t % R, :, 0:r], src).then_inc(turned_out, 1)

            def take_o(h, t):
                r = rows(t)
                act.wait_ge(attended, after(h, t))
                if t == 0:
                    act.wait_ge(o_free, h + 1)
                nc.scalar.copy(o[0:r, t, :], out[0:r, 0, 0:DV])
                act.wait_ge(o_taken, freed(h, t, 1))
                nc.scalar.activation(squares[0:r, :], out[0:r, 0, 0:DV], ACT.Square,
                                     accum_out=ss[0:r, t:t + 1]).then_inc(o_taken, 1)

            def steps(h, s):
                if 0 <= s - 3 < NT:
                    take_o(h, s - 3)
                if 0 <= s - 1 < NT:
                    turn_out(h, s - 1)

            def split_w(h, q):
                act.wait_ge(w_loaded, (h + 1) * 48)
                nc.scalar.copy(w_hi[:, 2 * q:2 * q + 2, :], w_raw[:, 2 * q:2 * q + 2, :]).then_inc(w_hi_s, 1)

            def split_g(h, q):
                act.wait_ge(g_loaded, (h + 1) * 16)
                nc.scalar.copy(g_hi[:, 4 * q:4 * q + 4, :], g_raw[:, 4 * q:4 * q + 4, :]).then_inc(g_hi_s, 1)

            def head(h, last):
                for t in range(NT):
                    steps(h, t)
                    if t in (2, 3):
                        split_g(h, t - 2)
                    take(h, t)
                for t in range(NT):
                    steps(h, NT + t)
                    if not last and 4 <= t < 8:
                        split_w(h + 1, t - 4)
                    act.wait_ge(projected_g, after(h, t))
                    nc.scalar.activation(g[0:rows(t), t, :], acc_g[0:rows(t), t % 2, 0:DV], ACT.Silu).then_inc(taken_g, 1)
                nc.scalar.activation(root[:], ss[:], ACT.Sqrt, scale=1.0 / DV, bias=ps.eps[:]).then_inc(rooted, 1)

            for q in range(4):
                split_w(0, q)
            with act.Fori(0, H - 1) as h:
                head(h, False)
            head(H - 1, True)

        @block.vector
        def _(dve):
            own_n = Count()
            for s in (rotated, masked, state_ready, new_ready):
                dve.sem_inc(s, CR)
            nc.vector.memset(ss[:], 1.0).then_inc(cleared, 1)
            dve.wait_ge(consts, 80)
            dve.sem_inc(own, own_n.up())

            def rotate(h, t):
                r = rows(t)
                dve.wait_ge(taken, after(h, t))
                dve.wait_ge(attended, freed(h, t, R))
                dve.wait_ge(own, own_n.now())
                halves = raw[0:r, t % R].rearrange("p n (a c) -> p n a c", a=2)
                table = sin[0:r, t].rearrange("p (a c) -> p a c", a=2)
                nc.vector.tensor_tensor(by_cos[0:r], raw[0:r, t % R], cos[0:r, t].unsqueeze(1).to_broadcast([r, 2, DK]), ALU.mult)
                for a in range(2):
                    last = nc.vector.tensor_tensor(by_sin[0:r, :, a * 64:(a + 1) * 64], halves[:, :, 1 - a, :],
                                                   table[:, a, :].unsqueeze(1).to_broadcast([r, 2, 64]), ALU.mult)
                last.then_inc(own, own_n.up())
                dve.wait_ge(own, own_n.now())
                nc.vector.tensor_tensor(rot[0:r, t % R], by_cos[0:r], by_sin[0:r], ALU.add).then_inc(rotated, 1)

            def mask(h, t):
                r = rows(t)
                dve.wait_ge(scored, h * NT + (t + 1))
                table = causal[:, 0:P] if t < NPT else causal[0:NS, P:P + NS]
                nc.vector.tensor_tensor(probs[0:r, t % R, 0:r], sc[0:r, 0, 0:r], table, ALU.mult).then_inc(masked, 1)

            def spread_k(h):
                dve.wait_ge(rotated, after(h, NPT))
                nc.vector.tensor_tensor(k_own[:], rot[0:NS, NPT % R, 1, :].unsqueeze(1).to_broadcast([NS, DB, DK]),
                                        own_rows[:].unsqueeze(2).to_broadcast([NS, DB, DK]), ALU.mult).then_inc(k_own_s, 1)

            def update(h, t):
                decay = tables[:, 0 if t < NPT else 1, 2, bass.ds(h, 1)]
                dve.wait_ge(attended, after(h, t))
                if t == 0:
                    dve.wait_ge(state_free, h + 1)
                    nc.vector.tensor_scalar(state[:], st[:, 0, 0:DV], decay, None, ALU.mult).then_inc(state_ready, 1)
                elif t < NPT:
                    dve.wait_ge(state_ready, after(h, t - 1))
                    nc.vector.tensor_tensor(state_sum[:], st[:, 0, 0:DV], state[:], ALU.add).then_inc(own, own_n.up())
                    dve.wait_ge(own, own_n.now())
                    nc.vector.tensor_scalar(state[:], state_sum[:], decay, None, ALU.mult).then_inc(state_ready, 1)
                else:
                    dve.wait_ge(new_free, h + 1)
                    for n, src in enumerate((acc[:, 0], acc[:, 1], st[:, 0], tr[:, 0])):
                        pair = slice(2 * n, 2 * n + 2)
                        last = nc.vector.tensor_tensor(new[:, pair, :], src.rearrange("p (b e) -> p b e", b=2),
                                                       old[:, pair, :], ALU.add)
                    last.then_inc(own, own_n.up())
                    dve.wait_ge(own, own_n.now())
                    nc.vector.tensor_scalar(new[:], new[:], decay, None, ALU.mult).then_inc(new_ready, 1)
                    dve.sem_inc(state_ready, 1)

            def steps(h, s):
                if 0 <= s - 3 < NT:
                    update(h, s - 3)
                if 0 <= s - 2 < NT:
                    mask(h, s - 2)

            def split_w(h, q):
                dve.wait_ge(w_hi_s, h * 4 + (q + 1))
                part = slice(2 * q, 2 * q + 2)
                nc.vector.tensor_tensor(w_lo[:, part, :], w_raw[:, part, :], w_hi[:, part, :].bitcast(F32),
                                        ALU.subtract).then_inc(w_lo_s, 1)

            def split_g(h, q):
                dve.wait_ge(g_hi_s, h * 2 + (q + 1))
                part = slice(4 * q, 4 * q + 4)
                nc.vector.tensor_tensor(g_lo[:, part, :], g_raw[:, part, :], g_hi[:, part, :].bitcast(F32),
                                        ALU.subtract).then_inc(g_lo_s, 1)

            def head(h, last):
                for t in range(NT):
                    steps(h, t)
                    if t in (2, 3):
                        split_g(h, t - 2)
                    rotate(h, t)
                spread_k(h)
                for t in range(NT):
                    steps(h, NT + t)
                    if not last and 4 <= t < 8:
                        split_w(h + 1, t - 4)
                dve.wait_ge(rooted, h + 1)
                nc.vector.reciprocal(rstd[:], root[:]).then_inc(own, own_n.up())
                dve.wait_ge(own, own_n.now())
                for t in range(NT):
                    r = rows(t)
                    nc.vector.scalar_tensor_tensor(o[0:r, t, :], o[0:r, t, :], rstd[0:r, t:t + 1], g[0:r, t, :],
                                                   ALU.mult, ALU.mult).then_inc(gated, 1)

            for q in range(4):
                split_w(0, q)
            with dve.Fori(0, H - 1) as h:
                own_n.enter(h, NT + (NPT - 1) + 1 + 1)
                head(h, False)
            own_n.leave(H - 1)
            head(H - 1, True)


def attention_layer(nc, t_in, t_out, ps):
    prompt_attention(nc, t_in, t_out, ps)
    sample_attention(nc, t_in, t_out, ps)


def prompt_attention(nc, t_in, t_out, ps):
    ctx = ExitStack()
    with ctx:
        def sb(name, shape, dt=F32):
            return ctx.enter_context(nc.sbuf_tensor(f"pa_{name}", shape, dt))

        sem = semaphores(nc, ctx, "pa")

        BODY_HEADS = 4
        UNITS = BODY_HEADS * NPT
        TURNS = AH // BODY_HEADS
        PAIRS = BODY_HEADS // 2
        LAG = 3
        CR = 8
        far_below = sb("far_below", [P, P])
        far_r = sb("far_r", [P, P], F32R)
        ident_r = sb("ident_r", [P, P], F32R)
        bias_row = sb("bias_row", [P, AH])
        bias = sb("bias", [P, 2, AH])
        bias_now = sb("bias_now", [P, 2, BODY_HEADS])
        k2, q2, v2, g2 = (sb(n, [P, 2, NPT, 2 * DH]) for n in ("k2", "q2", "v2", "g2"))
        q4 = sb("q4", [P, 2, 2, DH])
        k_parts = sb("k_parts", [P, NPT, 2, 2, DH], F32R)
        k_t = sb("k_t", [P, 2, SEQ], F32R)
        q_hi = sb("q_hi", [P, 2, P], F32R)
        q_lo = sb("q_lo", [P, 2, P], F32R)
        take = sb("take", [P, 2, SEQ])
        keep = sb("keep", [P, 2, SEQ])
        after_key = sb("after_key", [P, 2, SEQ + 8])
        w = sb("w", [P, 2, SEQ])
        w_t = sb("w_t", [P, 2, SEQ])
        o2 = sb("o2", [P, 2, NPT, 2 * DH])

        def bank(name, n=1):
            return ctx.enter_context(nc.psum_tensor(f"pa_{name}", [P, n, NB], F32))

        z, wt, kq, out = bank("z", 4), bank("wt", 2), bank("kq"), bank("out")
        consts, started = sem("consts"), sem("started")
        loaded = [sem("loaded0"), sem("loaded1")]
        stored = [sem("stored0"), sem("stored1")]
        k_hi_s, k_split, k_turned, k_taken = sem("k_hi_s"), sem("k_split"), sem("k_turned"), sem("k_taken")
        q_doubled, q_turned, q_hi_s, q_lo_s = sem("q_doubled"), sem("q_turned"), sem("q_hi_s"), sem("q_lo_s")
        scored, sticks, weighed = sem("scored"), sem("sticks"), sem("weighed")
        w_turned, w_taken_a, w_taken_v, attended, gated = (sem("w_turned"), sem("w_taken_a"), sem("w_taken_v"),
                                                           sem("attended"), sem("gated"))
        bias_s, scanned = sem("bias_s"), sem("scanned")
        out_free, out_taken = sem("out_free"), sem("out_taken")
        block = ctx.enter_context(nc.Block())

        def done(i, s):
            return i * UNITS + (s + 1 + CR)

        def wide(s):
            return ((s % NPT) + 1) * P

        def where(s):
            s %= UNITS
            return s // (2 * NPT), (s // NPT) % 2, s % NPT

        rows_of = {
            "k": t_out["k_prompt"][0].rearrange("(t p) h d -> p t (h d)", p=P),
            "q": ps.q_rows[0:SEQ, :].rearrange("(t p) c -> p t c", p=P),
            "v": t_out["v_prompt"][0].rearrange("(t p) h d -> p t (h d)", p=P),
            "g": ps.g_rows[0:SEQ, :].rearrange("(t p) c -> p t c", p=P),
        }

        @block.sync
        def _(sp):
            sp.dma_start(far_below[:], t_in["far_below"]).then_inc(consts, 16)
            sp.dma_start(bias_row[:], t_in["sb_bias"].to_broadcast([P, AH])).then_inc(consts, 16)
            with sp.Fori(0, TURNS) as i:
                for pair in range(PAIRS):
                    sp.wait_ge(gated, i * PAIRS + (pair + 1))
                    for buf, name in ((k2, "k"), (q2, "q"), (v2, "v"), (g2, "g")):
                        sp.dma_start(buf[:, pair], rows_of[name][:, :, bass.ds(i * (BODY_HEADS * DH) + pair * 2 * DH, 2 * DH)]).then_inc(loaded[pair], 16)

        @block.gpsimd
        def _(pool):
            pool.sem_inc(out_free, 2)

            def double(i, s):
                pair, hh, t = where(s)
                pool.wait_ge(loaded[pair], i * 64 + (64 if s < UNITS else 128))
                pool.wait_ge(q_turned, done(i, s - 2))
                pool.sem_inc(started, 1)
                src = q2[:, pair, t, hh * DH:(hh + 1) * DH].unsqueeze(1).to_broadcast([P, 2, DH])
                nc.gpsimd.tensor_copy(q4[:, s % 2], src).then_inc(q_doubled, 1)

            def store(i, pair):
                pool.wait_ge(gated, i * PAIRS + (pair + 3))
                pool.sem_inc(started, 1)
                dst = ps.attended[0:SEQ, :].rearrange("(t p) c -> p t c", p=P)
                pool.dma_start(dst[:, :, bass.ds(i * (BODY_HEADS * DH) + pair * 2 * DH, 2 * DH)], o2[:, pair]).then_inc(stored[pair], 16)

            def release(i, pair):
                pool.wait_ge(stored[pair], i * 16 + 16)
                pool.sem_inc(out_free, 1)

            def turn(i, first, last):
                for s in range(UNITS):
                    if not (last and s + 1 >= UNITS):
                        double(i, s + 1)
                    if s == 4 and not first:
                        store(i - 1, 1)
                    if s == 12 and not first:
                        release(i - 1, 1)
                    if s == 2 * NPT + 4:
                        store(i, 0)
                    if s == 2 * NPT + 12:
                        release(i, 0)

            double(0, 0)
            turn(0, True, False)
            with pool.Fori(1, TURNS - 1) as i:
                turn(i, False, False)
            turn(TURNS - 1, False, True)
            store(TURNS - 1, 1)
            pool.wait_ge(stored[0], 16 * TURNS)
            pool.wait_ge(stored[1], 16 * TURNS)

        @block.tensor
        def _(pe):
            for s in (scored, q_turned, w_turned, attended):
                pe.sem_inc(s, CR)

            def turn_q(i, s):
                pe.wait_ge(q_doubled, i * UNITS + (s + 1))
                pe.wait_ge(q_lo_s, done(i, s - 1))
                nc.tensor.transpose(kq[:, 0, 0:P], q4[:, s % 2].rearrange("p a d -> p (a d)"), ps.ident[:]).then_inc(q_turned, 1)

            def turn_k(head, hh, part, q_out):
                pe.wait_ge(q_lo_s, q_out)
                pe.wait_ge(k_split, head + (2 - hh))
                for n in range(4):
                    t = 4 * part + n
                    last = nc.tensor.transpose(kq[:, 0, n * P:(n + 1) * P],
                                               k_parts[:, t, hh].rearrange("p a d -> p (a d)").bitcast(F32), ps.ident[:])
                last.then_inc(k_turned, 1)

            def score(i, s):
                pair, hh, t = where(s)
                n = wide(s)
                pe.wait_ge(sticks, done(i, s - 2))
                if t == 0:
                    pe.wait_ge(k_taken, i * (2 * BODY_HEADS) + 2 * (s // NPT + 1))
                pe.wait_ge(q_lo_s, done(i, s))
                for c in range(0, n, NB):
                    m = min(NB, n - c)
                    own = c + m == n
                    dst = z[:, 2 * (s % 2) + c // NB, 0:m]
                    nc.tensor.matmul(dst, q_hi[:, s % 2, :], k_t[:, hh, c:c + m], start=True, stop=False)
                    last = nc.tensor.matmul(dst, q_lo[:, s % 2, :], k_t[:, hh, c:c + m], start=False, stop=not own)
                    if own:
                        last = nc.tensor.matmul(dst[:, m - P:m], ident_r[:], far_r[:], start=False, stop=True)
                last.then_inc(scored, 1)

            def turn_w(i, s):
                pe.wait_ge(weighed, done(i, s))
                pe.wait_ge(w_taken_a, done(i, s - 1))
                pe.wait_ge(w_taken_v, done(i, s - 1))
                for b in range(wide(s) // P):
                    last = nc.tensor.transpose(wt[:, b // 4, (b % 4) * P:(b % 4 + 1) * P], w[:, s % 2, b * P:(b + 1) * P], ps.ident[:])
                last.then_inc(w_turned, 1)

            def attend(i, s):
                pair, hh, t = where(s)
                pe.wait_ge(w_taken_a, done(i, s))
                pe.wait_ge(w_taken_v, done(i, s))
                pe.wait_ge(out_taken, done(i, s - 1))
                for b in range(t + 1):
                    last = nc.tensor.matmul(out[:, 0, 0:DH], w_t[:, s % 2, b * P:(b + 1) * P],
                                            v2[:, pair, b, hh * DH:(hh + 1) * DH], start=b == 0, stop=b == t)
                last.then_inc(attended, 1)

            def turn(i, first, last):
                for s in range(UNITS):
                    final = last and s + 1 >= UNITS
                    if not final:
                        turn_q(i, s + 1)
                    score(i, s)
                    if not first or s >= 2:
                        turn_w(i, s - 2)
                    if not first or s >= LAG:
                        attend(i, s - LAG)
                    if s % NPT in (3, 5) and not (last and s >= UNITS - NPT):
                        nxt = s // NPT + 1
                        turn_k(i * BODY_HEADS + nxt, nxt % 2, (s % NPT - 3) // 2, done(i, s + 1))
                        pe.wait_ge(k_taken, i * (2 * BODY_HEADS) + (2 * nxt + (s % NPT - 3) // 2 + 1))

            for part in range(2):
                if part:
                    pe.wait_ge(k_taken, 1)
                pe.wait_ge(k_split, 2)
                for n in range(4):
                    last = nc.tensor.transpose(kq[:, 0, n * P:(n + 1) * P],
                                               k_parts[:, 4 * part + n, 0].rearrange("p a d -> p (a d)").bitcast(F32), ps.ident[:])
                last.then_inc(k_turned, 1)
            pe.wait_ge(k_taken, 2)
            turn_q(0, 0)
            turn(0, True, False)
            with pe.Fori(1, TURNS - 1) as i:
                turn(i, False, False)
            turn(TURNS - 1, False, True)
            turn_w(TURNS - 1, UNITS - 2)
            attend(TURNS - 1, UNITS - 3)
            turn_w(TURNS - 1, UNITS - 1)
            attend(TURNS - 1, UNITS - 2)
            attend(TURNS - 1, UNITS - 1)

        @block.scalar
        def _(act):
            act.sem_inc(sticks, CR)
            act.sem_inc(w_taken_a, CR)

            def split_k(i, pair):
                act.wait_ge(loaded[pair % PAIRS], (i + (1 if pair < PAIRS else 2)) * 64)
                src = k2[:, pair % PAIRS].rearrange("p t (h d) -> p t h d", h=2)
                for hh in range(2):
                    last = nc.scalar.copy(k_parts[:, :, hh, 0, :], src[:, :, hh, :])
                last.then_inc(k_hi_s, 1)

            def take_k(i, s, part):
                nxt = s // NPT + 1
                act.wait_ge(k_turned, i * (2 * BODY_HEADS) + (2 * nxt + part + 1))
                nc.scalar.copy(k_t[:, nxt % 2, part * NB:(part + 1) * NB], kq[:, 0, :]).then_inc(k_taken, 1)

            def take_q(i, s):
                act.wait_ge(q_turned, done(i, s))
                act.wait_ge(scored, done(i, s - 2))
                nc.scalar.copy(q_hi[:, s % 2, :], kq[:, 0, 0:P]).then_inc(q_hi_s, 1)

            def stick(i, s):
                n = wide(s)
                if s == 0:
                    act.wait_ge(bias_s, i + 1)
                act.wait_ge(scored, done(i, s))
                act.wait_ge(weighed, done(i, s - 2))
                src = z[:, 2 * (s % 2):2 * (s % 2) + 2, :].rearrange("p a b -> p (a b)")[:, 0:n]
                head = s // NPT
                nc.scalar.activation(keep[:, s % 2, 0:n], src, ACT.Sigmoid, scale=-(DH ** -0.5), bias=bias_now[:, 1, head:head + 1])
                nc.scalar.activation(take[:, s % 2, 0:n], src, ACT.Sigmoid, scale=DH ** -0.5,
                                     bias=bias_now[:, 0, head:head + 1]).then_inc(sticks, 1)

            def take_w(i, s):
                n = min(wide(s), NB)
                act.wait_ge(w_turned, done(i, s))
                act.wait_ge(attended, done(i, s - 2))
                nc.scalar.copy(w_t[:, s % 2, 0:n], wt[:, 0, 0:n]).then_inc(w_taken_a, 1)

            def turn(i, first, last):
                for s in range(UNITS):
                    if not (last and s + 1 >= UNITS):
                        take_q(i, s + 1)
                    stick(i, s)
                    if not first or s >= 2:
                        take_w(i, s - 2)
                    if s % (2 * NPT) == NPT and not (last and s > 2 * NPT):
                        split_k(i, s // (2 * NPT) + 1)
                    if s % NPT in (3, 5) and not (last and s >= UNITS - NPT):
                        take_k(i, s, (s % NPT - 3) // 2)

            act.wait_ge(consts, 32)
            nc.scalar.copy(far_r[:], far_below[:])
            nc.scalar.copy(ident_r[:], ps.ident[:])
            split_k(0, 0)
            for part in range(2):
                act.wait_ge(k_turned, part + 1)
                nc.scalar.copy(k_t[:, 0, part * NB:(part + 1) * NB], kq[:, 0, :]).then_inc(k_taken, 1)
            take_q(0, 0)
            turn(0, True, False)
            with act.Fori(1, TURNS - 1) as i:
                turn(i, False, False)
            turn(TURNS - 1, False, True)
            take_w(TURNS - 1, UNITS - 2)
            take_w(TURNS - 1, UNITS - 1)

        @block.vector
        def _(dve):
            for s in (q_lo_s, weighed, w_taken_v, out_taken):
                dve.sem_inc(s, CR)
            dve.sem_inc(gated, 2)
            nc.vector.memset(after_key[:], 1.0).then_inc(scanned, 1)
            dve.wait_ge(consts, 32)
            nc.vector.tensor_copy(bias[:, 0], bias_row[:])
            nc.vector.tensor_scalar(bias[:, 1], bias_row[:], -1.0, None, ALU.mult).then_inc(scanned, 1)
            dve.wait_ge(scanned, 2)

            def split_k(pair, count):
                dve.wait_ge(k_hi_s, count)
                src = k2[:, pair % PAIRS].rearrange("p t (h d) -> p t h d", h=2)
                for hh in range(2):
                    last = nc.vector.tensor_tensor(k_parts[:, :, hh, 1, :], src[:, :, hh, :], k_parts[:, :, hh, 0, :].bitcast(F32),
                                                   ALU.subtract)
                last.then_inc(k_split, 2)

            def rest_q(i, s):
                dve.wait_ge(q_hi_s, i * UNITS + (s + 1))
                nc.vector.tensor_tensor(q_lo[:, s % 2, :], kq[:, 0, 0:P], q_hi[:, s % 2, :].bitcast(F32), ALU.subtract).then_inc(q_lo_s, 1)

            def weigh(i, s):
                n = wide(s)
                dve.wait_ge(sticks, done(i, s))
                dve.wait_ge(w_turned, done(i, s - 2))
                dve.wait_ge(weighed, done(i, s - 1))
                k, a = keep[:, s % 2, 0:n], after_key[:, s % 2, 0:n]
                nc.vector.tensor_tensor_scan(a[:, ::-1], k[:, ::-1], k[:, ::-1], 1.0, ALU.mult, ALU.bypass).then_inc(scanned, 1)
                dve.wait_ge(scanned, i * UNITS + (s + 3))
                nc.vector.tensor_tensor(w[:, s % 2, 0:n], take[:, s % 2, 0:n], after_key[:, s % 2, 1:n + 1], ALU.mult).then_inc(weighed, 1)

            def take_w(i, s):
                n = wide(s)
                if n <= NB:
                    dve.wait_ge(w_turned, done(i, s))
                    dve.sem_inc(w_taken_v, 1)
                    return
                dve.wait_ge(w_turned, done(i, s))
                dve.wait_ge(attended, done(i, s - 2))
                nc.vector.tensor_copy(w_t[:, s % 2, NB:n], wt[:, 1, 0:n - NB]).then_inc(w_taken_v, 1)

            def gate(i, s):
                pair, hh, t = where(s)
                dve.wait_ge(attended, done(i, s))
                if s % (2 * NPT) == 0:
                    dve.wait_ge(out_free, i * PAIRS + (s // (2 * NPT) + 1))
                cols = slice(hh * DH, (hh + 1) * DH)
                nc.vector.tensor_tensor(o2[:, pair, t, cols], out[:, 0, 0:DH], g2[:, pair, t, cols], ALU.mult).then_inc(out_taken, 1)
                if s % (2 * NPT) == 2 * NPT - 1:
                    dve.wait_ge(out_taken, done(i, s))
                    dve.sem_inc(gated, 1)

            def turn(i, first, last):
                for s in range(UNITS):
                    if not (last and s + 1 >= UNITS):
                        rest_q(i, s + 1)
                    if not first or s >= 1:
                        weigh(i, s - 1)
                    if s == 0:
                        nc.vector.tensor_scalar(bias_now[:], bias[:, :, bass.ds(i * BODY_HEADS, BODY_HEADS)], 1.0, None,
                                                ALU.mult).then_inc(bias_s, 1)
                    if not first or s >= 2:
                        take_w(i, s - 2)
                    if not first or s >= LAG:
                        gate(i, s - LAG)
                    if s % (2 * NPT) == NPT and not (last and s > 2 * NPT):
                        split_k(s // (2 * NPT) + 1, i * PAIRS + (s // (2 * NPT) + 2))

            split_k(0, 1)
            rest_q(0, 0)
            turn(0, True, False)
            with dve.Fori(1, TURNS - 1) as i:
                turn(i, False, False)
            turn(TURNS - 1, False, True)
            end = TURNS - 1
            weigh(end, UNITS - 1)
            take_w(end, UNITS - 2)
            gate(end, UNITS - 3)
            take_w(end, UNITS - 1)
            gate(end, UNITS - 2)
            gate(end, UNITS - 1)


def sample_attention(nc, t_in, t_out, ps):
    ctx = ExitStack()
    with ctx:
        def sb(name, shape, dt=F32):
            return ctx.enter_context(nc.sbuf_tensor(f"sa_{name}", shape, dt))

        sem = semaphores(nc, ctx, "sa")

        def bank(name, n=1):
            return ctx.enter_context(nc.psum_tensor(f"sa_{name}", [P, n, NB], F32))

        HP = AH // 2
        NK = PAST + NS
        pages = sb("pages", [1, DB * NPG], I32)
        hidden = sb("hidden", [P, 2, DB, NS])
        bias = sb("bias", [P, 2])
        new_rows = sb("new_rows", [NS, 4, D])
        new_t = sb("new_t", [P, 3, HP, NS])
        k_pages = sb("k_pages", [P, 2, NPG, D])
        v_pages = sb("v_pages", [P, 2, NPG, D])
        k_t = sb("k_t", [P, HP, PAST])
        q_diag = sb("q_diag", [P, 2, HP, P])
        take = sb("take", [P, 2, NK])
        keep = sb("keep", [P, 2, NK])
        after_key = sb("after_key", [P, 2, NK + 8])
        w = sb("w", [P, 2, NK])
        w_t = sb("w_t", [P, 2, NPG + 1, P])
        o_t = sb("o_t", [P, HP, NS])
        o_rows = sb("o_rows", [NS, D])
        kt, z, wt, out = bank("kt", 4), bank("z", 2), bank("wt"), bank("out")
        pages_s, consts, cleared = sem("pages_s"), sem("consts"), sem("cleared")
        loaded = [sem("loaded0"), sem("loaded1")]
        new_turned, new_taken, k_turned, k_taken, placed = (sem("new_turned"), sem("new_taken"), sem("k_turned"),
                                                            sem("k_taken"), sem("placed"))
        scored, sticks, masked, weighed, scanned = sem("scored"), sem("sticks"), sem("masked"), sem("weighed"), sem("scanned")
        w_turned, w_taken, attended, gated, stored = (sem("w_turned"), sem("w_taken"), sem("attended"), sem("gated"),
                                                      sem("stored"))
        back, back_taken = sem("back"), sem("back_taken")
        block = ctx.enter_context(nc.Block())
        CR = 2

        def done(i, b):
            return i * 2 + (b + 1 + CR)

        @block.sync
        def _(sp):
            sp.dma_start(pages[:], t_in["page_table"].rearrange("b (o n) -> o (b n)", o=1)).then_inc(pages_s, 16)
            sp.dma_start(hidden[:], t_in["hidden_s"]).then_inc(consts, 16)
            bias_col = t_in["sb_bias"].rearrange("o (h u) -> (o h) u", u=1)
            for hh in range(AH):
                sp.dma_start(bias[hh * DS:(hh + 1) * DS, 0:1], bias_col[hh:hh + 1, :].to_broadcast([DS, 1])).then_inc(consts, 16)
            for n, src in enumerate((ps.q_rows[SEQ:SEQ + NS, :], t_out["k_sample"].rearrange("b i h d -> (b i) (h d)"),
                                     t_out["v_sample"].rearrange("b i h d -> (b i) (h d)"), ps.g_rows[SEQ:SEQ + NS, :])):
                sp.dma_start(new_rows[:, n, :], src).then_inc(consts, 16)
            sp.wait_ge(pages_s, 16)
            with sp.Fori(0, DB // 2) as i:
                for b in range(2):
                    sp.wait_ge(attended, i * 2 + (b + 1))
                    for n in range(NPG):
                        page = sp.value_load(pages[0:1, bass.ds(i * (2 * NPG) + b * NPG + n, 1)], min_val=0,
                                             max_val=t_in["cache_k"].shape[0] - 1)
                        for buf, cache in ((k_pages, "cache_k"), (v_pages, "cache_v")):
                            sp.dma_start(buf[:, b, n, :], t_in[cache][bass.ds(page, 1)].rearrange("o s h d -> (o s) (h d)")).then_inc(loaded[b], 16)

        CONSTS = 16 * (1 + AH + 4)

        @block.gpsimd
        def _(pool):
            nc.gpsimd.memset(q_diag[:], 0.0).then_inc(cleared, 1)
            pool.wait_ge(back_taken, HP // 4)
            pool.dma_start(ps.attended[SEQ:SEQ + NS, :], o_rows[:]).then_inc(stored, 16)
            pool.wait_ge(stored, 16)

        @block.tensor
        def _(pe):
            for s in (k_turned, scored, w_turned, attended):
                pe.sem_inc(s, CR)
            pe.wait_ge(consts, CONSTS)
            for n, src in enumerate((0, 1, 3)):
                for k in range(HP):
                    last = nc.tensor.transpose(kt[:, n, k * NS:(k + 1) * NS], new_rows[:, src, k * P:(k + 1) * P], ps.ident[0:NS, 0:NS])
                last.then_inc(new_turned, 1)
            pe.wait_ge(new_taken, 3)

            def turn_k(i, b):
                pe.wait_ge(k_taken, i * 8 + (b * 4 + CR))
                pe.wait_ge(loaded[b], i * 64 + 64)
                for k in range(HP):
                    for n in range(NPG):
                        c0 = (k % 2) * PAST + n * P
                        last = nc.tensor.transpose(kt[:, k // 2, c0:c0 + P], k_pages[:, b, n, k * P:(k + 1) * P], ps.ident[:])
                last.then_inc(k_turned, 1)

            def score(i, b):
                pe.wait_ge(sticks, done(i, b - 2))
                pe.wait_ge(placed, i * 2 + (b + 1))
                pe.wait_ge(k_taken, i * 8 + (b * 4 + 4 + CR))
                for k in range(HP):
                    nc.tensor.matmul(z[:, b, 0:PAST], q_diag[:, b, k, :], k_t[:, k, :], start=k == 0, stop=k == HP - 1)
                for k in range(HP):
                    last = nc.tensor.matmul(z[:, b, PAST:NK], q_diag[:, b, k, :], new_t[:, 1, k, :], start=k == 0, stop=k == HP - 1)
                last.then_inc(scored, 1)

            def attend(i, b):
                pe.wait_ge(weighed, done(i, b))
                pe.wait_ge(w_taken, done(i, b - 1))
                for n in range(NPG):
                    nc.tensor.transpose(wt[:, 0, n * P:(n + 1) * P], w[:, b, n * P:(n + 1) * P], ps.ident[:])
                nc.tensor.transpose(wt[0:NS, 0, NPG * P:(NPG + 1) * P], w[:, b, PAST:NK], ps.ident[:]).then_inc(w_turned, 1)
                pe.wait_ge(w_taken, done(i, b))
                pe.wait_ge(gated, done(i, b - 1))
                for k in range(HP):
                    dst = out[:, 0, k * 2 * DS:(k + 1) * 2 * DS]
                    cols = slice(k * 2 * DS, (k + 1) * 2 * DS)
                    for n in range(NPG):
                        nc.tensor.matmul(dst, v_pages[:, b, n, k * P:(k + 1) * P], w_t[:, b, n, cols], start=n == 0, stop=False)
                    last = nc.tensor.matmul(dst, new_rows[:, 2, k * P:(k + 1) * P], w_t[0:NS, b, NPG, cols], start=False, stop=True)
                last.then_inc(attended, 1)

            turn_k(0, 0)
            score(0, 0)
            with pe.Fori(0, DB // 2 - 1) as i:
                for b in range(2):
                    turn_k(i, b + 1) if b == 0 else turn_k(i + 1, 0)
                    score(i, b + 1) if b == 0 else score(i + 1, 0)
                    attend(i, b)
            end = DB // 2 - 1
            turn_k(end, 1)
            score(end, 1)
            attend(end, 0)
            attend(end, 1)
            pe.wait_ge(gated, DB + CR)
            for k in range(HP):
                last = nc.tensor.transpose(kt[0:NS, k // 4, (k % 4) * P:(k % 4 + 1) * P], o_t[:, k, :], ps.ident[:])
            last.then_inc(back, 1)

        @block.scalar
        def _(act):
            act.sem_inc(sticks, CR)
            act.sem_inc(k_taken, CR)
            act.wait_ge(cleared, 2)
            for n in range(3):
                act.wait_ge(new_turned, n + 1)
                nc.scalar.copy(new_t[:, n].rearrange("p k c -> p (k c)"), kt[:, n, :]).then_inc(new_taken, 1)

            def step(i, b):
                act.wait_ge(k_turned, done(i, b))
                act.wait_ge(scored, done(i, b - 1))
                for q in range(4):
                    nc.scalar.copy(k_t[:, 2 * q:2 * q + 2, :].rearrange("p k c -> p (k c)"), kt[:, q, :]).then_inc(k_taken, 1)
                act.wait_ge(scored, done(i, b))
                act.wait_ge(weighed, done(i, b - 2))
                nc.scalar.activation(keep[:, b], z[:, b, 0:NK], ACT.Sigmoid, scale=-(DH ** -0.5), bias=bias[:, 1:2])
                nc.scalar.activation(take[:, b], z[:, b, 0:NK], ACT.Sigmoid, scale=DH ** -0.5, bias=bias[:, 0:1]).then_inc(sticks, 1)

            with act.Fori(0, DB // 2) as i:
                for b in range(2):
                    step(i, b)
            act.wait_ge(back, 1)
            for n in range(2):
                nc.scalar.copy(o_rows[:, n * NB:(n + 1) * NB], kt[0:NS, n, :]).then_inc(back_taken, 1)

        @block.vector
        def _(dve):
            for s in (weighed, w_taken, gated):
                dve.sem_inc(s, CR)
            nc.vector.memset(after_key[:], 1.0)
            dve.wait_ge(consts, CONSTS)
            nc.vector.tensor_scalar(bias[:, 1:2], bias[:, 0:1], -1.0, None, ALU.mult).then_inc(cleared, 1)
            dve.wait_ge(cleared, 2)
            dve.wait_ge(new_taken, 3)

            def place(i, b):
                dve.wait_ge(scored, done(i, b - 2))
                for hh in range(2):
                    part = slice(hh * DH, (hh + 1) * DH)
                    flat = q_diag[part, b].rearrange("p k c -> p (k c)")[:, hh * DS:]
                    dst = bass.AP(flat.tensor, flat.offset, [list(flat.ap[0]), [P + 2 * DS, HP], [1, DS]])
                    last = nc.vector.tensor_scalar(dst, new_t[part, 0, :, bass.ds(i * (2 * DS) + b * DS, DS)], 1.0, None, ALU.mult)
                last.then_inc(placed, 1)

            def weigh(i, b):
                dve.wait_ge(sticks, done(i, b))
                dve.wait_ge(scanned, i * 4 + (2 * b + 1))
                seq = bass.ds(i * 2 + b, 1)
                for buf, n, op in ((keep, 0, ALU.max), (take, 1, ALU.mult)):
                    last = nc.vector.tensor_tensor(buf[:, b, PAST:NK], buf[:, b, PAST:NK],
                                                   hidden[:, n, seq, :].rearrange("p o c -> p (o c)"), op)
                last.then_inc(scanned, 1)
                dve.wait_ge(scanned, i * 4 + (2 * b + 2))
                k = keep[:, b]
                nc.vector.tensor_tensor_scan(after_key[:, b, 0:NK][:, ::-1], k[:, ::-1], k[:, ::-1], 1.0, ALU.mult, ALU.bypass).then_inc(scanned, 1)
                dve.wait_ge(scanned, i * 4 + (2 * b + 3))
                dve.wait_ge(w_turned, done(i, b - 2))
                nc.vector.tensor_tensor(w[:, b], take[:, b], after_key[:, b, 1:NK + 1], ALU.mult).then_inc(weighed, 1)

            def finish(i, b):
                dve.wait_ge(w_turned, done(i, b))
                dve.wait_ge(attended, done(i, b - 2))
                nc.vector.tensor_copy(w_t[:, b, 0:NPG], wt[:, 0, 0:NPG * P].rearrange("p (n c) -> p n c", n=NPG))
                nc.vector.tensor_copy(w_t[0:NS, b, NPG], wt[0:NS, 0, NPG * P:(NPG + 1) * P]).then_inc(w_taken, 1)
                dve.wait_ge(attended, done(i, b))
                for hh in range(2):
                    part = slice(hh * DH, (hh + 1) * DH)
                    src = out[part, 0, 0:HP * 2 * DS].rearrange("p (k a i) -> p k a i", k=HP, a=2)[:, :, hh, :]
                    cols = bass.ds(i * (2 * DS) + b * DS, DS)
                    last = nc.vector.tensor_tensor(o_t[part, :, cols], src, new_t[part, 2, :, cols], ALU.mult)
                last.then_inc(gated, 1)

            dve.sem_inc(scanned, 1)
            place(0, 0)
            with dve.Fori(0, DB // 2 - 1) as i:
                for b in range(2):
                    place(i, 1) if b == 0 else place(i + 1, 0)
                    weigh(i, b)
                    finish(i, b)
            end = DB // 2 - 1
            place(end, 1)
            for b in range(2):
                weigh(end, b)
                finish(end, b)


def outward(nc, ps, tag, rows_in, w_rows, KT, w_gain, layer, x, finish):
    ctx = ExitStack()
    with ctx:
        def sb(name, shape, dt=F32):
            return ctx.enter_context(nc.sbuf_tensor(f"{tag}_{name}", shape, dt))

        sem = semaphores(nc, ctx, tag)

        NH = D // NB
        GR = KT // 4
        w_hi = sb("w_hi", [P, KT, NB], F32R)
        pairs = [overlaid(nc, ctx, f"{tag}_w_lo{n}", f"{tag}_w_raw{n}", [P, KT, NB]) for n in range(NH)]
        w_lo, w_raw = [p[0] for p in pairs], [p[1] for p in pairs]
        gate_p = sb("gate_p", [P, D])
        gate_s = sb("gate_s", [NS, D])
        a = sb("a", [P, KT * P])
        a_hi = sb("a_hi", [P, 2, KT, P], F32R)
        a_lo = sb("a_lo", [P, 2, KT, P], F32R)
        scaled = sb("scaled", [P, 2, NB])
        tr = ctx.enter_context(nc.psum_tensor(f"{tag}_tr", [P, 4, NB], F32))
        acc = ctx.enter_context(nc.psum_tensor(f"{tag}_acc", [P, 2, NB], F32))
        spread = ctx.enter_context(nc.psum_tensor(f"{tag}_spread", [P, 2, NB], F32))
        x_loaded, a_loaded = sem("x_loaded"), sem("a_loaded")
        w_loaded = [sem("w_loaded0"), sem("w_loaded1")]
        hi_s, lo_s, gate_s_s, gate_taken = sem("w_hi_s"), sem("w_lo_s"), sem("gate_spread"), sem("gate_taken")
        turned, a_hi_s, a_lo_s, made, scaled_s, added = (sem("turned"), sem("a_hi_s"), sem("a_lo_s"), sem("made"),
                                                         sem("scaled_s"), sem("added"))
        stored = sem("stored")
        block = ctx.enter_context(nc.Block())
        SPLITS = 4
        KS = KT // SPLITS

        CR = 2

        @block.sync
        def _(sp):
            w = w_rows.rearrange("(k p) n -> p k n", p=P)
            for n in range(NH):
                sp.dma_start(w_raw[n][:], w[:, :, n * NB:(n + 1) * NB]).then_inc(w_loaded[n], 16)
            if finish.load is not None:
                finish.load(sp, x, x_loaded)
            for n in range(NH):
                with sp.Fori(0, NPT) as t:
                    sp.wait_ge(turned, t + (n * NT + CR))
                    sp.dma_start(a[:], rows_in[bass.ds(t * P, P), :]).then_inc(a_loaded, 16)
                sp.wait_ge(turned, NPT + n * NT + CR)
                sp.dma_start(a[0:NS, :], rows_in[SEQ:SEQ + NS, :]).then_inc(a_loaded, 16)

        @block.tensor
        def _(pe):
            pe.sem_inc(turned, CR)
            pe.sem_inc(made, CR)
            for n in range(NH):
                nc.tensor.matmul(spread[:, n, :], ps.selector[:, 0:P], ps.gate[:, layer, n * NB:(n + 1) * NB],
                                 start=True, stop=True).then_inc(gate_s_s, 1)
            pe.wait_ge(gate_taken, 2)
            for n in range(NH):
                nc.tensor.matmul(spread[0:NS, n, :], ps.selector[:, P:P + NS], ps.gate[:, layer, n * NB:(n + 1) * NB],
                                 start=True, stop=True).then_inc(gate_s_s, 1)

            def turn(n, j):
                pe.wait_ge(a_loaded, (j + (n * NT + 1)) * 16)
                pe.wait_ge(a_lo_s, (j + (n * NT)) * GR + CR)
                for k in range(KT):
                    last = nc.tensor.transpose(tr[:, k // 4, (k % 4) * P:(k % 4 + 1) * P], a[:, k * P:(k + 1) * P], ps.ident[:])
                last.then_inc(turned, 1)

            def multiply(n, b, j, r):
                pe.wait_ge(a_lo_s, (j + (n * NT + 1)) * GR + CR)
                pe.wait_ge(added, j + (n * NT + CR - 1))
                for k in range(KT):
                    nc.tensor.matmul(acc[0:r, b, :], a_hi[:, b, k, 0:r], w_hi[:, k, :], start=k == 0, stop=False)
                    nc.tensor.matmul(acc[0:r, b, :], a_hi[:, b, k, 0:r], w_lo[n][:, k, :], start=False, stop=False)
                    last = nc.tensor.matmul(acc[0:r, b, :], a_lo[:, b, k, 0:r], w_hi[:, k, :], start=False, stop=k == KT - 1)
                last.then_inc(made, 1)

            for n in range(NH):
                turn(n, 0)
                pe.wait_ge(lo_s, SPLITS * (n + 1))
                with pe.Fori(0, NPT // 2) as i:
                    turn(n, i * 2 + 1)
                    multiply(n, 0, i * 2, P)
                    turn(n, i * 2 + 2)
                    multiply(n, 1, i * 2 + 1, P)
                multiply(n, 0, NPT, NS)

        @block.scalar
        def _(act):
            act.wait_ge(gate_s_s, 2)
            nc.scalar.copy(gate_p[:], spread[:].rearrange("p a b -> p (a b)")).then_inc(gate_taken, 2)
            act.wait_ge(gate_s_s, 4)
            nc.scalar.copy(gate_s[:], spread[0:NS].rearrange("p a b -> p (a b)")).then_inc(gate_taken, 1)

            def take(n, b, j):
                act.wait_ge(turned, j + (n * NT + CR + 1))
                act.wait_ge(made, j + (n * NT + CR - 1))
                for q in range(GR):
                    nc.scalar.copy(a_hi[:, b, 4 * q:4 * q + 4, :].rearrange("p k c -> p (k c)"), tr[:, q, :]).then_inc(a_hi_s, 1)

            for n in range(NH):
                act.wait_ge(w_loaded[n], 16)
                if n:
                    act.wait_ge(made, n * NT + CR)
                for k in range(KT):
                    scale = ps.ret_g[:, k:k + 1] if w_gain else 1.0
                    last = nc.scalar.activation(w_hi[:, k, :], w_raw[n][:, k, :], ACT.Copy, scale=scale)
                    if k % KS == KS - 1:
                        last.then_inc(hi_s, 1)
                take(n, 0, 0)
                with act.Fori(0, NPT // 2) as i:
                    take(n, 1, i * 2 + 1)
                    take(n, 0, i * 2 + 2)

        @block.vector
        def _(dve):
            dve.sem_inc(a_lo_s, CR)
            dve.sem_inc(added, CR)
            dve.wait_ge(gate_taken, 3)

            def take(n, b, j):
                for q in range(GR):
                    dve.wait_ge(a_hi_s, (j + n * NT) * GR + (q + 1))
                    cols = a_hi[:, b, 4 * q:4 * q + 4, :].rearrange("p k c -> p (k c)")
                    nc.vector.tensor_tensor(a_lo[:, b, 4 * q:4 * q + 4, :].rearrange("p k c -> p (k c)"), tr[:, q, :],
                                            cols.bitcast(F32), ALU.subtract).then_inc(a_lo_s, 1)

            def add(n, b, j, r, t):
                gate = gate_p[:, n * NB:(n + 1) * NB] if r == P else gate_s[:, n * NB:(n + 1) * NB]
                xs = x[0:r, t, n * NB:(n + 1) * NB]
                if not isinstance(t, int):
                    xs = xs.rearrange("p o c -> p (o c)")
                dve.wait_ge(made, j + (n * NT + CR + 1))
                nc.vector.tensor_tensor(scaled[0:r, b, :], acc[0:r, b, :], gate, ALU.mult).then_inc(scaled_s, 1)
                dve.wait_ge(scaled_s, j + (n * NT + 1))
                nc.vector.tensor_tensor(xs, xs, scaled[0:r, b, :], ALU.add).then_inc(added, 1)

            for n in range(NH):
                for q in range(SPLITS):
                    dve.wait_ge(hi_s, n * SPLITS + q + 1)
                    for k in range(KS * q, KS * (q + 1)):
                        if w_gain:
                            last = nc.vector.scalar_tensor_tensor(w_lo[n][:, k, :], w_raw[n][:, k, :], ps.ret_g[:, k:k + 1],
                                                                  w_hi[:, k, :].bitcast(F32), ALU.mult, ALU.subtract)
                        else:
                            last = nc.vector.tensor_tensor(w_lo[n][:, k, :], w_raw[n][:, k, :],
                                                           w_hi[:, k, :].bitcast(F32), ALU.subtract)
                    last.then_inc(lo_s, 1)
                if n == 0 and finish.load is not None:
                    dve.wait_ge(x_loaded, 32)
                take(n, 0, 0)
                with dve.Fori(0, NPT // 2) as i:
                    take(n, 1, i * 2 + 1)
                    add(n, 0, i * 2, P, bass.ds(i * 2, 1))
                    take(n, 0, i * 2 + 2)
                    add(n, 1, i * 2 + 1, P, bass.ds(i * 2 + 1, 1))
                add(n, 0, NPT, NS, NPT)

        if finish.store is not None:
            @block.gpsimd
            def _(pool):
                finish.store(pool, x, added, stored, CR)


class Finish:
    def __init__(self, load=None, store=None):
        self.load, self.store = load, store


def reload_x(t_in):
    def load(sp, x, sem):
        sp.dma_start(x[:, 0:NPT, :], t_in["x_prompt"][0].rearrange("(t p) d -> p t d", p=P)).then_inc(sem, 16)
        sp.dma_start(x[0:NS, NPT, :], t_in["x_sample"].rearrange("b i d -> (b i) d")).then_inc(sem, 16)
    return load


def store_y(t_out):
    def store(pool, x, added, stored, CR):
        with pool.Fori(0, NPT) as t:
            pool.wait_ge(added, t + (NT + CR + 1))
            pool.dma_start(t_out["y_prompt"][0][bass.ds(t * P, P), :], x[:, bass.ds(t, 1), :].rearrange("p o d -> p (o d)")).then_inc(stored, 16)
        pool.wait_ge(added, 2 * NT + CR)
        pool.dma_start(t_out["y_sample"].rearrange("b i d -> (b i) d"), x[0:NS, NPT, :]).then_inc(stored, 16)
        pool.wait_ge(stored, 16 * NT)
    return store


def shared_kv_and_queries(nc, t_in, t_out, ps, x):
    ctx = ExitStack()
    with ctx:
        hi = ctx.enter_context(nc.sbuf_tensor("kq_h_hi", [P, KD, SEQ + NS], F32R))
        lo = ctx.enter_context(nc.sbuf_tensor("kq_h_lo", [P, KD, SEQ + NS], F32R))

        def out_rows(name):
            return (t_out[name + "_prompt"][0].rearrange("s h d -> s (h d)"),
                    t_out[name + "_sample"].rearrange("b i h d -> (b i) (h d)"))

        def scratch(ap):
            return ap[0:SEQ, :], ap[SEQ:SEQ + NS, :]

        normed_transposed(nc, ps, x, hi, lo, 1, "kn")
        project_rows(nc, ps, "kv", hi, lo, t_in["w_kv"], ps.k_gain, ACT.Copy, out_rows("k"), out_rows("v"))
        normed_transposed(nc, ps, x, hi, lo, 2, "qn")
        project_rows(nc, ps, "qg", hi, lo, t_in["sb_w_in"][0], ps.q_gain, ACT.Silu, scratch(ps.q_rows), scratch(ps.g_rows))


def project_rows(nc, ps, tag, h_hi, h_lo, w_dram, head_gain, func, first, second):
    ctx = ExitStack()
    with ctx:
        def sb(name, shape, dt=F32):
            return ctx.enter_context(nc.sbuf_tensor(f"{tag}_{name}", shape, dt))

        sem = semaphores(nc, ctx, tag)

        NCH = 2 * D // NB
        HC = NB // DH
        w_hi = sb("w_hi", [P, 2, KD, NB], F32R)
        pairs = [overlaid(nc, ctx, f"{tag}_w_lo{n}", f"{tag}_w_raw{n}", [P, KD, NB]) for n in range(2)]
        w_lo, w_raw = [p[0] for p in pairs], [p[1] for p in pairs]
        y = sb("y", [P, 2, NB])
        squares = sb("squares", [P, 2, NB])
        ss = sb("ss", [P, 2, HC])
        root = sb("root", [P, 2, HC])
        rstd = sb("rstd", [P, 2, HC])
        out = sb("out", [P, 2, NB])
        acc = ctx.enter_context(nc.psum_tensor(f"{tag}_acc", [P, 4, NB], F32))
        w_loaded = [sem("w_loaded0"), sem("w_loaded1")]
        hi_s, lo_s, made = sem("w_hi_s"), sem("w_lo_s"), sem("made")
        taken, squared, summed, rooted, normed, ready = (sem("taken"), sem("squared"), sem("summed"), sem("rooted"),
                                                         sem("normed"), sem("ready"))
        own = sem("own")
        stored = [sem("stored0"), sem("stored1")]
        block = ctx.enter_context(nc.Block())
        SPLITS = 2
        KS = KD // SPLITS
        steps = [(c, t) for c in range(NCH) for t in range(NT)]
        NORMED = NCH // 2 * NT

        @block.sync
        def _(sp):
            w = w_dram.rearrange("(k p) n -> p k n", p=P)
            for c in range(NCH):
                if c >= 2:
                    sp.wait_ge(made, (c - 1) * NT)
                sp.dma_start(w_raw[c % 2][:], w[:, :, c * NB:(c + 1) * NB]).then_inc(w_loaded[c % 2], 16)

        @block.tensor
        def _(pe):
            for s, (c, t) in enumerate(steps):
                r = rows(t)
                if t == 0:
                    pe.wait_ge(lo_s, SPLITS * (c + 1))
                if s >= 4:
                    pe.wait_ge(taken, s - 3)
                cols = slice(t * P, t * P + r)
                for k in range(KD):
                    nc.tensor.matmul(acc[0:r, s % 4, :], h_hi[:, k, cols], w_hi[:, c % 2, k, :], start=k == 0, stop=False)
                    nc.tensor.matmul(acc[0:r, s % 4, :], h_hi[:, k, cols], w_lo[c % 2][:, k, :], start=False, stop=False)
                    last = nc.tensor.matmul(acc[0:r, s % 4, :], h_lo[:, k, cols], w_hi[:, c % 2, k, :], start=False, stop=k == KD - 1)
                last.then_inc(made, 1)

        @block.scalar
        def _(act):
            def split(c, q):
                act.wait_ge(w_loaded[c % 2], 16 * (c // 2 + 1))
                part = slice(KS * q, KS * (q + 1))
                nc.scalar.copy(w_hi[:, c % 2, part, :], w_raw[c % 2][:, part, :]).then_inc(hi_s, 1)

            for q in range(SPLITS):
                split(0, q)
            for s, (c, t) in enumerate(steps):
                r = rows(t)
                act.wait_ge(made, s + 1)
                if s < NORMED:
                    if s >= 2:
                        act.wait_ge(normed, s - 1)
                        act.wait_ge(summed, s - 1)
                    nc.scalar.activation(squares[0:r, s % 2, :], acc[0:r, s % 4, :], ACT.Square).then_inc(squared, 1)
                    nc.scalar.copy(y[0:r, s % 2, :], acc[0:r, s % 4, :]).then_inc(taken, 1)
                    act.wait_ge(summed, s + 1)
                    nc.scalar.activation(root[0:r, s % 2, :], ss[0:r, s % 2, :], ACT.Sqrt, scale=1.0 / DH,
                                         bias=ps.eps[0:r]).then_inc(rooted, 1)
                else:
                    act.wait_ge(stored[s % 2], 16 * (s // 2))
                    nc.scalar.activation(out[0:r, s % 2, :], acc[0:r, s % 4, :], func).then_inc(taken, 1)
                if t in (3, 5) and c + 1 < NCH:
                    split(c + 1, (t - 3) // 2)

        @block.vector
        def _(dve):
            def split(c, q):
                dve.wait_ge(hi_s, SPLITS * c + q + 1)
                part = slice(KS * q, KS * (q + 1))
                nc.vector.tensor_tensor(w_lo[c % 2][:, part, :], w_raw[c % 2][:, part, :], w_hi[:, c % 2, part, :].bitcast(F32),
                                        ALU.subtract).then_inc(lo_s, 1)

            for q in range(SPLITS):
                split(0, q)
            for s, (c, t) in enumerate(steps):
                r = rows(t)
                if s < NORMED:
                    def heads(buf):
                        return buf[0:r, s % 2, :].rearrange("p (h d) -> p h d", h=HC)

                    dve.wait_ge(squared, s + 1)
                    nc.vector.tensor_reduce(ss[0:r, s % 2, :], heads(squares), AX.X, ALU.add).then_inc(summed, 1)
                    dve.wait_ge(rooted, s + 1)
                    nc.vector.reciprocal(rstd[0:r, s % 2, :], root[0:r, s % 2, :]).then_inc(own, 1)
                    dve.wait_ge(own, 2 * s + 1)
                    nc.vector.tensor_tensor(heads(squares), heads(y), rstd[0:r, s % 2, :].unsqueeze(2).to_broadcast([r, HC, DH]),
                                            ALU.mult).then_inc(own, 1)
                    dve.wait_ge(own, 2 * s + 2)
                    if s >= 2:
                        dve.wait_ge(stored[s % 2], 16 * (s // 2))
                    nc.vector.tensor_tensor(heads(out), heads(squares), head_gain[0:r].unsqueeze(1).to_broadcast([r, HC, DH]),
                                            ALU.mult).then_inc(ready, 1)
                    dve.sem_inc(normed, 1)
                if t in (3, 5) and c + 1 < NCH:
                    split(c + 1, (t - 3) // 2)

        @block.gpsimd
        def _(pool):
            for s, (c, t) in enumerate(steps):
                r = rows(t)
                dst = (first if c < NCH // 2 else second)[0 if t < NPT else 1]
                c0 = (c % (NCH // 2)) * NB
                if s < NORMED:
                    pool.wait_ge(ready, s + 1)
                else:
                    pool.wait_ge(taken, s + 1)
                r0 = t * P if t < NPT else 0
                pool.dma_start(dst[r0:r0 + r, c0:c0 + NB], out[0:r, s % 2, :]).then_inc(stored[s % 2], 16)
            for n in range(2):
                pool.wait_ge(stored[n], 16 * len([s for s in range(len(steps)) if s % 2 == n]))


def diagonal(buf, blocks, width, n):
    flat = buf[:].rearrange("p b c -> p (b c)")
    return bass.AP(flat.tensor, flat.offset, [list(flat.ap[0]), [width + n, blocks], [1, n]])


def overlaid(nc, ctx, name, raw_name, shape):
    at = nc.sbuf_base
    lo = ctx.enter_context(nc.sbuf_tensor(name, shape, F32R))
    return lo, nc.alloc_sbuf_tensor_at(raw_name, shape, F32, offset=at)


def shape_constants():
    import numpy as np

    f = np.float32
    half = DK // 2
    inv_freq = 10000.0 ** (-np.arange(half, dtype=f) / f(half))
    pos = np.zeros((P, NT), f)
    pos[:, :NPT] = np.arange(SEQ).reshape(NPT, P).T
    pos[:, NPT] = PAST + np.arange(P) % DS
    ang = (pos[:, :, None] * inv_freq.astype(f)).astype(f)
    cos, sin = np.cos(ang), np.sin(ang)
    log_gamma = np.log1p(-np.exp2(-5.0 - np.arange(H)))
    decays = np.zeros((P, 2, 3, H))
    for kind, chunk in ((0, P), (1, DS)):
        i = (np.arange(P) % chunk)[:, None]
        decays[:, kind, 0] = np.exp(log_gamma * (i + 1.0))
        decays[:, kind, 1] = np.exp(-log_gamma * (i + 1.0)) * DK ** -0.5
        decays[:, kind, 2] = np.exp(log_gamma * chunk)
    j, i = np.arange(P)[:, None], np.arange(P)[None]
    causal = np.zeros((P, P + NS))
    causal[:, :P] = j <= i
    js, is_ = np.arange(NS)[:, None], np.arange(NS)[None]
    causal[:NS, P:] = (js <= is_) & (js // DS == is_ // DS)
    selector = np.zeros((NC, P + NS))
    selector[0, :P] = 1
    for b in range(DB):
        selector[1 + b, P + b * DS:P + (b + 1) * DS] = 1
    own_rows = (np.arange(NS)[:, None] // DS == np.arange(DB)[None])
    q, s = np.arange(P)[:, None], np.arange(P)[None]
    hidden = (s >= q)
    hq = np.arange(P) % DS
    tok = np.arange(NS)
    hidden_s = np.ones((P, DB, NS))
    for b in range(DB):
        hidden_s[:, b] = ~((tok[None] // DS == b) & (tok[None] % DS < hq[:, None]))
    out = {
        "ident": np.eye(P), "selector": selector, "own_rows": own_rows, "causal": causal, "decays": decays,
        "rope_cos": np.concatenate([cos, cos], -1), "rope_sin": np.concatenate([-sin, sin], -1),
        "far_below": hidden * FAR, "hidden_s": np.stack([hidden_s, 1 - hidden_s], 1),
    }
    return {k: np.ascontiguousarray(x, dtype=f) for k, x in out.items()}


INPUTS = ["x_prompt", "x_sample", "state_ret", "cache_k", "cache_v", "page_table", "c_prompt", "c_sample", "ada_w",
          "ada_b", "norm_g", "ret_w_in", "ret_norm_g", "ret_w_out", "kv_norm_g", "w_kv", "sb_q_g", "sb_k_g",
          "sb_w_in", "sb_w_out", "sb_bias"]
OUTPUTS = {"y_prompt": (1, SEQ, D), "y_sample": (DB, DS, D), "st_prompt": (1, 1, H, DK, DV),
           "st_sample": (1, DB, H, DK, DV), "k_prompt": (1, SEQ, AH, DH), "v_prompt": (1, SEQ, AH, DH),
           "k_sample": (DB, DS, AH, DH), "v_sample": (DB, DS, AH, DH)}


def kernel(**inputs):
    import numpy as np
    import concourse.bacc as bacc
    from concourse.bass_utils import run_bass_kernel_spmd

    nc = bacc.Bacc("TRN2", target_bir_lowering=False, num_devices=1)
    arrays = {name: np.ascontiguousarray(inputs[name]) for name in INPUTS}
    arrays.update(shape_constants())
    t_in = {name: nc.dram_tensor("in_" + name, a.shape, mybir.dt.from_np(a.dtype), kind="ExternalInput").ap()
            for name, a in arrays.items()}
    t_out = {name: nc.dram_tensor("out_" + name, shape, F32, kind="ExternalOutput").ap() for name, shape in OUTPUTS.items()}
    build_program(nc, t_in, t_out)
    results = run_bass_kernel_spmd(nc, [{"in_" + n: a for n, a in arrays.items()}], core_ids=[0]).results[0]
    return tuple(results["out_" + name] for name in OUTPUTS)
```

```python
import math
from contextlib import ExitStack

import concourse.bass as bass
from concourse import mybir
from concourse.alu_op_type import AluOpType as ALU

ACT = mybir.ActivationFunctionType
AX = mybir.AxisListType
F32 = mybir.dt.float32
F32R = mybir.dt.float32r
I32 = mybir.dt.int32

P = 128
D = 1024
KD = D // P
SEQ = 1024
NPT = SEQ // P
NT = NPT + 1
DB, DS = 8, 8
NS = DB * DS
NC = 1 + DB
PAST = 256
PAGE = 128
NPG = PAST // PAGE
H = 8
DK, DV = 128, 256
AH = 16
DH = 64
NB = 512
EPS = 1e-6
FAR = -2.0 ** 30


def semaphores(nc, ctx, prefix):
    made = []

    def sem(name):
        made.append(nc.alloc_semaphore(f"{prefix}_{name}"))
        return made[-1]

    def give_back():
        nc.clear_and_free_semaphores(made)
        nc.all_engine_barrier()

    ctx.callback(give_back)
    return sem


def rows(t):
    return P if t < NPT else NS


class Count:

    def __init__(self):
        self.base, self.n, self.turn, self.per = 0, 0, None, 0

    def up(self, k=1):
        self.n += k
        return k

    def now(self):
        if self.turn is None:
            return self.base + self.n
        return self.turn * self.per + (self.base + self.n)

    def enter(self, turn, per):
        self.base, self.n, self.turn, self.per = self.base + self.n, 0, turn, per

    def leave(self, turns):
        assert self.n == self.per, (self.n, self.per)
        self.base, self.n, self.turn = self.base + turns * self.per, 0, None


def build_program(nc, t_in, t_out):
    ctx = ExitStack()
    with ctx:
        persist = Persistent(nc, ctx, t_in)
        modulation(nc, t_in, persist)
        retention_layer(nc, t_in, t_out, persist)
        x = ctx.enter_context(nc.sbuf_tensor("x", [P, NT, D], F32))
        outward(nc, persist, "ro", persist.retained, t_in["ret_w_out"][0], H * DV // P, True, 0, x, Finish(load=reload_x(t_in)))
        shared_kv_and_queries(nc, t_in, t_out, persist, x)
        attention_layer(nc, t_in, t_out, persist)
        outward(nc, persist, "ao", persist.attended, t_in["sb_w_out"][0], KD, False, 1, x, Finish(store=store_y(t_out)))


class Persistent:

    def __init__(self, nc, ctx, t_in):
        def sb(name, shape, dt=F32):
            return ctx.enter_context(nc.sbuf_tensor(name, shape, dt))

        self.ident = sb("ident", [P, P])
        self.selector = sb("selector", [NC, P + NS])
        self.gain = sb("gain", [P, 3, KD, NC])
        self.shift = sb("shift", [P, 3, KD, NC])
        self.gate = sb("gate", [NC, 2, D])
        self.ret_g = sb("ret_g", [P, 2 * KD])
        self.k_gain = sb("k_gain", [P, DH])
        self.q_gain = sb("q_gain", [P, DH])
        self.eps = sb("eps", [P, 1])
        self.retained = nc.dram_tensor("retained", (NT * P, H * DV), F32, kind="Internal").ap()
        self.q_rows = nc.dram_tensor("q_rows", (NT * P, D), F32, kind="Internal").ap()
        self.g_rows = nc.dram_tensor("g_rows", (NT * P, D), F32, kind="Internal").ap()
        self.attended = nc.dram_tensor("attended", (NT * P, D), F32, kind="Internal").ap()


def modulation(nc, t_in, ps):
    ctx = ExitStack()
    with ctx:
        def sb(name, shape, dt=F32):
            return ctx.enter_context(nc.sbuf_tensor(name, shape, dt))

        sem = semaphores(nc, ctx, "mod")

        NCH = 3 * D // NB
        CG = 3
        SETS = 2 * NCH // CG
        cond = sb("cond", [NC, D])
        cond_act = sb("cond_act", [NC, D])
        cond_t = sb("cond_t", [P, KD, NC])
        vec_rows = sb("vec_rows", [5 * KD, P])
        vec_t = sb("vec_t", [P, 5 * KD])
        ada_bias = sb("ada_bias", [NC, 2, 3 * D])
        mod = sb("mod", [NC, 2, 3 * D])
        w = sb("ada_w_sb", [P, 2, KD, CG * NB])
        acc = ctx.enter_context(nc.psum_tensor("mod_acc", [P, 2, NB], F32))
        tr = ctx.enter_context(nc.psum_tensor("mod_tr", [P, NB], F32))
        tr2 = ctx.enter_context(nc.psum_tensor("mod_tr2", [P, NB], F32))
        loaded_pool = sem("loaded_pool")
        loaded, w_loaded, act_done = sem("loaded"), [[sem(f"ada_w{b}{k}") for k in range(2)] for b in range(2)], sem("mod_act")
        pe_c, pe_acc, pe_tr = sem("pe_cond_t"), sem("pe_mod_acc"), sem("pe_mod_tr")
        dve_c, dve_acc, dve_own = sem("dve_cond_t"), sem("dve_mod_acc"), sem("dve_mod_own")
        block = ctx.enter_context(nc.Block())

        @block.sync
        def _(sp):
            sp.dma_start(cond[0:1, :], t_in["c_prompt"]).then_inc(loaded, 16)
            sp.dma_start(cond[1:NC, :], t_in["c_sample"]).then_inc(loaded, 16)
            sp.dma_start(ps.ident[:], t_in["ident"]).then_inc(loaded, 16)
            sp.dma_start(vec_rows[0:2 * KD, :], t_in["norm_g"].rearrange("l (k p) -> (l k) p", p=P)).then_inc(loaded, 16)
            sp.dma_start(vec_rows[2 * KD:3 * KD, :], t_in["kv_norm_g"].rearrange("(k p) -> k p", p=P)).then_inc(loaded, 16)
            sp.dma_start(vec_rows[3 * KD:5 * KD, :], t_in["ret_norm_g"].rearrange("l (k p) -> (l k) p", p=P)).then_inc(loaded, 16)
            for n in range(SETS):
                if n >= 2:
                    sp.wait_ge(pe_acc, n - 1)
                la, c0 = n // 2, (n % 2) * CG * NB
                for k in range(2):
                    sp.dma_start(w[:, n % 2, 4 * k:4 * k + 4, :], t_in["ada_w"][la].rearrange("(k p) n -> p k n", p=P)[
                        :, 4 * k:4 * k + 4, c0:c0 + CG * NB]).then_inc(w_loaded[n % 2][k], 16)

        @block.gpsimd
        def _(pool):
            pool.dma_start(ada_bias[:], t_in["ada_b"].rearrange("(o l) n -> o l n", o=1).to_broadcast([NC, 2, 3 * D])).then_inc(loaded_pool, 16)
            pool.dma_start(ps.selector[:], t_in["selector"]).then_inc(loaded_pool, 16)
            pool.dma_start(ps.k_gain[:], t_in["sb_k_g"].rearrange("(o n) -> o n", o=1).to_broadcast([P, DH])).then_inc(loaded_pool, 16)
            pool.dma_start(ps.q_gain[:], t_in["sb_q_g"].to_broadcast([P, DH])).then_inc(loaded_pool, 16)


        @block.scalar
        def _(act):
            act.wait_ge(loaded, 96)
            nc.scalar.activation(cond_act[:], cond[:], ACT.Silu).then_inc(act_done, 1)

        @block.tensor
        def _(pe):
            pe.wait_ge(loaded, 96)
            pe.wait_ge(act_done, 1)
            for k in range(KD):
                last = nc.tensor.transpose(tr[:, k * NC:(k + 1) * NC], cond_act[:, k * P:(k + 1) * P], ps.ident[0:NC, 0:NC])
            last.then_inc(pe_c, 1)
            nc.tensor.transpose(tr2[:, 0:5 * KD], vec_rows[:], ps.ident[0:5 * KD, 0:5 * KD]).then_inc(pe_c, 1)
            pe.wait_ge(dve_c, 1)
            for n in range(SETS):
                if n >= 2:
                    pe.wait_ge(dve_acc, CG * (n - 1))
                for k in range(KD):
                    if k % 4 == 0:
                        pe.wait_ge(w_loaded[n % 2][k // 4], 16 * (n // 2 + 1))
                    for c in range(CG):
                        last = nc.tensor.matmul(acc[32 * c:32 * c + NC, n % 2, :], cond_t[:, k, :],
                                                w[:, n % 2, k, c * NB:(c + 1) * NB], start=k == 0, stop=k == KD - 1,
                                                tile_position=(0, 32 * c))
                last.then_inc(pe_acc, 1)
            pe.wait_ge(dve_acc, 2 * NCH)
            for la in range(2):
                for k in range(2 * KD):
                    at = (la * 2 * KD + k) * NC
                    last = nc.tensor.transpose(tr[:, at:at + NC], mod[:, la, k * P:(k + 1) * P], ps.ident[0:NC, 0:NC])
            last.then_inc(pe_tr, 1)

        @block.vector
        def _(dve):
            nc.vector.memset(ps.eps[:], EPS)
            dve.wait_ge(loaded_pool, 64)
            dve.wait_ge(pe_c, 1)
            nc.vector.tensor_copy(cond_t[:].rearrange("p k c -> p (k c)"), tr[:, 0:KD * NC]).then_inc(dve_c, 1)
            dve.wait_ge(pe_c, 2)
            nc.vector.tensor_copy(vec_t[:], tr2[:, 0:5 * KD]).then_inc(dve_own, 1)
            for n in range(SETS):
                dve.wait_ge(pe_acc, n + 1)
                for c in range(CG):
                    cols = slice(((n % 2) * CG + c) * NB, ((n % 2) * CG + c + 1) * NB)
                    nc.vector.tensor_tensor(mod[:, n // 2, cols], acc[32 * c:32 * c + NC, n % 2, :],
                                            ada_bias[:, n // 2, cols], ALU.add).then_inc(dve_acc, 1)
            dve.wait_ge(dve_own, 1)
            dve.wait_ge(dve_acc, 2 * NCH)
            nc.vector.tensor_copy(ps.gate[:], mod[:, :, 2 * D:3 * D])
            nc.vector.tensor_copy(ps.ret_g[:], vec_t[:, 3 * KD:5 * KD])
            nc.vector.memset(ps.shift[:, 1, :, :], 0.0)
            nc.vector.tensor_copy(ps.gain[:, 1, :, :], vec_t[:, 2 * KD:3 * KD].unsqueeze(2).to_broadcast([P, KD, NC]))
            dve.wait_ge(pe_tr, 1)
            m = tr[:, 0:4 * KD * NC].rearrange("p (l s k c) -> p l s k c", l=2, s=2, k=KD)
            for la in range(2):
                nc.vector.tensor_copy(ps.shift[:, 2 * la, :, :], m[:, la, 0])
                nc.vector.scalar_tensor_tensor(ps.gain[:, 2 * la, :, :], m[:, la, 1], 1.0,
                                               vec_t[:, la * KD:(la + 1) * KD].unsqueeze(2).to_broadcast([P, KD, NC]),
                                               ALU.add, ALU.mult)


def tile_preparation(nc, ps, sem, sets, x, xn, full, small, tr, hi, lo, x_ready, h_free):
    ss, root, rstd = small[:, 0], small[:, 1], small[:, 2]
    squared, rooted, inverted, scaled = sem("x_squared"), sem("x_rooted"), sem("x_inverted"), sem("x_scaled")
    turned, sample_scaled, full_ready = sem("turned_x"), sem("sample_scaled"), sem("full_ready")
    h_hi_s, h_lo_s = sem("h_hi_s"), sem("h_lo_s")

    def act_slot(act, n, s):
        if n == 0 and s < NT:
            r = rows(s)
            x_ready(act, s)
            if s >= 2:
                act.wait_ge(turned, s - 1)
            nc.scalar.activation(xn[0:r, s % 2, :], x(s), ACT.Square, accum_out=ss[0:r, s:s + 1]).then_inc(squared, 1)
            act.wait_ge(squared, s + 1)
            nc.scalar.activation(root[0:r, s:s + 1], ss[0:r, s:s + 1], ACT.Sqrt, scale=1.0 / D,
                                 bias=ps.eps[0:r]).then_inc(rooted, 1)
        t, q = s - 1, n * NT + s - 1
        if 0 <= t < NT:
            act.wait_ge(inverted, t + 1)
            if q >= 2:
                act.wait_ge(turned, q - 1)
            nc.scalar.activation(xn[0:rows(t), q % 2, :], x(t), ACT.Copy, scale=rstd[0:rows(t), t:t + 1]).then_inc(scaled, 1)
        t, q = s - 2, n * NT + s - 2
        if 0 <= t < NT:
            r = rows(t)
            act.wait_ge(full_ready, q + 1)
            h_free(act, n, t)
            nc.scalar.copy(hi[:, :, t * P:t * P + r], full[:, q % 2, :, 0:r]).then_inc(h_hi_s, 1)

    def pe_slot(pe, n, s):
        t, q = s - 1, n * NT + s - 1
        if 0 <= t < NT:
            r = rows(t)
            pe.wait_ge(scaled, q + 1)
            if q >= 2:
                pe.wait_ge(full_ready, q - 1)
            for k in range(KD):
                last = nc.tensor.transpose(tr(q)[:, k, 0:r], xn[0:r, q % 2, k * P:(k + 1) * P], ps.ident[0:r, 0:r])
            last.then_inc(turned, 1)

    def dve_slot(dve, n, s):
        t, q = s - 2, n * NT + s - 2
        if 0 <= t < NT:
            dve.wait_ge(turned, q + 1)
            if q >= 2:
                dve.wait_ge(h_lo_s, q - 1)
            if t < NPT:
                for k in range(KD):
                    last = nc.vector.tensor_scalar(full[:, q % 2, k, :], tr(q)[:, k, :], ps.gain[:, sets[n], k, 0:1],
                                                   ps.shift[:, sets[n], k, 0:1], ALU.mult, ALU.add)
                last.then_inc(full_ready, 1)
            else:
                each = [P, KD, DB, DS]
                cols = full[:, q % 2, :, 0:NS].rearrange("p k (b i) -> p k b i", b=DB)
                nc.vector.tensor_tensor(cols, tr(q)[:, :, 0:NS].rearrange("p k (b i) -> p k b i", b=DB),
                                        ps.gain[:, sets[n], :, 1:NC].unsqueeze(3).to_broadcast(each),
                                        ALU.mult).then_inc(sample_scaled, 1)
                dve.wait_ge(sample_scaled, n + 1)
                nc.vector.tensor_tensor(cols, cols, ps.shift[:, sets[n], :, 1:NC].unsqueeze(3).to_broadcast(each),
                                        ALU.add).then_inc(full_ready, 1)
        if n == 0 and s < NT:
            dve.wait_ge(rooted, s + 1)
            nc.vector.reciprocal(rstd[0:rows(s), s:s + 1], root[0:rows(s), s:s + 1]).then_inc(inverted, 1)
        t, q = s - 3, n * NT + s - 3
        if 0 <= t < NT:
            cols = slice(t * P, t * P + rows(t))
            dve.wait_ge(h_hi_s, q + 1)
            nc.vector.tensor_tensor(lo[:, :, cols], full[:, q % 2, :, 0:rows(t)], hi[:, :, cols].bitcast(F32),
                                    ALU.subtract).then_inc(h_lo_s, 1)

    return act_slot, pe_slot, dve_slot, scaled, h_lo_s


SLOTS = NT + 3


def retention_layer(nc, t_in, t_out, ps):
    ctx = ExitStack()
    with ctx:
        retention_heads(nc, t_in, t_out, ps)


def retention_heads(nc, t_in, t_out, ps):
    ctx = ExitStack()
    with ctx:
        def sb(name, shape, dt=F32):
            return ctx.enter_context(nc.sbuf_tensor(f"rt_{name}", shape, dt))

        sem = semaphores(nc, ctx, "rt")

        h_hi = sb("h_hi", [P, KD, SEQ + NS], F32R)
        h_lo = sb("h_lo", [P, KD, SEQ + NS], F32R)
        R = 3
        CR = 10
        QKV = 2 * DK + DV
        cos = sb("cos", [P, NT, DK])
        sin = sb("sin", [P, NT, DK])
        tables = sb("tables", [P, 2, 3, H])
        causal = sb("causal", [P, P + NS])
        own_rows = sb("own_rows", [NS, DB])
        w_hi = sb("w_hi", [P, KD, QKV], F32R)
        w_lo, w_raw = overlaid(nc, ctx, "rt_w_lo", "rt_w_raw", [P, KD, QKV])
        g_hi = sb("g_hi", [P, KD, DV], F32R)
        g_lo, g_raw = overlaid(nc, ctx, "rt_g_lo", "rt_g_raw", [P, KD, DV])
        raw = sb("raw", [P, R, 2, DK])
        by_cos = sb("by_cos", [P, 2, DK])
        by_sin = sb("by_sin", [P, 2, DK])
        rot = sb("rot", [P, R, 2, DK])
        v = sb("v", [P, R, DV])
        qk_t = sb("qk_t", [P, R, 2, P])
        probs = sb("probs", [P, R, P])
        state = sb("state", [P, DV])
        state_sum = sb("state_sum", [P, DV])
        at = nc.sbuf_base
        old = sb("old", [P, DB, DV])
        new = sb("new", [P, DB, DV])
        o = sb("o", [P, NT, DV])
        g = sb("g", [P, NT, DV])
        XR = 3
        x_ring = nc.alloc_sbuf_tensor_at("rt_x_ring", [P, XR, D], F32, offset=at)
        xn = nc.alloc_sbuf_tensor_at("rt_xn", [P, 2, D], F32, offset=at + 4 * XR * D)
        full = nc.alloc_sbuf_tensor_at("rt_full", [P, 2, KD, P], F32, offset=at + 4 * (XR + 2) * D)
        assert at + 4 * (XR + 4) * D <= nc.sbuf_base
        small = sb("small", [P, 3, NT])
        q_diag = sb("q_diag", [P, DB, NS])
        k_own = sb("k_own", [NS, DB, DK])
        squares = sb("squares", [P, DV])
        ss = sb("ss", [P, NT])
        root = sb("root", [P, NT])
        rstd = sb("rstd", [P, NT])

        def bank(name, n=1):
            return ctx.enter_context(nc.psum_tensor(f"rt_{name}", [P, n, NB], F32))

        acc, acc_g = bank("acc", 2), bank("acc_g", 2)
        tr, sc, out, st = bank("tr"), bank("sc"), bank("out"), bank("st")

        consts = sem("consts")
        w_loaded, g_loaded, old_loaded = sem("w_loaded"), sem("g_loaded"), sem("old_loaded")
        w_hi_s, w_lo_s, g_hi_s, g_lo_s = sem("w_hi"), sem("w_lo"), sem("g_hi"), sem("g_lo")
        projected, projected_g = sem("projected"), sem("projected_g")
        taken, taken_g, rotated, turned = sem("taken"), sem("taken_g"), sem("rotated"), sem("turned")
        turned_out, scored, masked, attended = sem("turned_out"), sem("scored"), sem("masked"), sem("attended")
        o_taken, state_ready, new_ready = sem("o_taken"), sem("state_ready"), sem("new_ready")
        rooted, gated, stored, cleared = sem("rooted"), sem("gated"), sem("stored"), sem("cleared")
        state_free, new_free, o_free, own = sem("state_free"), sem("new_free"), sem("o_free"), sem("own")
        k_own_s, storing = sem("k_own_s"), sem("storing")
        x_loaded = [sem(f"x_loaded{n}") for n in range(XR)]

        def x_ready(act, t):
            act.wait_ge(x_loaded[t % XR], 16 * (t // XR + 1))

        act_slot, pe_slot, dve_slot, x_used, h_ready = tile_preparation(
            nc, ps, sem, [0], lambda t: x_ring[0:rows(t), t % XR, :], xn, full, small,
            lambda q: (acc, acc_g)[q % 2][:].rearrange("p a (k c) -> p (a k) c", c=P), h_hi, h_lo, x_ready,
            lambda act, n, t: None)
        block = ctx.enter_context(nc.Block())

        def after(h, t):
            return h * NT + (CR + t + 1)

        def freed(h, t, ring):
            if t >= ring:
                return h * NT + (CR + t - ring + 1)
            last = max(u for u in range(NT) if u % ring == t % ring)
            return h * NT + (CR - NT + last + 1)

        w_in = t_in["ret_w_in"][0].rearrange("(k p) n -> p k n", p=P)

        @block.sync
        def _(sp):
            sp.dma_start(cos[:], t_in["rope_cos"]).then_inc(consts, 16)
            sp.dma_start(sin[:], t_in["rope_sin"]).then_inc(consts, 16)
            sp.dma_start(tables[:], t_in["decays"]).then_inc(consts, 16)
            sp.dma_start(causal[:], t_in["causal"]).then_inc(consts, 16)
            sp.dma_start(own_rows[:], t_in["own_rows"]).then_inc(consts, 16)
            with sp.Fori(0, H) as h:
                sp.wait_ge(projected, h * NT + CR)
                sp.dma_start(w_raw[:, :, 0:DK], w_in[:, :, bass.ds(h * DK, DK)]).then_inc(w_loaded, 16)
                sp.dma_start(w_raw[:, :, DK:2 * DK], w_in[:, :, bass.ds(h * DK + H * DK, DK)]).then_inc(w_loaded, 16)
                sp.dma_start(w_raw[:, :, 2 * DK:QKV], w_in[:, :, bass.ds(h * DV + 2 * H * DK, DV)]).then_inc(w_loaded, 16)
                sp.wait_ge(h_ready, NT)
                sp.wait_ge(new_ready, h + CR)
                sp.dma_start(old[:], t_in["state_ret"][0].rearrange("b h k e -> h k b e")[bass.ds(h, 1)].rearrange(
                    "o k b e -> (o k) b e")).then_inc(old_loaded, 16)
                sp.wait_ge(projected_g, h * NT + CR)
                sp.dma_start(g_raw[:], w_in[:, :, bass.ds(h * DV + 2 * H * DK + H * DV, DV)]).then_inc(g_loaded, 16)

        @block.gpsimd
        def _(pool):
            for t in range(NT):
                if t >= XR:
                    pool.wait_ge(x_used, t - XR + 1)
                src = t_in["x_prompt"][0, t * P:(t + 1) * P, :] if t < NPT else t_in["x_sample"].rearrange("b i d -> (b i) d")
                pool.dma_start(x_ring[0:rows(t), t % XR, :], src).then_inc(x_loaded[t % XR], 16)
                if t == XR - 1:
                    nc.gpsimd.memset(q_diag[:], 0.0).then_inc(cleared, 1)
            for s in (state_free, new_free, o_free):
                pool.sem_inc(s, 1)
            with pool.Fori(0, H) as h:
                pool.wait_ge(state_ready, after(h, NPT - 1))
                pool.sem_inc(storing, 1)
                pool.dma_start(t_out["st_prompt"][0, 0][bass.ds(h, 1)].rearrange("o k e -> (o k) e"), state[:]).then_inc(stored, 16)
                pool.wait_ge(stored, h * 64 + 16)
                pool.sem_inc(state_free, 1)
                pool.wait_ge(new_ready, h + (CR + 1))
                pool.sem_inc(storing, 1)
                pool.dma_start(t_out["st_sample"][0].rearrange("b h k e -> h k b e")[bass.ds(h, 1)].rearrange(
                    "o k b e -> (o k) b e"), new[:]).then_inc(stored, 16)
                pool.wait_ge(stored, h * 64 + 32)
                pool.sem_inc(new_free, 1)
                pool.wait_ge(gated, (h + 1) * NT)
                pool.sem_inc(storing, 1)
                pool.dma_start(ps.retained[0:SEQ, bass.ds(h * DV, DV)].rearrange("(t p) e -> p t e", p=P), o[:, 0:NPT, :]).then_inc(stored, 16)
                pool.dma_start(ps.retained[SEQ:SEQ + NS, bass.ds(h * DV, DV)], o[0:NS, NPT, :]).then_inc(stored, 16)
                pool.wait_ge(stored, h * 64 + 64)
                pool.sem_inc(o_free, 1)

        @block.tensor
        def _(pe):
            pe.sem_inc(projected, CR)
            pe.sem_inc(projected_g, CR)
            pe.sem_inc(attended, CR)
            for i in range(SLOTS):
                pe_slot(pe, 0, i)
            pe.wait_ge(h_ready, NT)
            pe.wait_ge(consts, 80)

            def turn(h, t):
                pe.wait_ge(rotated, after(h, t))
                pe.wait_ge(turned_out, freed(h, t, 1))
                for n in range(2):
                    last = nc.tensor.transpose(tr[:, 0, n * P:(n + 1) * P], rot[:, t % R, n, :], ps.ident[:])
                last.then_inc(turned, 1)

            def score(h, t):
                r = rows(t)
                pe.wait_ge(turned_out, after(h, t))
                pe.wait_ge(masked, freed(h, t, 1))
                nc.tensor.matmul(sc[0:r, 0, 0:r], qk_t[:, t % R, 1, 0:r], qk_t[:, t % R, 0, 0:r],
                                 start=True, stop=True).then_inc(scored, 1)

            def attend(h, t):
                r = rows(t)
                pe.wait_ge(masked, after(h, t))
                pe.wait_ge(o_taken, freed(h, t, 1))
                if t == NPT:
                    pe.wait_ge(old_loaded, (h + 1) * 16)
                    pe.wait_ge(k_own_s, h + 1)
                    for b in range(DB):
                        nc.tensor.matmul(out[0:r, 0, 0:DV], q_diag[:, b, :], old[:, b, :], start=b == 0, stop=False)
                elif t > 0:
                    pe.wait_ge(state_ready, after(h, t - 1))
                    nc.tensor.matmul(out[0:r, 0, 0:DV], qk_t[:, t % R, 0, :], state[:], start=True, stop=False)
                last = nc.tensor.matmul(out[0:r, 0, 0:DV], probs[0:r, t % R, 0:r], v[0:r, t % R, :], start=t == 0, stop=True)
                if t < NPT:
                    pe.wait_ge(state_ready, freed(h, t, 1) if t else h * NT + CR)
                    last = nc.tensor.matmul(st[:, 0, 0:DV], rot[0:r, t % R, 1, :], v[0:r, t % R, :], start=True, stop=True)
                else:
                    pe.wait_ge(state_ready, after(h, NPT - 1))
                    pe.wait_ge(taken, after(h, NPT))
                    for b in range(DB):
                        dst = (acc[:, 0], acc[:, 1], st[:, 0], tr[:, 0])[b // 2]
                        last = nc.tensor.matmul(dst[:, (b % 2) * DV:(b % 2 + 1) * DV], k_own[:, b, :], v[0:NS, t % R, :],
                                                start=b % 2 == 0, stop=True, skip_group_check=True)
                last.then_inc(attended, 1)

            def project(dst, whi, wlo, t, n):
                r = rows(t)
                for k in range(KD):
                    cols = slice(t * P, t * P + r)
                    nc.tensor.matmul(dst[0:r, 0:n], h_hi[:, k, cols], whi[:, k, :], start=k == 0, stop=False)
                    nc.tensor.matmul(dst[0:r, 0:n], h_hi[:, k, cols], wlo[:, k, :], start=False, stop=False)
                    last = nc.tensor.matmul(dst[0:r, 0:n], h_lo[:, k, cols], whi[:, k, :], start=False, stop=k == KD - 1)
                return last

            def later_steps(h, s):
                if 0 <= s - 3 < NT:
                    attend(h, s - 3)
                if 0 <= s - 2 < NT:
                    score(h, s - 2)
                if 0 <= s - 1 < NT:
                    turn(h, s - 1)

            with pe.Fori(0, H) as h:
                pe.wait_ge(new_ready, h + CR)
                pe.wait_ge(w_lo_s, (h + 1) * 4)
                for t in range(NT):
                    later_steps(h, t)
                    pe.wait_ge(taken, freed(h, t, 2))
                    project(acc[:, t % 2], w_hi, w_lo, t, QKV).then_inc(projected, 1)
                pe.wait_ge(g_lo_s, (h + 1) * 2)
                for t in range(NT):
                    later_steps(h, NT + t)
                    pe.wait_ge(taken_g, freed(h, t, 2))
                    project(acc_g[:, t % 2], g_hi, g_lo, t, DV).then_inc(projected_g, 1)

        @block.scalar
        def _(act):
            act.sem_inc(taken, CR)
            act.sem_inc(taken_g, CR)
            act.sem_inc(turned_out, CR)
            act.sem_inc(o_taken, CR)

            def take(h, t):
                r, kind = rows(t), 0 if t < NPT else 1
                act.wait_ge(projected, after(h, t))
                act.wait_ge(rotated, freed(h, t, R))
                act.wait_ge(attended, freed(h, t, R))
                nc.scalar.copy(v[0:r, t % R, :], acc[0:r, t % 2, 2 * DK:QKV])
                for n in range(2):
                    last = nc.scalar.activation(raw[0:r, t % R, n, :], acc[0:r, t % 2, n * DK:(n + 1) * DK], ACT.Copy,
                                                scale=tables[0:r, kind, n, bass.ds(h, 1)])
                last.then_inc(taken, 1)

            def turn_out(h, t):
                r = rows(t)
                act.wait_ge(turned, h * NT + (t + 1))
                act.wait_ge(attended, freed(h, t, R))
                if t == NPT:
                    nc.scalar.copy(diagonal(q_diag, DB, NS, DS), tr[:, 0, 0:NS].rearrange("p (b i) -> p b i", i=DS))
                src = tr[:, 0, 0:2 * P].rearrange("p (n c) -> p n c", n=2)[:, :, 0:r]
                nc.scalar.copy(qk_t[:, t % R, :, 0:r], src).then_inc(turned_out, 1)

            def take_o(h, t):
                r = rows(t)
                act.wait_ge(attended, after(h, t))
                if t == 0:
                    act.wait_ge(o_free, h + 1)
                nc.scalar.copy(o[0:r, t, :], out[0:r, 0, 0:DV])
                act.wait_ge(o_taken, freed(h, t, 1))
                nc.scalar.activation(squares[0:r, :], out[0:r, 0, 0:DV], ACT.Square,
                                     accum_out=ss[0:r, t:t + 1]).then_inc(o_taken, 1)

            def steps(h, s):
                if 0 <= s - 3 < NT:
                    take_o(h, s - 3)
                if 0 <= s - 1 < NT:
                    turn_out(h, s - 1)

            def split_w(h, q):
                act.wait_ge(w_loaded, (h + 1) * 48)
                nc.scalar.copy(w_hi[:, 2 * q:2 * q + 2, :], w_raw[:, 2 * q:2 * q + 2, :]).then_inc(w_hi_s, 1)

            def split_g(h, q):
                act.wait_ge(g_loaded, (h + 1) * 16)
                nc.scalar.copy(g_hi[:, 4 * q:4 * q + 4, :], g_raw[:, 4 * q:4 * q + 4, :]).then_inc(g_hi_s, 1)

            def head(h, last):
                for t in range(NT):
                    steps(h, t)
                    if t in (2, 3):
                        split_g(h, t - 2)
                    take(h, t)
                for t in range(NT):
                    steps(h, NT + t)
                    if not last and 4 <= t < 8:
                        split_w(h + 1, t - 4)
                    act.wait_ge(projected_g, after(h, t))
                    nc.scalar.activation(g[0:rows(t), t, :], acc_g[0:rows(t), t % 2, 0:DV], ACT.Silu).then_inc(taken_g, 1)
                nc.scalar.activation(root[:], ss[:], ACT.Sqrt, scale=1.0 / DV, bias=ps.eps[:]).then_inc(rooted, 1)

            for i in range(SLOTS):
                act_slot(act, 0, i)
                if i >= NT - 1:
                    split_w(0, i - (NT - 1))
            act.wait_ge(h_ready, NT)
            act.wait_ge(consts, 80)
            act.wait_ge(cleared, 2)

            with act.Fori(0, H - 1) as h:
                head(h, False)
            head(H - 1, True)

        @block.vector
        def _(dve):
            own_n = Count()
            for s in (rotated, masked, state_ready, new_ready):
                dve.sem_inc(s, CR)
            nc.vector.memset(ss[:], 1.0).then_inc(cleared, 1)
            dve.wait_ge(consts, 80)
            dve.sem_inc(own, own_n.up())

            def rotate(h, t):
                r = rows(t)
                dve.wait_ge(taken, after(h, t))
                dve.wait_ge(attended, freed(h, t, R))
                dve.wait_ge(own, own_n.now())
                halves = raw[0:r, t % R].rearrange("p n (a c) -> p n a c", a=2)
                table = sin[0:r, t].rearrange("p (a c) -> p a c", a=2)
                nc.vector.tensor_tensor(by_cos[0:r], raw[0:r, t % R], cos[0:r, t].unsqueeze(1).to_broadcast([r, 2, DK]), ALU.mult)
                for a in range(2):
                    last = nc.vector.tensor_tensor(by_sin[0:r, :, a * 64:(a + 1) * 64], halves[:, :, 1 - a, :],
                                                   table[:, a, :].unsqueeze(1).to_broadcast([r, 2, 64]), ALU.mult)
                last.then_inc(own, own_n.up())
                dve.wait_ge(own, own_n.now())
                nc.vector.tensor_tensor(rot[0:r, t % R], by_cos[0:r], by_sin[0:r], ALU.add).then_inc(rotated, 1)

            def mask(h, t):
                r = rows(t)
                dve.wait_ge(scored, h * NT + (t + 1))
                table = causal[:, 0:P] if t < NPT else causal[0:NS, P:P + NS]
                nc.vector.tensor_tensor(probs[0:r, t % R, 0:r], sc[0:r, 0, 0:r], table, ALU.mult).then_inc(masked, 1)

            def spread_k(h):
                dve.wait_ge(rotated, after(h, NPT))
                nc.vector.tensor_tensor(k_own[:], rot[0:NS, NPT % R, 1, :].unsqueeze(1).to_broadcast([NS, DB, DK]),
                                        own_rows[:].unsqueeze(2).to_broadcast([NS, DB, DK]), ALU.mult).then_inc(k_own_s, 1)

            def update(h, t):
                decay = tables[:, 0 if t < NPT else 1, 2, bass.ds(h, 1)]
                dve.wait_ge(attended, after(h, t))
                if t == 0:
                    dve.wait_ge(state_free, h + 1)
                    nc.vector.tensor_scalar(state[:], st[:, 0, 0:DV], decay, None, ALU.mult).then_inc(state_ready, 1)
                elif t < NPT:
                    dve.wait_ge(state_ready, after(h, t - 1))
                    nc.vector.tensor_tensor(state_sum[:], st[:, 0, 0:DV], state[:], ALU.add).then_inc(own, own_n.up())
                    dve.wait_ge(own, own_n.now())
                    nc.vector.tensor_scalar(state[:], state_sum[:], decay, None, ALU.mult).then_inc(state_ready, 1)
                else:
                    dve.wait_ge(new_free, h + 1)
                    for n, src in enumerate((acc[:, 0], acc[:, 1], st[:, 0], tr[:, 0])):
                        pair = slice(2 * n, 2 * n + 2)
                        last = nc.vector.tensor_tensor(new[:, pair, :], src.rearrange("p (b e) -> p b e", b=2),
                                                       old[:, pair, :], ALU.add)
                    last.then_inc(own, own_n.up())
                    dve.wait_ge(own, own_n.now())
                    nc.vector.tensor_scalar(new[:], new[:], decay, None, ALU.mult).then_inc(new_ready, 1)
                    dve.sem_inc(state_ready, 1)

            def steps(h, s):
                if 0 <= s - 3 < NT:
                    update(h, s - 3)
                if 0 <= s - 2 < NT:
                    mask(h, s - 2)

            def split_w(h, q):
                dve.wait_ge(w_hi_s, h * 4 + (q + 1))
                part = slice(2 * q, 2 * q + 2)
                nc.vector.tensor_tensor(w_lo[:, part, :], w_raw[:, part, :], w_hi[:, part, :].bitcast(F32),
                                        ALU.subtract).then_inc(w_lo_s, 1)

            def split_g(h, q):
                dve.wait_ge(g_hi_s, h * 2 + (q + 1))
                part = slice(4 * q, 4 * q + 4)
                nc.vector.tensor_tensor(g_lo[:, part, :], g_raw[:, part, :], g_hi[:, part, :].bitcast(F32),
                                        ALU.subtract).then_inc(g_lo_s, 1)

            def head(h, last):
                for t in range(NT):
                    steps(h, t)
                    if t in (2, 3):
                        split_g(h, t - 2)
                    rotate(h, t)
                spread_k(h)
                for t in range(NT):
                    steps(h, NT + t)
                    if not last and 4 <= t < 8:
                        split_w(h + 1, t - 4)
                dve.wait_ge(rooted, h + 1)
                nc.vector.reciprocal(rstd[:], root[:]).then_inc(own, own_n.up())
                dve.wait_ge(own, own_n.now())
                for t in range(NT):
                    r = rows(t)
                    nc.vector.scalar_tensor_tensor(o[0:r, t, :], o[0:r, t, :], rstd[0:r, t:t + 1], g[0:r, t, :],
                                                   ALU.mult, ALU.mult).then_inc(gated, 1)

            for i in range(SLOTS):
                dve_slot(dve, 0, i)
                if i >= NT - 1:
                    split_w(0, i - (NT - 1))
            dve.wait_ge(h_ready, NT)
            with dve.Fori(0, H - 1) as h:
                own_n.enter(h, NT + (NPT - 1) + 1 + 1)
                head(h, False)
            own_n.leave(H - 1)
            head(H - 1, True)


def attention_layer(nc, t_in, t_out, ps):
    prompt_attention(nc, t_in, t_out, ps)
    sample_attention(nc, t_in, t_out, ps)


def prompt_attention(nc, t_in, t_out, ps):
    ctx = ExitStack()
    with ctx:
        def sb(name, shape, dt=F32):
            return ctx.enter_context(nc.sbuf_tensor(f"pa_{name}", shape, dt))

        sem = semaphores(nc, ctx, "pa")

        BODY_HEADS = 4
        UNITS = BODY_HEADS * NPT
        TURNS = AH // BODY_HEADS
        PAIRS = BODY_HEADS // 2
        LAG = 3
        CR = 8
        far_below = sb("far_below", [P, P])
        far_r = sb("far_r", [P, P], F32R)
        ident_r = sb("ident_r", [P, P], F32R)
        bias_row = sb("bias_row", [P, AH])
        bias = sb("bias", [P, 2, AH])
        bias_now = sb("bias_now", [P, 2, BODY_HEADS])
        k2, q2, v2, g2 = (sb(n, [P, 2, NPT, 2 * DH]) for n in ("k2", "q2", "v2", "g2"))
        q4 = sb("q4", [P, 2, 2, DH])
        k_parts = sb("k_parts", [P, NPT, 2, 2, DH], F32R)
        k_t = sb("k_t", [P, 2, SEQ], F32R)
        q_hi = sb("q_hi", [P, 2, P], F32R)
        q_lo = sb("q_lo", [P, 2, P], F32R)
        take = sb("take", [P, 2, SEQ])
        keep = sb("keep", [P, 2, SEQ])
        after_key = sb("after_key", [P, 2, SEQ + 8])
        w = sb("w", [P, 2, SEQ])
        w_t = sb("w_t", [P, 2, SEQ])
        o2 = sb("o2", [P, 2, NPT, 2 * DH])

        def bank(name, n=1):
            return ctx.enter_context(nc.psum_tensor(f"pa_{name}", [P, n, NB], F32))

        z, wt, kq, out = bank("z", 4), bank("wt", 2), bank("kq"), bank("out")
        consts, started = sem("consts"), sem("started")
        loaded = [sem("loaded0"), sem("loaded1")]
        stored = [sem("stored0"), sem("stored1")]
        k_hi_s, k_split, k_turned, k_taken = sem("k_hi_s"), sem("k_split"), sem("k_turned"), sem("k_taken")
        q_doubled, q_turned, q_hi_s, q_lo_s = sem("q_doubled"), sem("q_turned"), sem("q_hi_s"), sem("q_lo_s")
        scored, sticks, weighed = sem("scored"), sem("sticks"), sem("weighed")
        w_turned, w_taken_a, w_taken_v, attended, gated = (sem("w_turned"), sem("w_taken_a"), sem("w_taken_v"),
                                                           sem("attended"), sem("gated"))
        bias_s, scanned = sem("bias_s"), sem("scanned")
        out_free, out_taken = sem("out_free"), sem("out_taken")
        block = ctx.enter_context(nc.Block())

        def done(i, s):
            return i * UNITS + (s + 1 + CR)

        def wide(s):
            return (where(s)[2] + 1) * P

        def where(s):
            s %= UNITS
            hh = (s // NPT) % 2
            return s // (2 * NPT), hh, (NPT - 1 - s % NPT) if hh else s % NPT

        rows_of = {
            "k": t_out["k_prompt"][0].rearrange("(t p) h d -> p t (h d)", p=P),
            "q": ps.q_rows[0:SEQ, :].rearrange("(t p) c -> p t c", p=P),
            "v": t_out["v_prompt"][0].rearrange("(t p) h d -> p t (h d)", p=P),
            "g": ps.g_rows[0:SEQ, :].rearrange("(t p) c -> p t c", p=P),
        }

        @block.sync
        def _(sp):
            sp.dma_start(far_below[:], t_in["far_below"]).then_inc(consts, 16)
            sp.dma_start(bias_row[:], t_in["sb_bias"].to_broadcast([P, AH])).then_inc(consts, 16)
            with sp.Fori(0, TURNS) as i:
                for pair in range(PAIRS):
                    sp.wait_ge(gated, i * PAIRS + (pair + 1))
                    for buf, name in ((k2, "k"), (q2, "q"), (v2, "v"), (g2, "g")):
                        sp.dma_start(buf[:, pair], rows_of[name][:, :, bass.ds(i * (BODY_HEADS * DH) + pair * 2 * DH, 2 * DH)]).then_inc(loaded[pair], 16)

        @block.gpsimd
        def _(pool):
            pool.sem_inc(out_free, 2)

            def double(i, s):
                pair, hh, t = where(s)
                pool.wait_ge(loaded[pair], i * 64 + (64 if s < UNITS else 128))
                pool.wait_ge(q_turned, done(i, s - 2))
                pool.sem_inc(started, 1)
                src = q2[:, pair, t, hh * DH:(hh + 1) * DH].unsqueeze(1).to_broadcast([P, 2, DH])
                nc.gpsimd.tensor_copy(q4[:, s % 2], src).then_inc(q_doubled, 1)

            def store(i, pair):
                pool.wait_ge(gated, i * PAIRS + (pair + 3))
                pool.sem_inc(started, 1)
                dst = ps.attended[0:SEQ, :].rearrange("(t p) c -> p t c", p=P)
                pool.dma_start(dst[:, :, bass.ds(i * (BODY_HEADS * DH) + pair * 2 * DH, 2 * DH)], o2[:, pair]).then_inc(stored[pair], 16)

            def release(i, pair):
                pool.wait_ge(stored[pair], i * 16 + 16)
                pool.sem_inc(out_free, 1)

            def turn(i, first, last):
                for s in range(UNITS):
                    if not (last and s + 1 >= UNITS):
                        double(i, s + 1)
                    if s == 4 and not first:
                        store(i - 1, 1)
                    if s == 12 and not first:
                        release(i - 1, 1)
                    if s == 2 * NPT + 4:
                        store(i, 0)
                    if s == 2 * NPT + 12:
                        release(i, 0)

            double(0, 0)
            turn(0, True, False)
            with pool.Fori(1, TURNS - 1) as i:
                turn(i, False, False)
            turn(TURNS - 1, False, True)
            store(TURNS - 1, 1)
            pool.wait_ge(stored[0], 16 * TURNS)
            pool.wait_ge(stored[1], 16 * TURNS)

        @block.tensor
        def _(pe):
            for s in (scored, q_turned, w_turned, attended):
                pe.sem_inc(s, CR)

            def turn_q(i, s):
                pe.wait_ge(q_doubled, i * UNITS + (s + 1))
                pe.wait_ge(q_lo_s, done(i, s - 1))
                nc.tensor.transpose(kq[:, 0, 0:P], q4[:, s % 2].rearrange("p a d -> p (a d)"), ps.ident[:]).then_inc(q_turned, 1)

            def turn_k(head, hh, part, q_out):
                pe.wait_ge(q_lo_s, q_out)
                pe.wait_ge(k_split, head + (2 - hh))
                for n in range(4):
                    t = 4 * part + n
                    last = nc.tensor.transpose(kq[:, 0, n * P:(n + 1) * P],
                                               k_parts[:, t, hh].rearrange("p a d -> p (a d)").bitcast(F32), ps.ident[:])
                last.then_inc(k_turned, 1)

            def score(i, s):
                pair, hh, t = where(s)
                n = wide(s)
                pe.wait_ge(sticks, done(i, s - 2))
                if s % NPT == 0:
                    pe.wait_ge(k_taken, i * (2 * BODY_HEADS) + 2 * (s // NPT + 1))
                pe.wait_ge(q_lo_s, done(i, s))
                for c in range(0, n, NB):
                    m = min(NB, n - c)
                    own = c + m == n
                    dst = z[:, 2 * (s % 2) + c // NB, 0:m]
                    nc.tensor.matmul(dst, q_hi[:, s % 2, :], k_t[:, hh, c:c + m], start=True, stop=False)
                    last = nc.tensor.matmul(dst, q_lo[:, s % 2, :], k_t[:, hh, c:c + m], start=False, stop=not own)
                    if own:
                        last = nc.tensor.matmul(dst[:, m - P:m], ident_r[:], far_r[:], start=False, stop=True)
                last.then_inc(scored, 1)

            def turn_w(i, s):
                pe.wait_ge(weighed, done(i, s))
                pe.wait_ge(w_taken_a, done(i, s - 1))
                pe.wait_ge(w_taken_v, done(i, s - 1))
                for b in range(wide(s) // P):
                    last = nc.tensor.transpose(wt[:, b // 4, (b % 4) * P:(b % 4 + 1) * P], w[:, s % 2, b * P:(b + 1) * P], ps.ident[:])
                last.then_inc(w_turned, 1)

            def attend(i, s):
                pair, hh, t = where(s)
                pe.wait_ge(w_taken_a, done(i, s))
                pe.wait_ge(w_taken_v, done(i, s))
                pe.wait_ge(out_taken, done(i, s - 1))
                for b in range(t + 1):
                    last = nc.tensor.matmul(out[:, 0, 0:DH], w_t[:, s % 2, b * P:(b + 1) * P],
                                            v2[:, pair, b, hh * DH:(hh + 1) * DH], start=b == 0, stop=b == t)
                last.then_inc(attended, 1)

            def turn(i, first, last):
                for s in range(UNITS):
                    final = last and s + 1 >= UNITS
                    if not final:
                        turn_q(i, s + 1)
                    score(i, s)
                    if not first or s >= 2:
                        turn_w(i, s - 2)
                    if not first or s >= LAG:
                        attend(i, s - LAG)
                    if s % NPT in (3, 5) and not (last and s >= UNITS - NPT):
                        nxt = s // NPT + 1
                        turn_k(i * BODY_HEADS + nxt, nxt % 2, (s % NPT - 3) // 2, done(i, s + 1))
                        pe.wait_ge(k_taken, i * (2 * BODY_HEADS) + (2 * nxt + (s % NPT - 3) // 2 + 1))

            for part in range(2):
                if part:
                    pe.wait_ge(k_taken, 1)
                pe.wait_ge(k_split, 2)
                for n in range(4):
                    last = nc.tensor.transpose(kq[:, 0, n * P:(n + 1) * P],
                                               k_parts[:, 4 * part + n, 0].rearrange("p a d -> p (a d)").bitcast(F32), ps.ident[:])
                last.then_inc(k_turned, 1)
            pe.wait_ge(k_taken, 2)
            turn_q(0, 0)
            turn(0, True, False)
            with pe.Fori(1, TURNS - 1) as i:
                turn(i, False, False)
            turn(TURNS - 1, False, True)
            turn_w(TURNS - 1, UNITS - 2)
            attend(TURNS - 1, UNITS - 3)
            turn_w(TURNS - 1, UNITS - 1)
            attend(TURNS - 1, UNITS - 2)
            attend(TURNS - 1, UNITS - 1)

        @block.scalar
        def _(act):
            act.sem_inc(sticks, CR)
            act.sem_inc(w_taken_a, CR)

            def split_k(i, pair):
                act.wait_ge(loaded[pair % PAIRS], (i + (1 if pair < PAIRS else 2)) * 64)
                src = k2[:, pair % PAIRS].rearrange("p t (h d) -> p t h d", h=2)
                for hh in range(2):
                    last = nc.scalar.copy(k_parts[:, :, hh, 0, :], src[:, :, hh, :])
                last.then_inc(k_hi_s, 1)

            def take_k(i, s, part):
                nxt = s // NPT + 1
                act.wait_ge(k_turned, i * (2 * BODY_HEADS) + (2 * nxt + part + 1))
                nc.scalar.copy(k_t[:, nxt % 2, part * NB:(part + 1) * NB], kq[:, 0, :]).then_inc(k_taken, 1)

            def take_q(i, s):
                act.wait_ge(q_turned, done(i, s))
                act.wait_ge(scored, done(i, s - 2))
                nc.scalar.copy(q_hi[:, s % 2, :], kq[:, 0, 0:P]).then_inc(q_hi_s, 1)

            def stick(i, s):
                n = wide(s)
                if s == 0:
                    act.wait_ge(bias_s, i + 1)
                act.wait_ge(scored, done(i, s))
                act.wait_ge(weighed, done(i, s - 2))
                src = z[:, 2 * (s % 2):2 * (s % 2) + 2, :].rearrange("p a b -> p (a b)")[:, 0:n]
                head = s // NPT
                nc.scalar.activation(keep[:, s % 2, 0:n], src, ACT.Sigmoid, scale=-(DH ** -0.5), bias=bias_now[:, 1, head:head + 1])
                nc.scalar.activation(take[:, s % 2, 0:n], src, ACT.Sigmoid, scale=DH ** -0.5,
                                     bias=bias_now[:, 0, head:head + 1]).then_inc(sticks, 1)

            def take_w(i, s):
                n = min(wide(s), NB)
                act.wait_ge(w_turned, done(i, s))
                act.wait_ge(attended, done(i, s - 2))
                nc.scalar.copy(w_t[:, s % 2, 0:n], wt[:, 0, 0:n]).then_inc(w_taken_a, 1)

            def turn(i, first, last):
                for s in range(UNITS):
                    if not (last and s + 1 >= UNITS):
                        take_q(i, s + 1)
                    stick(i, s)
                    if not first or s >= 2:
                        take_w(i, s - 2)
                    if s % (2 * NPT) == NPT and not (last and s > 2 * NPT):
                        split_k(i, s // (2 * NPT) + 1)
                    if s % NPT in (3, 5) and not (last and s >= UNITS - NPT):
                        take_k(i, s, (s % NPT - 3) // 2)

            act.wait_ge(consts, 32)
            nc.scalar.copy(far_r[:], far_below[:])
            nc.scalar.copy(ident_r[:], ps.ident[:])
            split_k(0, 0)
            for part in range(2):
                act.wait_ge(k_turned, part + 1)
                nc.scalar.copy(k_t[:, 0, part * NB:(part + 1) * NB], kq[:, 0, :]).then_inc(k_taken, 1)
            take_q(0, 0)
            turn(0, True, False)
            with act.Fori(1, TURNS - 1) as i:
                turn(i, False, False)
            turn(TURNS - 1, False, True)
            take_w(TURNS - 1, UNITS - 2)
            take_w(TURNS - 1, UNITS - 1)

        @block.vector
        def _(dve):
            for s in (q_lo_s, weighed, w_taken_v, out_taken):
                dve.sem_inc(s, CR)
            dve.sem_inc(gated, 2)
            nc.vector.memset(after_key[:], 1.0).then_inc(scanned, 1)
            dve.wait_ge(consts, 32)
            nc.vector.tensor_copy(bias[:, 0], bias_row[:])
            nc.vector.tensor_scalar(bias[:, 1], bias_row[:], -1.0, None, ALU.mult).then_inc(scanned, 1)
            dve.wait_ge(scanned, 2)

            def split_k(pair, count):
                dve.wait_ge(k_hi_s, count)
                src = k2[:, pair % PAIRS].rearrange("p t (h d) -> p t h d", h=2)
                for hh in range(2):
                    last = nc.vector.tensor_tensor(k_parts[:, :, hh, 1, :], src[:, :, hh, :], k_parts[:, :, hh, 0, :].bitcast(F32),
                                                   ALU.subtract)
                last.then_inc(k_split, 2)

            def rest_q(i, s):
                dve.wait_ge(q_hi_s, i * UNITS + (s + 1))
                nc.vector.tensor_tensor(q_lo[:, s % 2, :], kq[:, 0, 0:P], q_hi[:, s % 2, :].bitcast(F32), ALU.subtract).then_inc(q_lo_s, 1)

            def weigh(i, s):
                n = wide(s)
                dve.wait_ge(sticks, done(i, s))
                dve.wait_ge(w_turned, done(i, s - 2))
                dve.wait_ge(weighed, done(i, s - 1))
                k, a = keep[:, s % 2, 0:n], after_key[:, s % 2, 0:n]
                nc.vector.tensor_tensor_scan(a[:, ::-1], k[:, ::-1], k[:, ::-1], 1.0, ALU.mult, ALU.bypass).then_inc(scanned, 1)
                dve.wait_ge(scanned, i * UNITS + (s + 3))
                nc.vector.tensor_tensor(w[:, s % 2, 0:n], take[:, s % 2, 0:n], after_key[:, s % 2, 1:n + 1], ALU.mult).then_inc(weighed, 1)

            def take_w(i, s):
                n = wide(s)
                if n <= NB:
                    dve.wait_ge(w_turned, done(i, s))
                    dve.sem_inc(w_taken_v, 1)
                    return
                dve.wait_ge(w_turned, done(i, s))
                dve.wait_ge(attended, done(i, s - 2))
                nc.vector.tensor_copy(w_t[:, s % 2, NB:n], wt[:, 1, 0:n - NB]).then_inc(w_taken_v, 1)

            def gate(i, s):
                pair, hh, t = where(s)
                dve.wait_ge(attended, done(i, s))
                if s % (2 * NPT) == 0:
                    dve.wait_ge(out_free, i * PAIRS + (s // (2 * NPT) + 1))
                cols = slice(hh * DH, (hh + 1) * DH)
                nc.vector.tensor_tensor(o2[:, pair, t, cols], out[:, 0, 0:DH], g2[:, pair, t, cols], ALU.mult).then_inc(out_taken, 1)
                if s % (2 * NPT) == 2 * NPT - 1:
                    dve.wait_ge(out_taken, done(i, s))
                    dve.sem_inc(gated, 1)

            def turn(i, first, last):
                for s in range(UNITS):
                    if not (last and s + 1 >= UNITS):
                        rest_q(i, s + 1)
                    if not first or s >= 1:
                        weigh(i, s - 1)
                    if s == 0:
                        nc.vector.tensor_scalar(bias_now[:], bias[:, :, bass.ds(i * BODY_HEADS, BODY_HEADS)], 1.0, None,
                                                ALU.mult).then_inc(bias_s, 1)
                    if not first or s >= 2:
                        take_w(i, s - 2)
                    if not first or s >= LAG:
                        gate(i, s - LAG)
                    if s % (2 * NPT) == NPT and not (last and s > 2 * NPT):
                        split_k(s // (2 * NPT) + 1, i * PAIRS + (s // (2 * NPT) + 2))

            split_k(0, 1)
            rest_q(0, 0)
            turn(0, True, False)
            with dve.Fori(1, TURNS - 1) as i:
                turn(i, False, False)
            turn(TURNS - 1, False, True)
            end = TURNS - 1
            weigh(end, UNITS - 1)
            take_w(end, UNITS - 2)
            gate(end, UNITS - 3)
            take_w(end, UNITS - 1)
            gate(end, UNITS - 2)
            gate(end, UNITS - 1)


def sample_attention(nc, t_in, t_out, ps):
    ctx = ExitStack()
    with ctx:
        def sb(name, shape, dt=F32):
            return ctx.enter_context(nc.sbuf_tensor(f"sa_{name}", shape, dt))

        sem = semaphores(nc, ctx, "sa")

        def bank(name, n=1):
            return ctx.enter_context(nc.psum_tensor(f"sa_{name}", [P, n, NB], F32))

        HP = AH // 2
        NK = PAST + NS
        pages = sb("pages", [1, DB * NPG], I32)
        hidden = sb("hidden", [P, 2, DB, NS])
        bias = sb("bias", [P, 2])
        new_rows = sb("new_rows", [NS, 4, D])
        new_t = sb("new_t", [P, 3, HP, NS])
        RING = 4
        TURNS = DB // RING
        k_pages = sb("k_pages", [P, RING, NPG, D])
        v_pages = sb("v_pages", [P, RING, NPG, D])
        k_t = sb("k_t", [P, HP, PAST])
        q_diag = sb("q_diag", [P, 2, HP, P])
        take = sb("take", [P, 2, NK])
        keep = sb("keep", [P, 2, NK])
        after_key = sb("after_key", [P, 2, NK + 8])
        w = sb("w", [P, 2, NK])
        w_t = sb("w_t", [P, 2, NPG + 1, P])
        o_t = sb("o_t", [P, HP, NS])
        o_rows = sb("o_rows", [NS, D])
        kt, z, wt, out = bank("kt", 4), bank("z", 2), bank("wt"), bank("out")
        pages_s, consts, cleared = sem("pages_s"), sem("consts"), sem("cleared")
        loaded = [sem(f"loaded{n}") for n in range(4)]
        new_turned, new_taken, k_turned, k_taken, placed = (sem("new_turned"), sem("new_taken"), sem("k_turned"),
                                                            sem("k_taken"), sem("placed"))
        scored, sticks, masked, weighed, scanned = sem("scored"), sem("sticks"), sem("masked"), sem("weighed"), sem("scanned")
        w_turned, w_taken, attended, gated, stored = (sem("w_turned"), sem("w_taken"), sem("attended"), sem("gated"),
                                                      sem("stored"))
        back, back_taken = sem("back"), sem("back_taken")
        block = ctx.enter_context(nc.Block())
        CR = 4

        def done(i, b):
            return i * RING + (b + 1 + CR)

        @block.sync
        def _(sp):
            sp.dma_start(pages[:], t_in["page_table"].rearrange("b (o n) -> o (b n)", o=1)).then_inc(pages_s, 16)
            sp.dma_start(hidden[:], t_in["hidden_s"]).then_inc(consts, 16)
            bias_col = t_in["sb_bias"].rearrange("o (h u) -> (o h) u", u=1)
            for hh in range(AH):
                sp.dma_start(bias[hh * DS:(hh + 1) * DS, 0:1], bias_col[hh:hh + 1, :].to_broadcast([DS, 1])).then_inc(consts, 16)
            for n, src in enumerate((ps.q_rows[SEQ:SEQ + NS, :], t_out["k_sample"].rearrange("b i h d -> (b i) (h d)"),
                                     t_out["v_sample"].rearrange("b i h d -> (b i) (h d)"), ps.g_rows[SEQ:SEQ + NS, :])):
                sp.dma_start(new_rows[:, n, :], src).then_inc(consts, 16)
            sp.wait_ge(pages_s, 16)
            with sp.Fori(0, TURNS) as i:
                for b in range(RING):
                    sp.wait_ge(attended, done(i, b - RING))
                    for n in range(NPG):
                        page = sp.value_load(pages[0:1, bass.ds(i * (RING * NPG) + b * NPG + n, 1)], min_val=0,
                                             max_val=t_in["cache_k"].shape[0] - 1)
                        for buf, cache in ((k_pages, "cache_k"), (v_pages, "cache_v")):
                            sp.dma_start(buf[:, b, n, :], t_in[cache][bass.ds(page, 1)].rearrange("o s h d -> (o s) (h d)")).then_inc(loaded[b], 16)

        CONSTS = 16 * (1 + AH + 4)

        @block.gpsimd
        def _(pool):
            nc.gpsimd.memset(q_diag[:], 0.0).then_inc(cleared, 1)
            pool.wait_ge(back_taken, HP // 4)
            pool.dma_start(ps.attended[SEQ:SEQ + NS, :], o_rows[:]).then_inc(stored, 16)
            pool.wait_ge(stored, 16)

        @block.tensor
        def _(pe):
            for s in (k_turned, scored, w_turned, attended):
                pe.sem_inc(s, CR)
            pe.wait_ge(consts, CONSTS)
            for n, src in enumerate((0, 1, 3)):
                for k in range(HP):
                    last = nc.tensor.transpose(kt[:, n, k * NS:(k + 1) * NS], new_rows[:, src, k * P:(k + 1) * P], ps.ident[0:NS, 0:NS])
                last.then_inc(new_turned, 1)
            pe.wait_ge(new_taken, 3)

            def turn_k(i, b):
                pe.wait_ge(k_taken, i * (4 * RING) + (b * 4 + CR))
                pe.wait_ge(loaded[b], i * 64 + 64)
                for k in range(HP):
                    for n in range(NPG):
                        c0 = (k % 2) * PAST + n * P
                        last = nc.tensor.transpose(kt[:, k // 2, c0:c0 + P], k_pages[:, b, n, k * P:(k + 1) * P], ps.ident[:])
                last.then_inc(k_turned, 1)

            def score(i, b):
                pe.wait_ge(sticks, done(i, b - 2))
                pe.wait_ge(placed, i * RING + (b + 1))
                pe.wait_ge(k_taken, i * (4 * RING) + (b * 4 + 4 + CR))
                for k in range(HP):
                    nc.tensor.matmul(z[:, b % 2, 0:PAST], q_diag[:, b % 2, k, :], k_t[:, k, :], start=k == 0, stop=k == HP - 1)
                for k in range(HP):
                    last = nc.tensor.matmul(z[:, b % 2, PAST:NK], q_diag[:, b % 2, k, :], new_t[:, 1, k, :], start=k == 0, stop=k == HP - 1)
                last.then_inc(scored, 1)

            def turn_w(i, b):
                pe.wait_ge(weighed, done(i, b))
                pe.wait_ge(w_taken, done(i, b - 1))
                for n in range(NPG):
                    nc.tensor.transpose(wt[:, 0, n * P:(n + 1) * P], w[:, b % 2, n * P:(n + 1) * P], ps.ident[:])
                nc.tensor.transpose(wt[0:NS, 0, NPG * P:(NPG + 1) * P], w[:, b % 2, PAST:NK], ps.ident[:]).then_inc(w_turned, 1)

            def attend(i, b):
                pe.wait_ge(w_taken, done(i, b))
                pe.wait_ge(gated, done(i, b - 1))
                for k in range(HP):
                    dst = out[:, 0, k * 2 * DS:(k + 1) * 2 * DS]
                    cols = slice(k * 2 * DS, (k + 1) * 2 * DS)
                    for n in range(NPG):
                        nc.tensor.matmul(dst, v_pages[:, b, n, k * P:(k + 1) * P], w_t[:, b % 2, n, cols], start=n == 0, stop=False)
                    last = nc.tensor.matmul(dst, new_rows[:, 2, k * P:(k + 1) * P], w_t[0:NS, b % 2, NPG, cols], start=False, stop=True)
                last.then_inc(attended, 1)

            def step(i, b, last=False):
                nxt = (i, b + 1) if b + 1 < RING else (i + 1, 0)
                if not last:
                    turn_k(*nxt)
                turn_w(i, b)
                if not last:
                    score(*nxt)
                attend(i, b)

            turn_k(0, 0)
            score(0, 0)
            with pe.Fori(0, TURNS - 1) as i:
                for b in range(RING):
                    step(i, b)
            for b in range(RING):
                step(TURNS - 1, b, b == RING - 1)
            pe.wait_ge(gated, DB + CR)
            for k in range(HP):
                last = nc.tensor.transpose(kt[0:NS, k // 4, (k % 4) * P:(k % 4 + 1) * P], o_t[:, k, :], ps.ident[:])
            last.then_inc(back, 1)

        @block.scalar
        def _(act):
            act.sem_inc(sticks, CR)
            act.sem_inc(k_taken, CR)
            act.wait_ge(cleared, 2)
            for n in range(3):
                act.wait_ge(new_turned, n + 1)
                nc.scalar.copy(new_t[:, n].rearrange("p k c -> p (k c)"), kt[:, n, :]).then_inc(new_taken, 1)

            def step(i, b):
                act.wait_ge(k_turned, done(i, b))
                act.wait_ge(scored, done(i, b - 1))
                for q in range(4):
                    nc.scalar.copy(k_t[:, 2 * q:2 * q + 2, :].rearrange("p k c -> p (k c)"), kt[:, q, :]).then_inc(k_taken, 1)
                act.wait_ge(scored, done(i, b))
                act.wait_ge(weighed, done(i, b - 2))
                nc.scalar.activation(keep[:, b % 2], z[:, b % 2, 0:NK], ACT.Sigmoid, scale=-(DH ** -0.5), bias=bias[:, 1:2])
                nc.scalar.activation(take[:, b % 2], z[:, b % 2, 0:NK], ACT.Sigmoid, scale=DH ** -0.5, bias=bias[:, 0:1]).then_inc(sticks, 1)

            with act.Fori(0, TURNS) as i:
                for b in range(RING):
                    step(i, b)
            act.wait_ge(back, 1)
            for n in range(2):
                nc.scalar.copy(o_rows[:, n * NB:(n + 1) * NB], kt[0:NS, n, :]).then_inc(back_taken, 1)

        @block.vector
        def _(dve):
            for s in (weighed, w_taken, gated):
                dve.sem_inc(s, CR)
            nc.vector.memset(after_key[:], 1.0)
            dve.wait_ge(consts, CONSTS)
            nc.vector.tensor_scalar(bias[:, 1:2], bias[:, 0:1], -1.0, None, ALU.mult).then_inc(cleared, 1)
            dve.wait_ge(cleared, 2)
            dve.wait_ge(new_taken, 3)

            def place(i, b):
                dve.wait_ge(scored, done(i, b - 2))
                for hh in range(2):
                    part = slice(hh * DH, (hh + 1) * DH)
                    flat = q_diag[part, b % 2].rearrange("p k c -> p (k c)")[:, hh * DS:]
                    dst = bass.AP(flat.tensor, flat.offset, [list(flat.ap[0]), [P + 2 * DS, HP], [1, DS]])
                    last = nc.vector.tensor_scalar(dst, new_t[part, 0, :, bass.ds(i * (RING * DS) + b * DS, DS)], 1.0, None, ALU.mult)
                last.then_inc(placed, 1)

            def weigh(i, b):
                dve.wait_ge(sticks, done(i, b))
                dve.wait_ge(scanned, i * (2 * RING) + (2 * b + 1))
                seq = bass.ds(i * RING + b, 1)
                for buf, n, op in ((keep, 0, ALU.max), (take, 1, ALU.mult)):
                    last = nc.vector.tensor_tensor(buf[:, b % 2, PAST:NK], buf[:, b % 2, PAST:NK],
                                                   hidden[:, n, seq, :].rearrange("p o c -> p (o c)"), op)
                last.then_inc(scanned, 1)
                dve.wait_ge(scanned, i * (2 * RING) + (2 * b + 2))
                k = keep[:, b % 2]
                nc.vector.tensor_tensor_scan(after_key[:, b % 2, 0:NK][:, ::-1], k[:, ::-1], k[:, ::-1], 1.0, ALU.mult, ALU.bypass).then_inc(scanned, 1)
                dve.wait_ge(scanned, i * (2 * RING) + (2 * b + 3))
                dve.wait_ge(w_turned, done(i, b - 2))
                nc.vector.tensor_tensor(w[:, b % 2], take[:, b % 2], after_key[:, b % 2, 1:NK + 1], ALU.mult).then_inc(weighed, 1)

            def finish(i, b):
                dve.wait_ge(w_turned, done(i, b))
                dve.wait_ge(attended, done(i, b - 2))
                nc.vector.tensor_copy(w_t[:, b % 2, 0:NPG], wt[:, 0, 0:NPG * P].rearrange("p (n c) -> p n c", n=NPG))
                nc.vector.tensor_copy(w_t[0:NS, b % 2, NPG], wt[0:NS, 0, NPG * P:(NPG + 1) * P]).then_inc(w_taken, 1)
                dve.wait_ge(attended, done(i, b))
                for hh in range(2):
                    part = slice(hh * DH, (hh + 1) * DH)
                    src = out[part, 0, 0:HP * 2 * DS].rearrange("p (k a i) -> p k a i", k=HP, a=2)[:, :, hh, :]
                    cols = bass.ds(i * (RING * DS) + b * DS, DS)
                    last = nc.vector.tensor_tensor(o_t[part, :, cols], src, new_t[part, 2, :, cols], ALU.mult)
                last.then_inc(gated, 1)

            dve.sem_inc(scanned, 1)
            place(0, 0)
            def step(i, b, last=False):
                nxt = (i, b + 1) if b + 1 < RING else (i + 1, 0)
                if not last:
                    place(*nxt)
                weigh(i, b)
                finish(i, b)

            with dve.Fori(0, TURNS - 1) as i:
                for b in range(RING):
                    step(i, b)
            for b in range(RING):
                step(TURNS - 1, b, b == RING - 1)


def outward(nc, ps, tag, rows_in, w_rows, KT, w_gain, layer, x, finish):
    ctx = ExitStack()
    with ctx:
        def sb(name, shape, dt=F32):
            return ctx.enter_context(nc.sbuf_tensor(f"{tag}_{name}", shape, dt))

        sem = semaphores(nc, ctx, tag)

        NH = D // NB
        GR = KT // 4
        SPLITS = 4
        KS = KT // SPLITS
        w_hi = sb("w_hi", [P, KT, NB], F32R)
        pairs = [overlaid(nc, ctx, f"{tag}_w_lo{n}", f"{tag}_w_raw{n}", [P, KT, NB]) for n in range(NH)]
        w_lo, w_raw = [p[0] for p in pairs], [p[1] for p in pairs]
        gate_p = sb("gate_p", [P, D])
        gate_s = sb("gate_s", [NS, D])
        a = sb("a", [P, KT * P])
        a_hi = sb("a_hi", [P, 2, KT, P], F32R)
        a_lo = sb("a_lo", [P, 2, KT, P], F32R)
        scaled = sb("scaled", [P, 2, NB])
        tr = ctx.enter_context(nc.psum_tensor(f"{tag}_tr", [P, 4, NB], F32))
        acc = ctx.enter_context(nc.psum_tensor(f"{tag}_acc", [P, 2, NB], F32))
        spread = ctx.enter_context(nc.psum_tensor(f"{tag}_spread", [P, 2, NB], F32))
        x_loaded, a_loaded = [sem("x_loaded0"), sem("x_loaded1")], sem("a_loaded")
        w_loaded = [[sem(f"w_loaded{n}_{q}") for q in range(SPLITS)] for n in range(NH)]
        hi_s, lo_s, gate_s_s, gate_taken = sem("w_hi_s"), sem("w_lo_s"), sem("gate_spread"), sem("gate_taken")
        turned, a_hi_s, a_lo_s, made, scaled_s, added = (sem("turned"), sem("a_hi_s"), sem("a_lo_s"), sem("made"),
                                                         sem("scaled_s"), sem("added"))
        stored = sem("stored")
        block = ctx.enter_context(nc.Block())
        CR = 2

        @block.sync
        def _(sp):
            w = w_rows.rearrange("(k p) n -> p k n", p=P)

            def load_w(n):
                for q in range(SPLITS):
                    part = slice(KS * q, KS * (q + 1))
                    sp.dma_start(w_raw[n][:, part, :], w[:, part, n * NB:(n + 1) * NB]).then_inc(w_loaded[n][q], 16)

            def load_rows(n, first, end):
                with sp.Fori(first, end) as t:
                    sp.wait_ge(turned, t + (n * NT + CR))
                    sp.dma_start(a[:], rows_in[bass.ds(t * P, P), :]).then_inc(a_loaded, 16)

            load_w(0)
            sp.dma_start(a[:], rows_in[0:P, :]).then_inc(a_loaded, 16)
            for n in range(NH):
                if finish.load is not None:
                    finish.load(sp, x[:, :, n * NB:(n + 1) * NB], n, x_loaded[n])
                load_rows(n, 1 - n, 3)
                if n == 0:
                    load_w(1)
                load_rows(n, 3, NPT)
                sp.wait_ge(turned, NPT + n * NT + CR)
                sp.dma_start(a[0:NS, :], rows_in[SEQ:SEQ + NS, :]).then_inc(a_loaded, 16)

        @block.tensor
        def _(pe):
            pe.sem_inc(turned, CR)
            pe.sem_inc(made, CR)
            for n in range(NH):
                nc.tensor.matmul(spread[:, n, :], ps.selector[:, 0:P], ps.gate[:, layer, n * NB:(n + 1) * NB],
                                 start=True, stop=True).then_inc(gate_s_s, 1)
            pe.wait_ge(gate_taken, 2)
            for n in range(NH):
                nc.tensor.matmul(spread[0:NS, n, :], ps.selector[:, P:P + NS], ps.gate[:, layer, n * NB:(n + 1) * NB],
                                 start=True, stop=True).then_inc(gate_s_s, 1)

            def turn(n, j):
                pe.wait_ge(a_loaded, (j + (n * NT + 1)) * 16)
                pe.wait_ge(a_lo_s, (j + (n * NT)) * GR + CR)
                for k in range(KT):
                    last = nc.tensor.transpose(tr[:, k // 4, (k % 4) * P:(k % 4 + 1) * P], a[:, k * P:(k + 1) * P], ps.ident[:])
                last.then_inc(turned, 1)

            def multiply(n, b, j, r):
                pe.wait_ge(a_lo_s, (j + (n * NT + 1)) * GR + CR)
                pe.wait_ge(added, j + (n * NT + CR - 1))
                for k in range(KT):
                    nc.tensor.matmul(acc[0:r, b, :], a_hi[:, b, k, 0:r], w_hi[:, k, :], start=k == 0, stop=False)
                    nc.tensor.matmul(acc[0:r, b, :], a_hi[:, b, k, 0:r], w_lo[n][:, k, :], start=False, stop=False)
                    last = nc.tensor.matmul(acc[0:r, b, :], a_lo[:, b, k, 0:r], w_hi[:, k, :], start=False, stop=k == KT - 1)
                last.then_inc(made, 1)

            for n in range(NH):
                turn(n, 0)
                pe.wait_ge(lo_s, SPLITS * (n + 1))
                with pe.Fori(0, NPT // 2) as i:
                    turn(n, i * 2 + 1)
                    multiply(n, 0, i * 2, P)
                    turn(n, i * 2 + 2)
                    multiply(n, 1, i * 2 + 1, P)
                multiply(n, 0, NPT, NS)

        @block.scalar
        def _(act):
            act.wait_ge(gate_s_s, 2)
            nc.scalar.copy(gate_p[:], spread[:].rearrange("p a b -> p (a b)")).then_inc(gate_taken, 2)
            act.wait_ge(gate_s_s, 4)
            nc.scalar.copy(gate_s[:], spread[0:NS].rearrange("p a b -> p (a b)")).then_inc(gate_taken, 1)

            def take(n, b, j):
                act.wait_ge(turned, j + (n * NT + CR + 1))
                act.wait_ge(made, j + (n * NT + CR - 1))
                for q in range(GR):
                    nc.scalar.copy(a_hi[:, b, 4 * q:4 * q + 4, :].rearrange("p k c -> p (k c)"), tr[:, q, :]).then_inc(a_hi_s, 1)

            for n in range(NH):
                if n:
                    act.wait_ge(made, n * NT + CR)
                for k in range(KT):
                    if k % KS == 0:
                        act.wait_ge(w_loaded[n][k // KS], 16)
                    scale = ps.ret_g[:, k:k + 1] if w_gain else 1.0
                    last = nc.scalar.activation(w_hi[:, k, :], w_raw[n][:, k, :], ACT.Copy, scale=scale)
                    if k % KS == KS - 1:
                        last.then_inc(hi_s, 1)
                take(n, 0, 0)
                with act.Fori(0, NPT // 2) as i:
                    take(n, 1, i * 2 + 1)
                    take(n, 0, i * 2 + 2)

        @block.vector
        def _(dve):
            dve.sem_inc(a_lo_s, CR)
            dve.sem_inc(added, CR)
            dve.wait_ge(gate_taken, 3)

            def take(n, b, j):
                for q in range(GR):
                    dve.wait_ge(a_hi_s, (j + n * NT) * GR + (q + 1))
                    cols = a_hi[:, b, 4 * q:4 * q + 4, :].rearrange("p k c -> p (k c)")
                    nc.vector.tensor_tensor(a_lo[:, b, 4 * q:4 * q + 4, :].rearrange("p k c -> p (k c)"), tr[:, q, :],
                                            cols.bitcast(F32), ALU.subtract).then_inc(a_lo_s, 1)

            def add(n, b, j, r, t):
                gate = gate_p[:, n * NB:(n + 1) * NB] if r == P else gate_s[:, n * NB:(n + 1) * NB]
                xs = x[0:r, t, n * NB:(n + 1) * NB]
                if not isinstance(t, int):
                    xs = xs.rearrange("p o c -> p (o c)")
                dve.wait_ge(made, j + (n * NT + CR + 1))
                nc.vector.tensor_tensor(scaled[0:r, b, :], acc[0:r, b, :], gate, ALU.mult).then_inc(scaled_s, 1)
                dve.wait_ge(scaled_s, j + (n * NT + 1))
                nc.vector.tensor_tensor(xs, xs, scaled[0:r, b, :], ALU.add).then_inc(added, 1)

            for n in range(NH):
                for q in range(SPLITS):
                    dve.wait_ge(hi_s, n * SPLITS + q + 1)
                    for k in range(KS * q, KS * (q + 1)):
                        if w_gain:
                            last = nc.vector.scalar_tensor_tensor(w_lo[n][:, k, :], w_raw[n][:, k, :], ps.ret_g[:, k:k + 1],
                                                                  w_hi[:, k, :].bitcast(F32), ALU.mult, ALU.subtract)
                        else:
                            last = nc.vector.tensor_tensor(w_lo[n][:, k, :], w_raw[n][:, k, :],
                                                           w_hi[:, k, :].bitcast(F32), ALU.subtract)
                    last.then_inc(lo_s, 1)
                take(n, 0, 0)
                if finish.load is not None:
                    dve.wait_ge(x_loaded[n], 32)
                with dve.Fori(0, NPT // 2) as i:
                    take(n, 1, i * 2 + 1)
                    add(n, 0, i * 2, P, bass.ds(i * 2, 1))
                    take(n, 0, i * 2 + 2)
                    add(n, 1, i * 2 + 1, P, bass.ds(i * 2 + 1, 1))
                add(n, 0, NPT, NS, NPT)

        if finish.store is not None:
            @block.gpsimd
            def _(pool):
                finish.store(pool, x, added, stored, CR)


class Finish:
    def __init__(self, load=None, store=None):
        self.load, self.store = load, store


def reload_x(t_in):
    def load(sp, x_cols, n, sem):
        cols = slice(n * NB, (n + 1) * NB)
        sp.dma_start(x_cols[:, 0:NPT, :], t_in["x_prompt"][0].rearrange("(t p) d -> p t d", p=P)[:, :, cols]).then_inc(sem, 16)
        sp.dma_start(x_cols[0:NS, NPT, :], t_in["x_sample"].rearrange("b i d -> (b i) d")[:, cols]).then_inc(sem, 16)
    return load


def store_y(t_out):
    def store(pool, x, added, stored, CR):
        with pool.Fori(0, NPT) as t:
            pool.wait_ge(added, t + (NT + CR + 1))
            pool.dma_start(t_out["y_prompt"][0][bass.ds(t * P, P), :], x[:, bass.ds(t, 1), :].rearrange("p o d -> p (o d)")).then_inc(stored, 16)
        pool.wait_ge(added, 2 * NT + CR)
        pool.dma_start(t_out["y_sample"].rearrange("b i d -> (b i) d"), x[0:NS, NPT, :]).then_inc(stored, 16)
        pool.wait_ge(stored, 16 * NT)
    return store


def shared_kv_and_queries(nc, t_in, t_out, ps, x):
    ctx = ExitStack()
    with ctx:
        def sb(name, shape, dt=F32):
            return ctx.enter_context(nc.sbuf_tensor(f"kq_{name}", shape, dt))

        sem = semaphores(nc, ctx, "kq")

        def out_rows(name):
            return (t_out[name + "_prompt"][0].rearrange("s h d -> s (h d)"),
                    t_out[name + "_sample"].rearrange("b i h d -> (b i) (h d)"))

        def scratch(ap):
            return ap[0:SEQ, :], ap[SEQ:SEQ + NS, :]

        h_hi = sb("h_hi", [P, KD, SEQ + NS], F32R)
        h_lo = sb("h_lo", [P, KD, SEQ + NS], F32R)
        w_hi = sb("w_hi", [P, 2, KD, NB], F32R)
        pairs = [overlaid(nc, ctx, f"kq_w_lo{n}", f"kq_w_raw{n}", [P, KD, NB]) for n in range(2)]
        w_lo, w_raw = [p[0] for p in pairs], [p[1] for p in pairs]
        HC = NB // DH
        y = sb("y", [P, 2, NB])
        squares = sb("squares", [P, 2, NB])
        ss = sb("ss", [P, 2, HC])
        root = sb("root", [P, 2, HC])
        rstd = sb("rstd", [P, 2, HC])
        out = sb("out", [P, 2, NB])
        xn = sb("xn", [P, 2, D])
        full = sb("full", [P, 2, KD, P])
        small = sb("small", [P, 3, NT])
        acc = ctx.enter_context(nc.psum_tensor("kq_acc", [P, 4, NB], F32))
        tr = ctx.enter_context(nc.psum_tensor("kq_tr", [P, 4, NB], F32))
        w_loaded = [sem("w_loaded0"), sem("w_loaded1")]
        hi_s, lo_s, made = sem("w_hi_s"), sem("w_lo_s"), sem("made")
        taken, squared, summed, rooted, normed, ready = (sem("taken"), sem("squared"), sem("summed"), sem("rooted"),
                                                         sem("normed"), sem("ready"))
        own = sem("own")
        stored = [sem("stored0"), sem("stored1")]

        k_out, v_out, q_out, g_out = out_rows("k"), out_rows("v"), scratch(ps.q_rows), scratch(ps.g_rows)
        w_kv, w_qg = t_in["w_kv"], t_in["sb_w_in"][0]
        chunks = [(w_kv, 2, None, ACT.Copy, v_out), (w_kv, 0, ps.k_gain, None, k_out),
                  (w_kv, 1, ps.k_gain, None, k_out), (w_kv, 3, None, ACT.Copy, v_out),
                  (w_qg, 2, None, ACT.Silu, g_out), (w_qg, 0, ps.q_gain, None, q_out),
                  (w_qg, 1, ps.q_gain, None, q_out), (w_qg, 3, None, ACT.Silu, g_out)]
        SWITCH = 4
        steps = [(c, t) for c in range(len(chunks)) for t in range(NT)]
        SPLITS = 4
        KS = KD // SPLITS
        LEAD = 4

        def normed_before(s):
            return len([1 for c, t in steps[:s] if chunks[c][2] is not None])

        def last_use(s):
            return 16 * (s // 2)

        def h_free(act, n, t):
            if n == 1:
                act.wait_ge(made, (SWITCH - 1) * NT + t + 1)

        def slots_at(s):
            found = []
            if s + LEAD < SLOTS:
                found.append((0, s + LEAD))
            if (SWITCH - 1) * NT <= s < (SWITCH - 1) * NT + SLOTS:
                found.append((1, s - (SWITCH - 1) * NT))
            return found

        act_slot, pe_slot, dve_slot, _, h_ready = tile_preparation(
            nc, ps, sem, [1, 2], lambda t: x[0:rows(t), t, :], xn, full, small,
            lambda q: tr[:, 2 * (q % 2):2 * (q % 2) + 2, :].rearrange("p a (k c) -> p (a k) c", c=P), h_hi, h_lo,
            lambda act, t: None, h_free)
        block = ctx.enter_context(nc.Block())

        @block.sync
        def _(sp):
            for c, (w, n, _, _, _) in enumerate(chunks):
                if c >= 2:
                    sp.wait_ge(made, (c - 1) * NT)
                sp.dma_start(w_raw[c % 2][:], w.rearrange("(k p) n -> p k n", p=P)[:, :, n * NB:(n + 1) * NB]).then_inc(w_loaded[c % 2], 16)

        @block.tensor
        def _(pe):
            for i in range(LEAD):
                pe_slot(pe, 0, i)
            for s, (c, t) in enumerate(steps):
                r = rows(t)
                if t == 0:
                    pe.wait_ge(lo_s, SPLITS * (c + 1))
                if c in (0, SWITCH):
                    pe.wait_ge(h_ready, (c // SWITCH) * NT + t + 1)
                if s >= 4:
                    pe.wait_ge(taken, s - 3)
                cols = slice(t * P, t * P + r)
                for k in range(KD):
                    nc.tensor.matmul(acc[0:r, s % 4, :], h_hi[:, k, cols], w_hi[:, c % 2, k, :], start=k == 0, stop=False)
                    nc.tensor.matmul(acc[0:r, s % 4, :], h_hi[:, k, cols], w_lo[c % 2][:, k, :], start=False, stop=False)
                    last = nc.tensor.matmul(acc[0:r, s % 4, :], h_lo[:, k, cols], w_hi[:, c % 2, k, :], start=False, stop=k == KD - 1)
                last.then_inc(made, 1)
                for n, i in slots_at(s):
                    pe_slot(pe, n, i)

        @block.scalar
        def _(act):
            def split(c, q):
                act.wait_ge(w_loaded[c % 2], 16 * (c // 2 + 1))
                part = slice(KS * q, KS * (q + 1))
                nc.scalar.copy(w_hi[:, c % 2, part, :], w_raw[c % 2][:, part, :]).then_inc(hi_s, 1)

            for i in range(LEAD):
                act_slot(act, 0, i)
                split(0, i)
            for s, (c, t) in enumerate(steps):
                for n, i in slots_at(s):
                    act_slot(act, n, i)
                r = rows(t)
                act.wait_ge(made, s + 1)
                if chunks[c][2] is not None:
                    m = normed_before(s)
                    if m >= 2:
                        act.wait_ge(normed, m - 1)
                        act.wait_ge(summed, m - 1)
                    nc.scalar.activation(squares[0:r, m % 2, :], acc[0:r, s % 4, :], ACT.Square).then_inc(squared, 1)
                    nc.scalar.copy(y[0:r, m % 2, :], acc[0:r, s % 4, :]).then_inc(taken, 1)
                    act.wait_ge(summed, m + 1)
                    nc.scalar.activation(root[0:r, m % 2, :], ss[0:r, m % 2, :], ACT.Sqrt, scale=1.0 / DH,
                                         bias=ps.eps[0:r]).then_inc(rooted, 1)
                else:
                    if s >= 2:
                        act.wait_ge(stored[s % 2], last_use(s))
                    nc.scalar.activation(out[0:r, s % 2, :], acc[0:r, s % 4, :], chunks[c][3]).then_inc(taken, 1)
                if 3 <= t < 3 + SPLITS and c + 1 < len(chunks):
                    split(c + 1, t - 3)

        @block.vector
        def _(dve):
            def split(c, q):
                dve.wait_ge(hi_s, SPLITS * c + q + 1)
                part = slice(KS * q, KS * (q + 1))
                nc.vector.tensor_tensor(w_lo[c % 2][:, part, :], w_raw[c % 2][:, part, :], w_hi[:, c % 2, part, :].bitcast(F32),
                                        ALU.subtract).then_inc(lo_s, 1)

            for i in range(LEAD):
                dve_slot(dve, 0, i)
                split(0, i)
            for s, (c, t) in enumerate(steps):
                for n, i in slots_at(s):
                    dve_slot(dve, n, i)
                r = rows(t)
                if chunks[c][2] is not None:
                    m, head_gain = normed_before(s), chunks[c][2]

                    def heads(buf, i):
                        return buf[0:r, i % 2, :].rearrange("p (h d) -> p h d", h=HC)

                    dve.wait_ge(squared, m + 1)
                    nc.vector.tensor_reduce(ss[0:r, m % 2, :], heads(squares, m), AX.X, ALU.add).then_inc(summed, 1)
                    dve.wait_ge(rooted, m + 1)
                    nc.vector.reciprocal(rstd[0:r, m % 2, :], root[0:r, m % 2, :]).then_inc(own, 1)
                    dve.wait_ge(own, 2 * m + 1)
                    nc.vector.tensor_tensor(heads(squares, m), heads(y, m), rstd[0:r, m % 2, :].unsqueeze(2).to_broadcast([r, HC, DH]),
                                            ALU.mult).then_inc(own, 1)
                    dve.wait_ge(own, 2 * m + 2)
                    if s >= 2:
                        dve.wait_ge(stored[s % 2], last_use(s))
                    nc.vector.tensor_tensor(heads(out, s), heads(squares, m), head_gain[0:r].unsqueeze(1).to_broadcast([r, HC, DH]),
                                            ALU.mult).then_inc(ready, 1)
                    dve.sem_inc(normed, 1)
                if 3 <= t < 3 + SPLITS and c + 1 < len(chunks):
                    split(c + 1, t - 3)

        @block.gpsimd
        def _(pool):
            for s, (c, t) in enumerate(steps):
                r = rows(t)
                _, n, head_gain, _, dst = chunks[c]
                c0 = (n % 2) * NB
                if head_gain is not None:
                    pool.wait_ge(ready, normed_before(s + 1))
                else:
                    pool.wait_ge(taken, s + 1)
                r0 = t * P if t < NPT else 0
                pool.dma_start(dst[0 if t < NPT else 1][r0:r0 + r, c0:c0 + NB], out[0:r, s % 2, :]).then_inc(stored[s % 2], 16)
            for n in range(2):
                pool.wait_ge(stored[n], 16 * len([s for s in range(len(steps)) if s % 2 == n]))


def diagonal(buf, blocks, width, n):
    flat = buf[:].rearrange("p b c -> p (b c)")
    return bass.AP(flat.tensor, flat.offset, [list(flat.ap[0]), [width + n, blocks], [1, n]])


def overlaid(nc, ctx, name, raw_name, shape):
    at = nc.sbuf_base
    lo = ctx.enter_context(nc.sbuf_tensor(name, shape, F32R))
    return lo, nc.alloc_sbuf_tensor_at(raw_name, shape, F32, offset=at)


def shape_constants():
    import numpy as np

    f = np.float32
    half = DK // 2
    inv_freq = 10000.0 ** (-np.arange(half, dtype=f) / f(half))
    pos = np.zeros((P, NT), f)
    pos[:, :NPT] = np.arange(SEQ).reshape(NPT, P).T
    pos[:, NPT] = PAST + np.arange(P) % DS
    ang = (pos[:, :, None] * inv_freq.astype(f)).astype(f)
    cos, sin = np.cos(ang), np.sin(ang)
    log_gamma = np.log1p(-np.exp2(-5.0 - np.arange(H)))
    decays = np.zeros((P, 2, 3, H))
    for kind, chunk in ((0, P), (1, DS)):
        i = (np.arange(P) % chunk)[:, None]
        decays[:, kind, 0] = np.exp(log_gamma * (i + 1.0))
        decays[:, kind, 1] = np.exp(-log_gamma * (i + 1.0)) * DK ** -0.5
        decays[:, kind, 2] = np.exp(log_gamma * chunk)
    j, i = np.arange(P)[:, None], np.arange(P)[None]
    causal = np.zeros((P, P + NS))
    causal[:, :P] = j <= i
    js, is_ = np.arange(NS)[:, None], np.arange(NS)[None]
    causal[:NS, P:] = (js <= is_) & (js // DS == is_ // DS)
    selector = np.zeros((NC, P + NS))
    selector[0, :P] = 1
    for b in range(DB):
        selector[1 + b, P + b * DS:P + (b + 1) * DS] = 1
    own_rows = (np.arange(NS)[:, None] // DS == np.arange(DB)[None])
    q, s = np.arange(P)[:, None], np.arange(P)[None]
    hidden = (s >= q)
    hq = np.arange(P) % DS
    tok = np.arange(NS)
    hidden_s = np.ones((P, DB, NS))
    for b in range(DB):
        hidden_s[:, b] = ~((tok[None] // DS == b) & (tok[None] % DS < hq[:, None]))
    out = {
        "ident": np.eye(P), "selector": selector, "own_rows": own_rows, "causal": causal, "decays": decays,
        "rope_cos": np.concatenate([cos, cos], -1), "rope_sin": np.concatenate([-sin, sin], -1),
        "far_below": hidden * FAR, "hidden_s": np.stack([hidden_s, 1 - hidden_s], 1),
    }
    return {k: np.ascontiguousarray(x, dtype=f) for k, x in out.items()}


INPUTS = ["x_prompt", "x_sample", "state_ret", "cache_k", "cache_v", "page_table", "c_prompt", "c_sample", "ada_w",
          "ada_b", "norm_g", "ret_w_in", "ret_norm_g", "ret_w_out", "kv_norm_g", "w_kv", "sb_q_g", "sb_k_g",
          "sb_w_in", "sb_w_out", "sb_bias"]
OUTPUTS = {"y_prompt": (1, SEQ, D), "y_sample": (DB, DS, D), "st_prompt": (1, 1, H, DK, DV),
           "st_sample": (1, DB, H, DK, DV), "k_prompt": (1, SEQ, AH, DH), "v_prompt": (1, SEQ, AH, DH),
           "k_sample": (DB, DS, AH, DH), "v_sample": (DB, DS, AH, DH)}


def kernel(**inputs):
    import numpy as np
    import concourse.bacc as bacc
    from concourse.bass_utils import run_bass_kernel_spmd

    nc = bacc.Bacc("TRN2", target_bir_lowering=False, num_devices=1)
    arrays = {name: np.ascontiguousarray(inputs[name]) for name in INPUTS}
    arrays.update(shape_constants())
    t_in = {name: nc.dram_tensor("in_" + name, a.shape, mybir.dt.from_np(a.dtype), kind="ExternalInput").ap()
            for name, a in arrays.items()}
    t_out = {name: nc.dram_tensor("out_" + name, shape, F32, kind="ExternalOutput").ap() for name, shape in OUTPUTS.items()}
    build_program(nc, t_in, t_out)
    results = run_bass_kernel_spmd(nc, [{"in_" + n: a for n, a in arrays.items()}], core_ids=[0]).results[0]
    return tuple(results["out_" + name] for name in OUTPUTS)
```

```python
from contextlib import ExitStack

import concourse.bass as bass
from concourse import mybir
from concourse.alu_op_type import AluOpType as ALU

ACT = mybir.ActivationFunctionType
AX = mybir.AxisListType
F32 = mybir.dt.float32
F32R = mybir.dt.float32r
I32 = mybir.dt.int32

P = 128
D = 1024
KD = D // P
SEQ = 1024
NPT = SEQ // P
NT = NPT + 1
DB, DS = 8, 8
NS = DB * DS
NC = 1 + DB
PAST = 256
PAGE = 128
NPG = PAST // PAGE
H = 8
DK, DV = 128, 256
AH = 16
DH = 64
NB = 512
EPS = 1e-6
FAR = -2.0 ** 30


def semaphores(nc, ctx, prefix):
    made = []

    def sem(name):
        made.append(nc.alloc_semaphore(f"{prefix}_{name}"))
        return made[-1]

    def give_back():
        nc.clear_and_free_semaphores(made)
        nc.all_engine_barrier()

    ctx.callback(give_back)
    return sem


def rows(t):
    return P if t < NPT else NS


class Count:

    def __init__(self):
        self.base, self.n, self.turn, self.per = 0, 0, None, 0

    def up(self, k=1):
        self.n += k
        return k

    def now(self):
        if self.turn is None:
            return self.base + self.n
        return self.turn * self.per + (self.base + self.n)

    def enter(self, turn, per):
        self.base, self.n, self.turn, self.per = self.base + self.n, 0, turn, per

    def leave(self, turns):
        assert self.n == self.per, (self.n, self.per)
        self.base, self.n, self.turn = self.base + turns * self.per, 0, None


def build_program(nc, t_in, t_out):
    ctx = ExitStack()
    with ctx:
        persist = Persistent(nc, ctx, t_in)
        tiles = FirstTiles(nc)
        modulation(nc, t_in, persist, tiles)
        first = FirstWeights(nc, "ro", t_in["ret_w_out"][0], H * DV // P)
        retention_heads(nc, t_in, t_out, persist, tiles, first)
        x = ctx.enter_context(nc.sbuf_tensor("x", [P, NT, D], F32))
        outward(nc, t_in, persist, "ro", persist.retained, first, True, 0, x, Finish(load=reload_x(t_in)))
        shared_kv_and_queries(nc, t_in, t_out, persist, x)
        first = FirstWeights(nc, "ao", t_in["sb_w_out"][0], KD)
        attention_layer(nc, t_in, t_out, persist, first)
        outward(nc, t_in, persist, "ao", persist.attended, first, False, 1, x, Finish(store=store_y(t_out)))


class Persistent:

    def __init__(self, nc, ctx, t_in):
        def sb(name, shape, dt=F32):
            return ctx.enter_context(nc.sbuf_tensor(name, shape, dt))

        self.ident = sb("ident", [P, P])
        self.gain = sb("gain", [P, 3, KD, NC])
        self.shift = sb("shift", [P, 3, KD, NC])
        self.gate = sb("gate", [NC, 2, D])
        self.cond_t = sb("cond_t", [P, KD, NC])
        self.norm_g = sb("norm_g", [P, KD])
        self.ret_g = sb("ret_g", [P, 2 * KD])
        self.k_gain = sb("k_gain", [P, DH])
        self.q_gain = sb("q_gain", [P, DH])
        self.eps = sb("eps", [P, 1])
        self.retained = nc.dram_tensor("retained", (NT * P, H * DV), F32, kind="Internal").ap()
        self.q_rows = nc.dram_tensor("q_rows", (NT * P, D), F32, kind="Internal").ap()
        self.g_rows = nc.dram_tensor("g_rows", (NT * P, D), F32, kind="Internal").ap()
        self.attended = nc.dram_tensor("attended", (NT * P, D), F32, kind="Internal").ap()


def modulation(nc, t_in, ps, tiles):
    ctx = ExitStack()
    with ctx:
        def sb(name, shape, dt=F32):
            return ctx.enter_context(nc.sbuf_tensor(name, shape, dt))

        sem = semaphores(nc, ctx, "mod")

        NCH = 3 * D // NB
        CG = 3
        SETS = NCH // CG
        cond = sb("cond", [NC, D])
        cond_act = sb("cond_act", [NC, D])
        vec_rows = sb("vec_rows", [5 * KD, P])
        vec_t = sb("vec_t", [P, 5 * KD])
        ada_bias = sb("ada_bias", [NC, 2, 3 * D])
        mod = sb("mod", [NC, 3 * D])
        w = sb("ada_w_sb", [P, 2, KD, CG * NB])
        acc = ctx.enter_context(nc.psum_tensor("mod_acc", [P, 2, NB], F32))
        tr = ctx.enter_context(nc.psum_tensor("mod_tr", [P, NB], F32))
        tr2 = ctx.enter_context(nc.psum_tensor("mod_tr2", [P, NB], F32))
        loaded_pool, tiles_loaded = sem("loaded_pool"), sem("tiles_loaded")
        assert nc.sbuf_base <= nc.sbuf_top - 2 * KD * (2 * DK + 2 * DV) * 4
        loaded, w_loaded, act_done = sem("loaded"), [[sem(f"ada_w{b}{k}") for k in range(2)] for b in range(2)], sem("mod_act")
        pe_c, pe_acc, pe_tr = sem("pe_cond_t"), sem("pe_mod_acc"), sem("pe_mod_tr")
        dve_c, dve_acc, dve_own = sem("dve_cond_t"), sem("dve_mod_acc"), sem("dve_mod_own")
        block = ctx.enter_context(nc.Block())

        @block.sync
        def _(sp):
            sp.dma_start(cond[0:1, :], t_in["c_prompt"]).then_inc(loaded, 16)
            sp.dma_start(cond[1:NC, :], t_in["c_sample"]).then_inc(loaded, 16)
            sp.dma_start(ps.ident[:], t_in["ident"]).then_inc(loaded, 16)
            sp.dma_start(vec_rows[0:2 * KD, :], t_in["norm_g"].rearrange("l (k p) -> (l k) p", p=P)).then_inc(loaded, 16)
            sp.dma_start(vec_rows[2 * KD:3 * KD, :], t_in["kv_norm_g"].rearrange("(k p) -> k p", p=P)).then_inc(loaded, 16)
            sp.dma_start(vec_rows[3 * KD:5 * KD, :], t_in["ret_norm_g"].rearrange("l (k p) -> (l k) p", p=P)).then_inc(loaded, 16)
            for n in range(SETS):
                c0 = n * CG * NB
                for k in range(2):
                    sp.dma_start(w[:, n, 4 * k:4 * k + 4, :], t_in["ada_w"][0].rearrange("(k p) n -> p k n", p=P)[
                        :, 4 * k:4 * k + 4, c0:c0 + CG * NB]).then_inc(w_loaded[n][k], 16)
            tiles.load(sp, t_in, tiles_loaded)

        @block.gpsimd
        def _(pool):
            pool.dma_start(ada_bias[:], t_in["ada_b"].rearrange("(o l) n -> o l n", o=1).to_broadcast([NC, 2, 3 * D])).then_inc(loaded_pool, 16)
            pool.dma_start(ps.k_gain[:], t_in["sb_k_g"].rearrange("(o n) -> o n", o=1).to_broadcast([P, DH])).then_inc(loaded_pool, 16)
            pool.dma_start(ps.q_gain[:], t_in["sb_q_g"].to_broadcast([P, DH])).then_inc(loaded_pool, 16)


        @block.scalar
        def _(act):
            act.wait_ge(loaded, 96)
            nc.scalar.activation(cond_act[:], cond[:], ACT.Silu).then_inc(act_done, 1)

        @block.tensor
        def _(pe):
            pe.wait_ge(loaded, 96)
            pe.wait_ge(act_done, 1)
            for k in range(KD):
                last = nc.tensor.transpose(tr[:, k * NC:(k + 1) * NC], cond_act[:, k * P:(k + 1) * P], ps.ident[0:NC, 0:NC])
            last.then_inc(pe_c, 1)
            nc.tensor.transpose(tr2[:, 0:5 * KD], vec_rows[:], ps.ident[0:5 * KD, 0:5 * KD]).then_inc(pe_c, 1)
            pe.wait_ge(dve_c, 1)
            for n in range(SETS):
                for k in range(KD):
                    if k % 4 == 0:
                        pe.wait_ge(w_loaded[n][k // 4], 16)
                    for c in range(CG):
                        last = nc.tensor.matmul(acc[32 * c:32 * c + NC, n, :], ps.cond_t[:, k, :],
                                                w[:, n, k, c * NB:(c + 1) * NB], start=k == 0, stop=k == KD - 1,
                                                tile_position=(0, 32 * c))
                last.then_inc(pe_acc, 1)
            pe.wait_ge(dve_acc, NCH)
            for k in range(2 * KD):
                last = nc.tensor.transpose(tr[:, k * NC:(k + 1) * NC], mod[:, k * P:(k + 1) * P], ps.ident[0:NC, 0:NC])
            last.then_inc(pe_tr, 1)

        @block.vector
        def _(dve):
            nc.vector.memset(ps.eps[:], EPS)
            dve.wait_ge(loaded_pool, 48)
            dve.wait_ge(pe_c, 1)
            nc.vector.tensor_copy(ps.cond_t[:].rearrange("p k c -> p (k c)"), tr[:, 0:KD * NC]).then_inc(dve_c, 1)
            dve.wait_ge(pe_c, 2)
            nc.vector.tensor_copy(vec_t[:], tr2[:, 0:5 * KD]).then_inc(dve_own, 1)
            for n in range(SETS):
                dve.wait_ge(pe_acc, n + 1)
                for c in range(CG):
                    cols = slice((n * CG + c) * NB, (n * CG + c + 1) * NB)
                    nc.vector.tensor_tensor(mod[:, cols], acc[32 * c:32 * c + NC, n, :], ada_bias[:, 0, cols],
                                            ALU.add).then_inc(dve_acc, 1)
            dve.wait_ge(dve_own, 1)
            dve.wait_ge(dve_acc, NCH)
            nc.vector.tensor_copy(ps.gate[:, 0, :], mod[:, 2 * D:3 * D])
            nc.vector.tensor_copy(ps.gate[:, 1, :], ada_bias[:, 1, 2 * D:3 * D])
            nc.vector.tensor_copy(ps.norm_g[:], vec_t[:, KD:2 * KD])
            nc.vector.tensor_copy(ps.ret_g[:], vec_t[:, 3 * KD:5 * KD])
            nc.vector.memset(ps.shift[:, 1, :, :], 0.0)
            nc.vector.tensor_copy(ps.gain[:, 1, :, :], vec_t[:, 2 * KD:3 * KD].unsqueeze(2).to_broadcast([P, KD, NC]))
            dve.wait_ge(pe_tr, 1)
            m = tr[:, 0:2 * KD * NC].rearrange("p (s k c) -> p s k c", s=2, k=KD)
            nc.vector.tensor_copy(ps.shift[:, 0, :, :], m[:, 0])
            nc.vector.scalar_tensor_tensor(ps.gain[:, 0, :, :], m[:, 1], 1.0,
                                           vec_t[:, 0:KD].unsqueeze(2).to_broadcast([P, KD, NC]), ALU.add, ALU.mult)


def tile_preparation(nc, ps, sem, sets, x, xn, full, squares, small, tr, hi, lo, x_ready, xn_free, h_free):
    ss, root, rstd = small[:, 0], small[:, 1], small[:, 2]
    squared, rooted, inverted, scaled = sem("x_squared"), sem("x_rooted"), sem("x_inverted"), sem("x_scaled")
    turned, sample_scaled, full_ready = sem("turned_x"), sem("sample_scaled"), sem("full_ready")
    h_hi_s, h_lo_s = sem("h_hi_s"), sem("h_lo_s")

    def act_slot(act, n, s):
        t, q = s - 1, n * NT + s - 1
        if 0 <= t < NT:
            act.wait_ge(inverted, t + 1)
            xn_free(act, n, t)
            if q >= 2:
                act.wait_ge(turned, q - 1)
            nc.scalar.activation(xn[0:rows(t), q % 2, :], x(t), ACT.Copy, scale=rstd[0:rows(t), t:t + 1]).then_inc(scaled, 1)
        if n == 0 and s < NT:
            r = rows(s)
            x_ready(act, s)
            if s:
                act.wait_ge(squared, s)
            nc.scalar.activation(squares[0:r], x(s), ACT.Square, accum_out=ss[0:r, s:s + 1]).then_inc(squared, 1)
            act.wait_ge(squared, s + 1)
            nc.scalar.activation(root[0:r, s:s + 1], ss[0:r, s:s + 1], ACT.Sqrt, scale=1.0 / D,
                                 bias=ps.eps[0:r]).then_inc(rooted, 1)
        t, q = s - 2, n * NT + s - 2
        if 0 <= t < NT:
            r = rows(t)
            act.wait_ge(full_ready, q + 1)
            h_free(act, n, t)
            nc.scalar.copy(hi[:, :, t * P:t * P + r], full[:, q % 2, :, 0:r]).then_inc(h_hi_s, 1)

    def pe_slot(pe, n, s):
        t, q = s - 1, n * NT + s - 1
        if 0 <= t < NT:
            r = rows(t)
            pe.wait_ge(scaled, q + 1)
            if q >= 2:
                pe.wait_ge(full_ready, q - 1)
            for k in range(KD):
                last = nc.tensor.transpose(tr(q)[:, k, 0:r], xn[0:r, q % 2, k * P:(k + 1) * P], ps.ident[0:r, 0:r])
            last.then_inc(turned, 1)

    def dve_slot(dve, n, s):
        t, q = s - 2, n * NT + s - 2
        if 0 <= t < NT:
            dve.wait_ge(turned, q + 1)
            if q >= 2:
                dve.wait_ge(h_lo_s, q - 1)
            if t < NPT:
                for k in range(KD):
                    last = nc.vector.tensor_scalar(full[:, q % 2, k, :], tr(q)[:, k, :], ps.gain[:, sets[n], k, 0:1],
                                                   ps.shift[:, sets[n], k, 0:1], ALU.mult, ALU.add)
                last.then_inc(full_ready, 1)
            else:
                each = [P, KD, DB, DS]
                cols = full[:, q % 2, :, 0:NS].rearrange("p k (b i) -> p k b i", b=DB)
                nc.vector.tensor_tensor(cols, tr(q)[:, :, 0:NS].rearrange("p k (b i) -> p k b i", b=DB),
                                        ps.gain[:, sets[n], :, 1:NC].unsqueeze(3).to_broadcast(each),
                                        ALU.mult).then_inc(sample_scaled, 1)
                dve.wait_ge(sample_scaled, n + 1)
                nc.vector.tensor_tensor(cols, cols, ps.shift[:, sets[n], :, 1:NC].unsqueeze(3).to_broadcast(each),
                                        ALU.add).then_inc(full_ready, 1)
        if n == 0 and s < NT:
            dve.wait_ge(rooted, s + 1)
            nc.vector.reciprocal(rstd[0:rows(s), s:s + 1], root[0:rows(s), s:s + 1]).then_inc(inverted, 1)

    def rest_slot(engine, n, s):
        t, q = s - 3, n * NT + s - 3
        if 0 <= t < NT:
            cols = slice(t * P, t * P + rows(t))
            engine.wait_ge(h_hi_s, q + 1)
            dst = lo[:, :, cols] if t < NPT else hi[:, :, SEQ + NS:]
            engine.tensor_tensor(dst, full[:, q % 2, :, 0:rows(t)], hi[:, :, cols].bitcast(F32),
                                    ALU.subtract).then_inc(h_lo_s, 1)

    return act_slot, pe_slot, dve_slot, rest_slot, scaled, h_lo_s


def product(nc, dst, h_hi, h_lo, w_hi, w_lo, t):
    for k in range(KD):
        if t < NPT:
            cols = slice(t * P, (t + 1) * P)
            nc.tensor.matmul(dst, h_hi[:, k, cols], w_hi[:, k, :], start=k == 0, stop=False)
            nc.tensor.matmul(dst, h_hi[:, k, cols], w_lo[:, k, :], start=False, stop=False)
            last = nc.tensor.matmul(dst, h_lo[:, k, cols], w_hi[:, k, :], start=False, stop=k == KD - 1)
        else:
            nc.tensor.matmul(dst, h_hi[:, k, SEQ:SEQ + 2 * NS], w_hi[:, k, :], start=k == 0, stop=False)
            last = nc.tensor.matmul(dst, h_hi[:, k, SEQ:SEQ + 2 * NS], w_lo[:, k, :], start=False, stop=k == KD - 1)
    return last


SLOTS = NT + 3


def retention_heads(nc, t_in, t_out, ps, tiles, first):
    ctx = ExitStack()
    with ctx:
        def sb(name, shape, dt=F32):
            return ctx.enter_context(nc.sbuf_tensor(f"rt_{name}", shape, dt))

        sem = semaphores(nc, ctx, "rt")

        h_hi = sb("h_hi", [P, KD, SEQ + 2 * NS], F32R)
        h_lo = sb("h_lo", [P, KD, SEQ], F32R)
        R = 3
        CR = 10
        QKV = 2 * DK + DV
        cos = sb("cos", [P, NT, DK])
        sin = sb("sin", [P, NT, DK])
        tables = sb("tables", [P, 2, 3, H])
        causal = sb("causal", [P, P + NS])
        own_rows = sb("own_rows", [NS, DB])
        raw = sb("raw", [P, R, 2, DK])
        by_cos = sb("by_cos", [P, 2, DK])
        by_sin = sb("by_sin", [P, 2, DK])
        rot = sb("rot", [P, R, 2, DK])
        v = sb("v", [P, R, DV])
        qk_t = sb("qk_t", [P, R, 2, P])
        probs = sb("probs", [P, R, P])
        state = sb("state", [P, DV])
        state_sum = sb("state_sum", [P, DV])
        at = nc.sbuf_base
        old = sb("old", [P, DB, DV])
        new = sb("new", [P, DB, DV])
        o = sb("o", [P, NT, DV])
        g = sb("g", [P, NT, DV])
        XR, x_ring = tiles.XR, tiles.x_ring
        xn = nc.alloc_sbuf_tensor_at("rt_xn", [P, 2, D], F32, offset=at)
        full = nc.alloc_sbuf_tensor_at("rt_full", [P, 2, KD, P], F32, offset=at + 4 * 2 * D)
        assert at + 4 * 4 * D <= nc.sbuf_base
        x_squares = sb("x_squares", [P, D])
        small = sb("small", [P, 3, NT])
        q_diag = sb("q_diag", [P, DB, NS])
        k_own = sb("k_own", [NS, DB, DK])
        qkv_s = sb("qkv_s", [NS, QKV])
        squares = sb("squares", [P, DV])
        ss = sb("ss", [P, NT])
        root = sb("root", [P, NT])
        rstd = sb("rstd", [P, NT])

        at = at_top(nc, 2 * KD * (QKV + DV) * 4)
        g_hi = nc.alloc_sbuf_tensor_at("rt_g_hi", [P, KD, DV], F32R, offset=at)
        g_lo = nc.alloc_sbuf_tensor_at("rt_g_lo", [P, KD, DV], F32R, offset=at + KD * DV * 4)
        g_raw = nc.alloc_sbuf_tensor_at("rt_g_raw", [P, KD, DV], F32, offset=at + KD * DV * 4)
        at += 2 * KD * DV * 4
        w_hi = nc.alloc_sbuf_tensor_at("rt_w_hi", [P, KD, QKV], F32R, offset=at)
        w_lo = nc.alloc_sbuf_tensor_at("rt_w_lo", [P, KD, QKV], F32R, offset=at + KD * QKV * 4)
        w_raw = nc.alloc_sbuf_tensor_at("rt_w_raw", [P, KD, QKV], F32, offset=at + KD * QKV * 4)

        def bank(name, n=1):
            return ctx.enter_context(nc.psum_tensor(f"rt_{name}", [P, n, NB], F32))

        acc, acc_g = bank("acc", 2), bank("acc_g", 2)
        tr, sc, out, st = bank("tr"), bank("sc"), bank("out"), bank("st")

        consts = sem("consts")
        w_loaded, g_loaded, old_loaded = sem("w_loaded"), sem("g_loaded"), sem("old_loaded")
        w_hi_s, w_lo_s, g_hi_s, g_lo_s = sem("w_hi"), sem("w_lo"), sem("g_hi"), sem("g_lo")
        projected, projected_g = sem("projected"), sem("projected_g")
        taken, taken_g, rotated, turned = sem("taken"), sem("taken_g"), sem("rotated"), sem("turned")
        turned_out, scored, masked, attended = sem("turned_out"), sem("scored"), sem("masked"), sem("attended")
        o_taken, state_ready, new_ready = sem("o_taken"), sem("state_ready"), sem("new_ready")
        rooted, gated, stored, cleared = sem("rooted"), sem("gated"), sem("stored"), sem("cleared")
        state_free, new_free, o_free, own = sem("state_free"), sem("new_free"), sem("o_free"), sem("own")
        k_own_s, storing = sem("k_own_s"), sem("storing")
        merged, merged_g, next_loaded = sem("merged"), sem("merged_g"), sem("next_loaded")
        x_loaded = [sem(f"x_loaded{n}") for n in range(XR)]

        SPLIT_SLOTS = (6, 8, 10, 11)

        def x_ready(act, t):
            if t >= XR:
                act.wait_ge(x_loaded[t % XR], 16 * (t // XR))

        act_slot, pe_slot, dve_slot, rest_slot, x_used, h_ready = tile_preparation(
            nc, ps, sem, [0], lambda t: x_ring[0:rows(t), t % XR, :], xn, full, x_squares, small,
            lambda q: (acc, acc_g)[q % 2][:].rearrange("p a (k c) -> p (a k) c", c=P), h_hi, h_lo, x_ready,
            lambda act, n, t: None, lambda act, n, t: None)
        block = ctx.enter_context(nc.Block())

        def after(h, t):
            return h * NT + (CR + t + 1)

        def freed(h, t, ring):
            if t >= ring:
                return h * NT + (CR + t - ring + 1)
            last = max(u for u in range(NT) if u % ring == t % ring)
            return h * NT + (CR - NT + last + 1)

        w_in = t_in["ret_w_in"][0].rearrange("(k p) n -> p k n", p=P)

        @block.sync
        def _(sp):
            sp.dma_start(cos[:], t_in["rope_cos"]).then_inc(consts, 16)
            sp.dma_start(sin[:], t_in["rope_sin"]).then_inc(consts, 16)
            sp.dma_start(tables[:], t_in["decays"]).then_inc(consts, 16)
            sp.dma_start(causal[:], t_in["causal"]).then_inc(consts, 16)
            sp.dma_start(own_rows[:], t_in["own_rows"]).then_inc(consts, 16)
            with sp.Fori(0, H) as h:
                sp.wait_ge(projected, h * NT + CR)
                sp.dma_start(w_raw[:, :, 0:DK], w_in[:, :, bass.ds(h * DK, DK)]).then_inc(w_loaded, 16)
                sp.dma_start(w_raw[:, :, DK:2 * DK], w_in[:, :, bass.ds(h * DK + H * DK, DK)]).then_inc(w_loaded, 16)
                sp.dma_start(w_raw[:, :, 2 * DK:QKV], w_in[:, :, bass.ds(h * DV + 2 * H * DK, DV)]).then_inc(w_loaded, 16)
                sp.wait_ge(h_ready, NT)
                sp.wait_ge(new_ready, h + CR)
                sp.dma_start(old[:], t_in["state_ret"][0].rearrange("b h k e -> h k b e")[bass.ds(h, 1)].rearrange(
                    "o k b e -> (o k) b e")).then_inc(old_loaded, 16)
                sp.wait_ge(projected_g, h * NT + CR)
                sp.dma_start(g_raw[:], w_in[:, :, bass.ds(h * DV + 2 * H * DK + H * DV, DV)]).then_inc(g_loaded, 16)
            sp.wait_ge(projected, H * NT + CR)
            first.load(sp, next_loaded)

        @block.gpsimd
        def _(pool):
            nc.gpsimd.memset(q_diag[:], 0.0).then_inc(cleared, 1)
            for i in range(SLOTS):
                if i >= 2 and i - 2 + XR < NT:
                    t = i - 2 + XR
                    pool.wait_ge(x_used, t - XR + 1)
                    pool.dma_start(x_ring[0:rows(t), t % XR, :], input_rows(t_in, t)).then_inc(x_loaded[t % XR], 16)
                rest_slot(pool, 0, i)
            for s in (state_free, new_free, o_free):
                pool.sem_inc(s, 1)
            with pool.Fori(0, H) as h:
                pool.wait_ge(state_ready, after(h, NPT - 1))
                pool.sem_inc(storing, 1)
                pool.dma_start(t_out["st_prompt"][0, 0][bass.ds(h, 1)].rearrange("o k e -> (o k) e"), state[:]).then_inc(stored, 16)
                pool.wait_ge(stored, h * 64 + 16)
                pool.sem_inc(state_free, 1)
                pool.wait_ge(new_ready, h + (CR + 1))
                pool.sem_inc(storing, 1)
                pool.dma_start(t_out["st_sample"][0].rearrange("b h k e -> h k b e")[bass.ds(h, 1)].rearrange(
                    "o k b e -> (o k) b e"), new[:]).then_inc(stored, 16)
                pool.wait_ge(stored, h * 64 + 32)
                pool.sem_inc(new_free, 1)
                pool.wait_ge(gated, (h + 1) * NT)
                pool.sem_inc(storing, 1)
                pool.dma_start(ps.retained[0:SEQ, bass.ds(h * DV, DV)].rearrange("(t p) e -> p t e", p=P), o[:, 0:NPT, :]).then_inc(stored, 16)
                pool.dma_start(ps.retained[SEQ:SEQ + NS, bass.ds(h * DV, DV)], o[0:NS, NPT, :]).then_inc(stored, 16)
                pool.wait_ge(stored, h * 64 + 64)
                pool.sem_inc(o_free, 1)

        @block.tensor
        def _(pe):
            pe.sem_inc(projected, CR)
            pe.sem_inc(projected_g, CR)
            pe.sem_inc(attended, CR)
            for i in range(SLOTS):
                pe_slot(pe, 0, i)
            pe.wait_ge(h_ready, NT)
            pe.wait_ge(consts, 80)

            def turn(h, t):
                pe.wait_ge(rotated, after(h, t))
                pe.wait_ge(turned_out, freed(h, t, 1))
                for n in range(2):
                    last = nc.tensor.transpose(tr[:, 0, n * P:(n + 1) * P], rot[:, t % R, n, :], ps.ident[:])
                last.then_inc(turned, 1)

            def score(h, t):
                r = rows(t)
                pe.wait_ge(turned_out, after(h, t))
                pe.wait_ge(masked, freed(h, t, 1))
                nc.tensor.matmul(sc[0:r, 0, 0:r], qk_t[:, t % R, 1, 0:r], qk_t[:, t % R, 0, 0:r],
                                 start=True, stop=True).then_inc(scored, 1)

            def attend(h, t):
                r = rows(t)
                pe.wait_ge(masked, after(h, t))
                pe.wait_ge(o_taken, freed(h, t, 1))
                if t == NPT:
                    pe.wait_ge(old_loaded, (h + 1) * 16)
                    pe.wait_ge(k_own_s, h + 1)
                    for b in range(DB):
                        nc.tensor.matmul(out[0:r, 0, 0:DV], q_diag[:, b, :], old[:, b, :], start=b == 0, stop=False)
                elif t > 0:
                    pe.wait_ge(state_ready, after(h, t - 1))
                    nc.tensor.matmul(out[0:r, 0, 0:DV], qk_t[:, t % R, 0, :], state[:], start=True, stop=False)
                last = nc.tensor.matmul(out[0:r, 0, 0:DV], probs[0:r, t % R, 0:r], v[0:r, t % R, :], start=t == 0, stop=True)
                if t < NPT:
                    pe.wait_ge(state_ready, freed(h, t, 1) if t else h * NT + CR)
                    last = nc.tensor.matmul(st[:, 0, 0:DV], rot[0:r, t % R, 1, :], v[0:r, t % R, :], start=True, stop=True)
                else:
                    pe.wait_ge(state_ready, after(h, NPT - 1))
                    pe.wait_ge(taken, after(h, NPT))
                    for b in range(DB):
                        dst = (acc[:, 0], acc[:, 1], st[:, 0], tr[:, 0])[b // 2]
                        last = nc.tensor.matmul(dst[:, (b % 2) * DV:(b % 2 + 1) * DV], k_own[:, b, :], v[0:NS, t % R, :],
                                                start=b % 2 == 0, stop=True, skip_group_check=True)
                last.then_inc(attended, 1)

            def later_steps(h, s):
                if 0 <= s - 3 < NT:
                    attend(h, s - 3)
                if 0 <= s - 2 < NT:
                    score(h, s - 2)

            with pe.Fori(0, H) as h:
                pe.wait_ge(new_ready, h + CR)
                pe.wait_ge(w_lo_s, (h + 1) * 4)
                for t in range(NT):
                    later_steps(h, t)
                    pe.wait_ge(taken, freed(h, t, 2))
                    product(nc, acc[:, t % 2, 0:QKV], h_hi, h_lo, w_hi, w_lo, t).then_inc(projected, 1)
                    if t:
                        turn(h, t - 1)
                pe.wait_ge(g_lo_s, (h + 1) * 2)
                for t in range(NT):
                    later_steps(h, NT + t)
                    pe.wait_ge(taken_g, freed(h, t, 2))
                    product(nc, acc_g[:, t % 2, 0:DV], h_hi, h_lo, g_hi, g_lo, t).then_inc(projected_g, 1)
                    if t == 0:
                        turn(h, NT - 1)

        @block.scalar
        def _(act):
            act.sem_inc(taken, CR)
            act.sem_inc(taken_g, CR)
            act.sem_inc(turned_out, CR)
            act.sem_inc(o_taken, CR)

            def take(h, t):
                r, kind = rows(t), 0 if t < NPT else 1
                if t < NPT:
                    act.wait_ge(projected, after(h, t))
                    src = acc[:, t % 2, :]
                else:
                    act.wait_ge(merged, h + 1)
                    src = qkv_s
                act.wait_ge(rotated, freed(h, t, R))
                act.wait_ge(attended, freed(h, t, R))
                nc.scalar.copy(v[0:r, t % R, :], src[0:r, 2 * DK:QKV])
                for n in range(2):
                    last = nc.scalar.activation(raw[0:r, t % R, n, :], src[0:r, n * DK:(n + 1) * DK], ACT.Copy,
                                                scale=tables[0:r, kind, n, bass.ds(h, 1)])
                last.then_inc(taken, 1)

            def turn_out(h, t):
                r = rows(t)
                act.wait_ge(turned, h * NT + (t + 1))
                act.wait_ge(attended, freed(h, t, R))
                if t == NPT:
                    nc.scalar.copy(diagonal(q_diag, DB, NS, DS), tr[:, 0, 0:NS].rearrange("p (b i) -> p b i", i=DS))
                src = tr[:, 0, 0:2 * P].rearrange("p (n c) -> p n c", n=2)[:, :, 0:r]
                nc.scalar.copy(qk_t[:, t % R, :, 0:r], src).then_inc(turned_out, 1)

            def take_o(h, t):
                r = rows(t)
                act.wait_ge(attended, after(h, t))
                if t == 0:
                    act.wait_ge(o_free, h + 1)
                nc.scalar.copy(o[0:r, t, :], out[0:r, 0, 0:DV])
                act.wait_ge(o_taken, freed(h, t, 1))
                nc.scalar.activation(squares[0:r, :], out[0:r, 0, 0:DV], ACT.Square,
                                     accum_out=ss[0:r, t:t + 1]).then_inc(o_taken, 1)

            def split_w(h, q):
                act.wait_ge(w_loaded, (h + 1) * 48)
                nc.scalar.copy(w_hi[:, 2 * q:2 * q + 2, :], w_raw[:, 2 * q:2 * q + 2, :]).then_inc(w_hi_s, 1)

            def split_g(h, q):
                act.wait_ge(g_loaded, (h + 1) * 16)
                nc.scalar.copy(g_hi[:, 4 * q:4 * q + 4, :], g_raw[:, 4 * q:4 * q + 4, :]).then_inc(g_hi_s, 1)

            def head(h, last):
                for t in range(NT):
                    if t >= 3:
                        take_o(h, t - 3)
                    if t in (2, 3):
                        split_g(h, t - 2)
                    if t:
                        turn_out(h, t - 1)
                    take(h, t)
                for t in range(NT):
                    if t < 3:
                        take_o(h, NT + t - 3)
                    if not last and 4 <= t < 8:
                        split_w(h + 1, t - 4)
                    if t < NPT:
                        act.wait_ge(projected_g, after(h, t))
                        nc.scalar.activation(g[:, t, :], acc_g[:, t % 2, 0:DV], ACT.Silu).then_inc(taken_g, 1)
                    else:
                        act.wait_ge(merged_g, h + 1)
                        nc.scalar.activation(g[0:NS, t, :], g[0:NS, t, :], ACT.Silu).then_inc(taken_g, 1)
                    if t == 0:
                        turn_out(h, NT - 1)
                nc.scalar.activation(root[:], ss[:], ACT.Sqrt, scale=1.0 / DV, bias=ps.eps[:]).then_inc(rooted, 1)

            for i in range(SLOTS):
                act_slot(act, 0, i)
                if i in SPLIT_SLOTS:
                    split_w(0, SPLIT_SLOTS.index(i))
            act.wait_ge(h_ready, NT)
            act.wait_ge(consts, 80)
            act.wait_ge(cleared, 2)

            with act.Fori(0, H - 1) as h:
                head(h, False)
            head(H - 1, True)

        @block.vector
        def _(dve):
            own_n = Count()
            for s in (rotated, masked, state_ready, new_ready):
                dve.sem_inc(s, CR)
            nc.vector.memset(ss[:], 1.0).then_inc(cleared, 1)
            dve.wait_ge(consts, 80)
            dve.sem_inc(own, own_n.up())

            def rotate(h, t):
                r = rows(t)
                dve.wait_ge(taken, after(h, t))
                dve.wait_ge(attended, freed(h, t, R))
                dve.wait_ge(rotated, freed(h, t, 1))
                dve.wait_ge(own, own_n.now())
                halves = raw[0:r, t % R].rearrange("p n (a c) -> p n a c", a=2)
                table = sin[0:r, t].rearrange("p (a c) -> p a c", a=2)
                nc.vector.tensor_tensor(by_cos[0:r], raw[0:r, t % R], cos[0:r, t].unsqueeze(1).to_broadcast([r, 2, DK]), ALU.mult)
                for a in range(2):
                    last = nc.vector.tensor_tensor(by_sin[0:r, :, a * 64:(a + 1) * 64], halves[:, :, 1 - a, :],
                                                   table[:, a, :].unsqueeze(1).to_broadcast([r, 2, 64]), ALU.mult)
                last.then_inc(own, own_n.up())
                dve.wait_ge(own, own_n.now())
                nc.vector.tensor_tensor(rot[0:r, t % R], by_cos[0:r], by_sin[0:r], ALU.add).then_inc(rotated, 1)

            def mask(h, t):
                r = rows(t)
                dve.wait_ge(scored, h * NT + (t + 1))
                table = causal[:, 0:P] if t < NPT else causal[0:NS, P:P + NS]
                nc.vector.tensor_tensor(probs[0:r, t % R, 0:r], sc[0:r, 0, 0:r], table, ALU.mult).then_inc(masked, 1)

            def spread_k(h):
                dve.wait_ge(rotated, after(h, NPT))
                nc.vector.tensor_tensor(k_own[:], rot[0:NS, NPT % R, 1, :].unsqueeze(1).to_broadcast([NS, DB, DK]),
                                        own_rows[:].unsqueeze(2).to_broadcast([NS, DB, DK]), ALU.mult).then_inc(k_own_s, 1)

            def update(h, t):
                decay = tables[:, 0 if t < NPT else 1, 2, bass.ds(h, 1)]
                dve.wait_ge(attended, after(h, t))
                if t == 0:
                    dve.wait_ge(state_free, h + 1)
                    nc.vector.tensor_scalar(state[:], st[:, 0, 0:DV], decay, None, ALU.mult).then_inc(state_ready, 1)
                elif t < NPT:
                    dve.wait_ge(state_ready, after(h, t - 1))
                    nc.vector.tensor_tensor(state_sum[:], st[:, 0, 0:DV], state[:], ALU.add).then_inc(own, own_n.up())
                    dve.wait_ge(own, own_n.now())
                    nc.vector.tensor_scalar(state[:], state_sum[:], decay, None, ALU.mult).then_inc(state_ready, 1)
                else:
                    dve.wait_ge(new_free, h + 1)
                    for n, src in enumerate((acc[:, 0], acc[:, 1], st[:, 0], tr[:, 0])):
                        pair = slice(2 * n, 2 * n + 2)
                        last = nc.vector.tensor_tensor(new[:, pair, :], src.rearrange("p (b e) -> p b e", b=2),
                                                       old[:, pair, :], ALU.add)
                    last.then_inc(own, own_n.up())
                    dve.wait_ge(own, own_n.now())
                    nc.vector.tensor_scalar(new[:], new[:], decay, None, ALU.mult).then_inc(new_ready, 1)
                    dve.sem_inc(state_ready, 1)

            def steps(h, s):
                if 0 <= s - 3 < NT:
                    update(h, s - 3)
                if 0 <= s - 2 < NT:
                    mask(h, s - 2)

            def split_w(h, q):
                dve.wait_ge(w_hi_s, h * 4 + (q + 1))
                part = slice(2 * q, 2 * q + 2)
                nc.vector.tensor_tensor(w_lo[:, part, :], w_raw[:, part, :], w_hi[:, part, :].bitcast(F32),
                                        ALU.subtract).then_inc(w_lo_s, 1)

            def split_g(h, q):
                dve.wait_ge(g_hi_s, h * 2 + (q + 1))
                part = slice(4 * q, 4 * q + 4)
                nc.vector.tensor_tensor(g_lo[:, part, :], g_raw[:, part, :], g_hi[:, part, :].bitcast(F32),
                                        ALU.subtract).then_inc(g_lo_s, 1)

            def head(h, last):
                for t in range(NT):
                    steps(h, t)
                    if t in (2, 3):
                        split_g(h, t - 2)
                    if t == NPT:
                        dve.wait_ge(projected, after(h, t))
                        dve.wait_ge(taken, h * NT + CR)
                        nc.vector.tensor_copy(qkv_s[:], acc[0:NS, t % 2, :]).then_inc(own, own_n.up())
                        dve.wait_ge(own, own_n.now())
                        nc.vector.tensor_tensor(qkv_s[:], qkv_s[:], acc[NS:P, t % 2, :], ALU.add).then_inc(merged, 1)
                    rotate(h, t)
                for t in range(NT):
                    steps(h, NT + t)
                    if t == 1:
                        spread_k(h)
                    if t == NPT:
                        dve.wait_ge(projected_g, after(h, t))
                        nc.vector.tensor_copy(g[0:NS, t, :], acc_g[0:NS, t % 2, 0:DV]).then_inc(own, own_n.up())
                        dve.wait_ge(own, own_n.now())
                        nc.vector.tensor_tensor(g[0:NS, t, :], g[0:NS, t, :], acc_g[NS:P, t % 2, 0:DV], ALU.add).then_inc(merged_g, 1)
                    if not last and 4 <= t < 8:
                        split_w(h + 1, t - 4)
                dve.wait_ge(rooted, h + 1)
                nc.vector.reciprocal(rstd[:], root[:]).then_inc(own, own_n.up())
                dve.wait_ge(own, own_n.now())
                for t in range(NT):
                    r = rows(t)
                    nc.vector.scalar_tensor_tensor(o[0:r, t, :], o[0:r, t, :], rstd[0:r, t:t + 1], g[0:r, t, :],
                                                   ALU.mult, ALU.mult).then_inc(gated, 1)

            for i in range(SLOTS):
                dve_slot(dve, 0, i)
                if i in SPLIT_SLOTS:
                    split_w(0, SPLIT_SLOTS.index(i))
            dve.wait_ge(h_ready, NT)
            with dve.Fori(0, H - 1) as h:
                own_n.enter(h, NT + (NPT - 1) + 1 + 1 + 2)
                head(h, False)
            own_n.leave(H - 1)
            head(H - 1, True)


class SampleInputs:
    RING = 4

    def __init__(self, nc, ctx):
        def sb(name, shape, dt=F32):
            return ctx.enter_context(nc.sbuf_tensor(f"sa_{name}", shape, dt))

        self.pages = sb("pages", [1, DB * NPG], I32)
        self.hidden = sb("hidden", [P, 2, DB, NS])
        self.bias_col = sb("bias_col", [AH, 1])
        self.head_rows = sb("head_rows", [AH, P])
        self.new_rows = sb("new_rows", [NS, 4, D])
        self.k_pages = sb("k_pages", [P, self.RING, NPG, D])

    def load(self, sp, t_in, t_out, ps, pages_s, inputs_s):
        sp.dma_start(self.pages[:], t_in["page_table"].rearrange("b (o n) -> o (b n)", o=1)).then_inc(pages_s, 16)
        sp.dma_start(self.hidden[:], t_in["hidden_s"]).then_inc(inputs_s, 16)
        sp.dma_start(self.bias_col[:], t_in["sb_bias"].rearrange("o (h u) -> (o h) u", u=1)).then_inc(inputs_s, 16)
        sp.dma_start(self.head_rows[:], t_in["head_rows"]).then_inc(inputs_s, 16)
        for n, src in enumerate((ps.q_rows[SEQ:SEQ + NS, :], t_out["k_sample"].rearrange("b i h d -> (b i) (h d)"),
                                 t_out["v_sample"].rearrange("b i h d -> (b i) (h d)"), ps.g_rows[SEQ:SEQ + NS, :])):
            sp.dma_start(self.new_rows[:, n, :], src).then_inc(inputs_s, 16)
        sp.wait_ge(pages_s, 16)
        for b in range(self.RING):
            for n in range(NPG):
                self.load_page(sp, t_in, "cache_k", self.k_pages[:, b, n, :], b * NPG + n, inputs_s)

    def load_page(self, sp, t_in, cache, dst, entry, signal):
        page = sp.value_load(self.pages[0:1, bass.ds(entry, 1)], min_val=0, max_val=t_in[cache].shape[0] - 1)
        sp.dma_start(dst, t_in[cache][bass.ds(page, 1)].rearrange("o s h d -> (o s) (h d)")).then_inc(signal, 16)

    LOADED = 16 * (3 + 4 + RING * NPG)


def attention_layer(nc, t_in, t_out, ps, first):
    ctx = ExitStack()
    with ctx:
        sample = SampleInputs(nc, ctx)
        prompt_attention(nc, t_in, t_out, ps, sample)
        sample_attention(nc, t_in, t_out, ps, sample, first)


def prompt_attention(nc, t_in, t_out, ps, sample):
    ctx = ExitStack()
    with ctx:
        def sb(name, shape, dt=F32):
            return ctx.enter_context(nc.sbuf_tensor(f"pa_{name}", shape, dt))

        sem = semaphores(nc, ctx, "pa")

        BODY_HEADS = 4
        UNITS = BODY_HEADS * NPT
        TURNS = AH // BODY_HEADS
        PAIRS = BODY_HEADS // 2
        LAG = 3
        CR = 8
        far_below = sb("far_below", [P, P])
        far_r = sb("far_r", [P, P], F32R)
        ident_r = sb("ident_r", [P, P], F32R)
        bias_row = sb("bias_row", [P, AH])
        bias = sb("bias", [P, 2, AH])
        bias_now = sb("bias_now", [P, 2, BODY_HEADS])
        k2, q2, v2, g2 = (sb(n, [P, 2, NPT, 2 * DH]) for n in ("k2", "q2", "v2", "g2"))
        q4 = sb("q4", [P, 2, 2, DH])
        k_parts = sb("k_parts", [P, NPT, 2, 2, DH], F32R)
        k_t = sb("k_t", [P, 2, SEQ], F32R)
        q_hi = sb("q_hi", [P, 2, P], F32R)
        q_lo = sb("q_lo", [P, 2, P], F32R)
        take = sb("take", [P, 2, SEQ])
        keep = sb("keep", [P, 2, SEQ])
        after_key = sb("after_key", [P, 2, SEQ + 8])
        w = sb("w", [P, 2, SEQ])
        w_t = sb("w_t", [P, 2, SEQ])
        o2 = sb("o2", [P, 2, NPT, 2 * DH])

        def bank(name, n=1):
            return ctx.enter_context(nc.psum_tensor(f"pa_{name}", [P, n, NB], F32))

        z, wt, kq, out = bank("z", 4), bank("wt", 2), bank("kq"), bank("out")
        consts, started = sem("consts"), sem("started")
        loaded = {name: [sem(f"{name}_loaded{n}") for n in range(2)] for name in "kqvg"}
        stored = [sem("stored0"), sem("stored1")]
        k_hi_s, k_split, k_turned, k_taken = sem("k_hi_s"), sem("k_split"), sem("k_turned"), sem("k_taken")
        q_doubled, q_turned, q_hi_s, q_lo_s = sem("q_doubled"), sem("q_turned"), sem("q_hi_s"), sem("q_lo_s")
        scored, sticks, weighed = sem("scored"), sem("sticks"), sem("weighed")
        w_turned, w_taken_a, w_taken_v, attended, gated = (sem("w_turned"), sem("w_taken_a"), sem("w_taken_v"),
                                                           sem("attended"), sem("gated"))
        bias_s, scanned = sem("bias_s"), sem("scanned")
        out_free, out_taken = sem("out_free"), sem("out_taken")
        pages_s, inputs_s = sem("pages_s"), sem("inputs_s")
        block = ctx.enter_context(nc.Block())

        def done(i, s):
            return i * UNITS + (s + 1 + CR)

        def wide(s):
            return (where(s)[2] + 1) * P

        def where(s):
            s %= UNITS
            hh = (s // NPT) % 2
            return s // (2 * NPT), hh, (NPT - 1 - s % NPT) if hh else s % NPT

        K_TURNS, K_SPLIT = (1, 2, 13, 14), 12

        def k_part(s):
            return K_TURNS.index(s % (2 * NPT)) % 2

        rows_of = {
            "k": t_out["k_prompt"][0].rearrange("(t p) h d -> p t (h d)", p=P),
            "q": ps.q_rows[0:SEQ, :].rearrange("(t p) c -> p t c", p=P),
            "v": t_out["v_prompt"][0].rearrange("(t p) h d -> p t (h d)", p=P),
            "g": ps.g_rows[0:SEQ, :].rearrange("(t p) c -> p t c", p=P),
        }

        @block.sync
        def _(sp):
            sp.dma_start(far_below[:], t_in["far_below"]).then_inc(consts, 16)
            sp.dma_start(bias_row[:], t_in["sb_bias"].to_broadcast([P, AH])).then_inc(consts, 16)
            with sp.Fori(0, TURNS) as i:
                for pair in range(PAIRS):
                    sp.wait_ge(gated, i * PAIRS + (pair + 1))
                    for buf, name in ((k2, "k"), (q2, "q"), (v2, "v"), (g2, "g")):
                        sp.dma_start(buf[:, pair], rows_of[name][:, :, bass.ds(i * (BODY_HEADS * DH) + pair * 2 * DH, 2 * DH)]).then_inc(loaded[name][pair], 16)
            sample.load(sp, t_in, t_out, ps, pages_s, inputs_s)
            sp.wait_ge(inputs_s, sample.LOADED)

        @block.gpsimd
        def _(pool):
            pool.sem_inc(out_free, 2)

            def double(i, s):
                pair, hh, t = where(s)
                pool.wait_ge(loaded["q"][pair], i * 16 + (16 if s < UNITS else 32))
                pool.wait_ge(q_turned, done(i, s - 2))
                pool.sem_inc(started, 1)
                src = q2[:, pair, t, hh * DH:(hh + 1) * DH].unsqueeze(1).to_broadcast([P, 2, DH])
                nc.gpsimd.tensor_copy(q4[:, s % 2], src).then_inc(q_doubled, 1)

            def store(i, pair):
                pool.wait_ge(gated, i * PAIRS + (pair + 3))
                pool.sem_inc(started, 1)
                dst = ps.attended[0:SEQ, :].rearrange("(t p) c -> p t c", p=P)
                pool.dma_start(dst[:, :, bass.ds(i * (BODY_HEADS * DH) + pair * 2 * DH, 2 * DH)], o2[:, pair]).then_inc(stored[pair], 16)

            def release(i, pair):
                pool.wait_ge(stored[pair], i * 16 + 16)
                pool.sem_inc(out_free, 1)

            def turn(i, first, last):
                for s in range(UNITS):
                    if not (last and s + 2 >= UNITS):
                        double(i, s + 2)
                    if s == 4 and not first:
                        store(i - 1, 1)
                    if s == 12 and not first:
                        release(i - 1, 1)
                    if s == 2 * NPT + 4:
                        store(i, 0)
                    if s == 2 * NPT + 12:
                        release(i, 0)

            double(0, 0)
            double(0, 1)
            turn(0, True, False)
            with pool.Fori(1, TURNS - 1) as i:
                turn(i, False, False)
            turn(TURNS - 1, False, True)
            store(TURNS - 1, 1)
            pool.wait_ge(stored[0], 16 * TURNS)
            pool.wait_ge(stored[1], 16 * TURNS)

        @block.tensor
        def _(pe):
            for s in (scored, q_turned, w_turned, attended):
                pe.sem_inc(s, CR)

            def turn_q(i, s):
                pe.wait_ge(q_doubled, i * UNITS + (s + 1))
                pe.wait_ge(q_lo_s, done(i, s - 1))
                nc.tensor.transpose(kq[:, 0, 0:P], q4[:, s % 2].rearrange("p a d -> p (a d)"), ps.ident[:]).then_inc(q_turned, 1)

            def turn_k(head, hh, part, q_out):
                pe.wait_ge(q_lo_s, q_out)
                pe.wait_ge(k_split, head + (2 - hh))
                for n in range(4):
                    t = 4 * part + n
                    last = nc.tensor.transpose(kq[:, 0, n * P:(n + 1) * P],
                                               k_parts[:, t, hh].rearrange("p a d -> p (a d)").bitcast(F32), ps.ident[:])
                last.then_inc(k_turned, 1)

            def score(i, s):
                pair, hh, t = where(s)
                n = wide(s)
                pe.wait_ge(sticks, done(i, s - 2))
                if s % NPT == 0:
                    pe.wait_ge(k_taken, i * (2 * BODY_HEADS) + 2 * (s // NPT + 1))
                pe.wait_ge(q_lo_s, done(i, s))
                for c in range(0, n, NB):
                    m = min(NB, n - c)
                    own = c + m == n
                    dst = z[:, 2 * (s % 2) + c // NB, 0:m]
                    nc.tensor.matmul(dst, q_hi[:, s % 2, :], k_t[:, hh, c:c + m], start=True, stop=False)
                    last = nc.tensor.matmul(dst, q_lo[:, s % 2, :], k_t[:, hh, c:c + m], start=False, stop=not own)
                    if own:
                        last = nc.tensor.matmul(dst[:, m - P:m], ident_r[:], far_r[:], start=False, stop=True)
                last.then_inc(scored, 1)

            def turn_w(i, s):
                pe.wait_ge(weighed, done(i, s))
                pe.wait_ge(w_taken_a, done(i, s - 1))
                pe.wait_ge(w_taken_v, done(i, s - 1))
                for b in range(wide(s) // P):
                    last = nc.tensor.transpose(wt[:, b // 4, (b % 4) * P:(b % 4 + 1) * P], w[:, s % 2, b * P:(b + 1) * P], ps.ident[:])
                last.then_inc(w_turned, 1)

            def attend(i, s):
                pair, hh, t = where(s)
                pe.wait_ge(w_taken_a, done(i, s))
                pe.wait_ge(w_taken_v, done(i, s))
                pe.wait_ge(out_taken, done(i, s - 1))
                if s % (2 * NPT) == 0:
                    pe.wait_ge(loaded["v"][pair], i * 16 + 16)
                for b in range(t + 1):
                    last = nc.tensor.matmul(out[:, 0, 0:DH], w_t[:, s % 2, b * P:(b + 1) * P],
                                            v2[:, pair, b, hh * DH:(hh + 1) * DH], start=b == 0, stop=b == t)
                last.then_inc(attended, 1)

            def turn(i, first, last):
                for s in range(UNITS):
                    if not (last and s + 2 >= UNITS):
                        turn_q(i, s + 2)
                    if not (last and s + 1 >= UNITS):
                        score(i, s + 1)
                    if not first or s >= 2:
                        turn_w(i, s - 2)
                    if not first or s >= LAG:
                        attend(i, s - LAG)
                    if s % (2 * NPT) in K_TURNS and not (last and s >= UNITS - NPT):
                        nxt = s // NPT + 1
                        turn_k(i * BODY_HEADS + nxt, nxt % 2, k_part(s), done(i, s + 2))
                        pe.wait_ge(k_taken, i * (2 * BODY_HEADS) + (2 * nxt + k_part(s) + 1))

            for part in range(2):
                if part:
                    pe.wait_ge(k_taken, 1)
                pe.wait_ge(k_split, 2)
                for n in range(4):
                    last = nc.tensor.transpose(kq[:, 0, n * P:(n + 1) * P],
                                               k_parts[:, 4 * part + n, 0].rearrange("p a d -> p (a d)").bitcast(F32), ps.ident[:])
                last.then_inc(k_turned, 1)
            pe.wait_ge(k_taken, 2)
            turn_q(0, 0)
            turn_q(0, 1)
            score(0, 0)
            turn(0, True, False)
            with pe.Fori(1, TURNS - 1) as i:
                turn(i, False, False)
            turn(TURNS - 1, False, True)
            turn_w(TURNS - 1, UNITS - 2)
            attend(TURNS - 1, UNITS - 3)
            turn_w(TURNS - 1, UNITS - 1)
            attend(TURNS - 1, UNITS - 2)
            attend(TURNS - 1, UNITS - 1)

        @block.scalar
        def _(act):
            act.sem_inc(sticks, CR)
            act.sem_inc(w_taken_a, CR)

            def split_k(i, pair):
                act.wait_ge(loaded["k"][pair % PAIRS], (i + (1 if pair < PAIRS else 2)) * 16)
                src = k2[:, pair % PAIRS].rearrange("p t (h d) -> p t h d", h=2)
                for hh in range(2):
                    last = nc.scalar.copy(k_parts[:, :, hh, 0, :], src[:, :, hh, :])
                last.then_inc(k_hi_s, 1)

            def take_k(i, s, part):
                nxt = s // NPT + 1
                act.wait_ge(k_turned, i * (2 * BODY_HEADS) + (2 * nxt + part + 1))
                nc.scalar.copy(k_t[:, nxt % 2, part * NB:(part + 1) * NB], kq[:, 0, :]).then_inc(k_taken, 1)

            def take_q(i, s):
                act.wait_ge(q_turned, done(i, s))
                act.wait_ge(scored, done(i, s - 2))
                nc.scalar.copy(q_hi[:, s % 2, :], kq[:, 0, 0:P]).then_inc(q_hi_s, 1)

            def stick(i, s):
                n = wide(s)
                if s == 0:
                    act.wait_ge(bias_s, i + 1)
                act.wait_ge(scored, done(i, s))
                act.wait_ge(weighed, done(i, s - 2))
                src = z[:, 2 * (s % 2):2 * (s % 2) + 2, :].rearrange("p a b -> p (a b)")[:, 0:n]
                head = s // NPT
                nc.scalar.activation(keep[:, s % 2, 0:n], src, ACT.Sigmoid, scale=-(DH ** -0.5), bias=bias_now[:, 1, head:head + 1])
                nc.scalar.activation(take[:, s % 2, 0:n], src, ACT.Sigmoid, scale=DH ** -0.5,
                                     bias=bias_now[:, 0, head:head + 1]).then_inc(sticks, 1)

            def take_w(i, s):
                n = min(wide(s), NB)
                act.wait_ge(w_turned, done(i, s))
                act.wait_ge(attended, done(i, s - 2))
                nc.scalar.copy(w_t[:, s % 2, 0:n], wt[:, 0, 0:n]).then_inc(w_taken_a, 1)

            def turn(i, first, last):
                for s in range(UNITS):
                    if not (last and s + 2 >= UNITS):
                        take_q(i, s + 2)
                    stick(i, s)
                    if not first or s >= 2:
                        take_w(i, s - 2)
                    if s % (2 * NPT) == K_SPLIT and not (last and s > 2 * NPT):
                        split_k(i, s // (2 * NPT) + 1)
                    if s % (2 * NPT) in K_TURNS and not (last and s >= UNITS - NPT):
                        take_k(i, s, k_part(s))

            act.wait_ge(consts, 32)
            nc.scalar.copy(far_r[:], far_below[:])
            nc.scalar.copy(ident_r[:], ps.ident[:])
            split_k(0, 0)
            for part in range(2):
                act.wait_ge(k_turned, part + 1)
                nc.scalar.copy(k_t[:, 0, part * NB:(part + 1) * NB], kq[:, 0, :]).then_inc(k_taken, 1)
            take_q(0, 0)
            take_q(0, 1)
            turn(0, True, False)
            with act.Fori(1, TURNS - 1) as i:
                turn(i, False, False)
            turn(TURNS - 1, False, True)
            take_w(TURNS - 1, UNITS - 2)
            take_w(TURNS - 1, UNITS - 1)

        @block.vector
        def _(dve):
            for s in (q_lo_s, weighed, w_taken_v, out_taken):
                dve.sem_inc(s, CR)
            dve.sem_inc(gated, 2)
            nc.vector.memset(after_key[:], 1.0).then_inc(scanned, 1)
            dve.wait_ge(consts, 32)
            nc.vector.tensor_copy(bias[:, 0], bias_row[:])
            nc.vector.tensor_scalar(bias[:, 1], bias_row[:], -1.0, None, ALU.mult).then_inc(scanned, 1)
            dve.wait_ge(scanned, 2)

            def split_k(pair, count):
                dve.wait_ge(k_hi_s, count)
                src = k2[:, pair % PAIRS].rearrange("p t (h d) -> p t h d", h=2)
                for hh in range(2):
                    last = nc.vector.tensor_tensor(k_parts[:, :, hh, 1, :], src[:, :, hh, :], k_parts[:, :, hh, 0, :].bitcast(F32),
                                                   ALU.subtract)
                last.then_inc(k_split, 2)

            def rest_q(i, s):
                dve.wait_ge(q_hi_s, i * UNITS + (s + 1))
                nc.vector.tensor_tensor(q_lo[:, s % 2, :], kq[:, 0, 0:P], q_hi[:, s % 2, :].bitcast(F32), ALU.subtract).then_inc(q_lo_s, 1)

            def weigh(i, s):
                n = wide(s)
                dve.wait_ge(sticks, done(i, s))
                dve.wait_ge(w_turned, done(i, s - 2))
                dve.wait_ge(weighed, done(i, s - 1))
                k, a = keep[:, s % 2, 0:n], after_key[:, s % 2, 0:n]
                nc.vector.tensor_tensor_scan(a[:, ::-1], k[:, ::-1], k[:, ::-1], 1.0, ALU.mult, ALU.bypass).then_inc(scanned, 1)
                dve.wait_ge(scanned, i * UNITS + (s + 3))
                nc.vector.tensor_tensor(w[:, s % 2, 0:n], take[:, s % 2, 0:n], after_key[:, s % 2, 1:n + 1], ALU.mult).then_inc(weighed, 1)

            def take_w(i, s):
                n = wide(s)
                if n <= NB:
                    dve.wait_ge(w_turned, done(i, s))
                    dve.sem_inc(w_taken_v, 1)
                    return
                dve.wait_ge(w_turned, done(i, s))
                dve.wait_ge(attended, done(i, s - 2))
                nc.vector.tensor_copy(w_t[:, s % 2, NB:n], wt[:, 1, 0:n - NB]).then_inc(w_taken_v, 1)

            def gate(i, s):
                pair, hh, t = where(s)
                dve.wait_ge(attended, done(i, s))
                if s % (2 * NPT) == 0:
                    dve.wait_ge(loaded["g"][pair], i * 16 + 16)
                    dve.wait_ge(out_free, i * PAIRS + (s // (2 * NPT) + 1))
                cols = slice(hh * DH, (hh + 1) * DH)
                nc.vector.tensor_tensor(o2[:, pair, t, cols], out[:, 0, 0:DH], g2[:, pair, t, cols], ALU.mult).then_inc(out_taken, 1)
                if s % (2 * NPT) == 2 * NPT - 1:
                    dve.wait_ge(out_taken, done(i, s))
                    dve.sem_inc(gated, 1)

            def turn(i, first, last):
                for s in range(UNITS):
                    if not (last and s + 2 >= UNITS):
                        rest_q(i, s + 2)
                    if not first or s >= 1:
                        weigh(i, s - 1)
                    if s == 0:
                        nc.vector.tensor_scalar(bias_now[:], bias[:, :, bass.ds(i * BODY_HEADS, BODY_HEADS)], 1.0, None,
                                                ALU.mult).then_inc(bias_s, 1)
                    if not first or s >= 2:
                        take_w(i, s - 2)
                    if not first or s >= LAG:
                        gate(i, s - LAG)
                    if s % (2 * NPT) == K_SPLIT and not (last and s > 2 * NPT):
                        split_k(s // (2 * NPT) + 1, i * PAIRS + (s // (2 * NPT) + 2))

            split_k(0, 1)
            rest_q(0, 0)
            rest_q(0, 1)
            turn(0, True, False)
            with dve.Fori(1, TURNS - 1) as i:
                turn(i, False, False)
            turn(TURNS - 1, False, True)
            end = TURNS - 1
            weigh(end, UNITS - 1)
            take_w(end, UNITS - 2)
            gate(end, UNITS - 3)
            take_w(end, UNITS - 1)
            gate(end, UNITS - 2)
            gate(end, UNITS - 1)


def sample_attention(nc, t_in, t_out, ps, sample, first):
    ctx = ExitStack()
    with ctx:
        def sb(name, shape, dt=F32):
            return ctx.enter_context(nc.sbuf_tensor(f"sa_{name}", shape, dt))

        sem = semaphores(nc, ctx, "sa")

        def bank(name, n=1):
            return ctx.enter_context(nc.psum_tensor(f"sa_{name}", [P, n, NB], F32))

        HP = AH // 2
        NK = PAST + NS
        hidden, new_rows, k_pages = sample.hidden, sample.new_rows, sample.k_pages
        bias = sb("bias", [P, 2])
        q_t = sb("q_t", [P, HP, NS])
        g_t = sb("g_t", [P, HP, NS])
        RING = sample.RING
        TURNS = DB // RING
        v_pages = sb("v_pages", [P, RING, NPG, D])
        k_t = sb("k_t", [P, 2, HP, NK])
        q_diag = sb("q_diag", [P, 2, HP, P])
        take = sb("take", [P, 2, NK])
        keep = sb("keep", [P, 2, NK])
        after_key = sb("after_key", [P, 2, NK + 8])
        w = sb("w", [P, 2, NK])
        w_t = sb("w_t", [P, 2, NPG + 1, P])
        o_t = sb("o_t", [P, HP, NS])
        o_rows = sb("o_rows", [NS, D])
        kt, z, wt, out = bank("kt", 4), bank("z", 2), bank("wt"), bank("out")
        cleared = sem("cleared")
        k_loaded = [sem(f"k_loaded{n}") for n in range(RING)]
        v_loaded = [sem(f"v_loaded{n}") for n in range(RING)]
        new_turned, new_taken, k_turned, k_taken, placed = (sem("new_turned"), sem("new_taken"), sem("k_turned"),
                                                            sem("k_taken"), sem("placed"))
        scored, sticks, masked, weighed, scanned = sem("scored"), sem("sticks"), sem("masked"), sem("weighed"), sem("scanned")
        w_turned, w_taken, attended, gated, stored = (sem("w_turned"), sem("w_taken"), sem("attended"), sem("gated"),
                                                      sem("stored"))
        back, back_taken, next_loaded = sem("back"), sem("back_taken"), sem("next_loaded")
        block = ctx.enter_context(nc.Block())
        CR = 4

        def done(i, b):
            return i * RING + (b + 1 + CR)

        def ahead(i, b, n):
            return (i, b + n) if b + n < RING else (i + 1, b + n - RING)

        @block.sync
        def _(sp):
            def load_values(i, b):
                for n in range(NPG):
                    sample.load_page(sp, t_in, "cache_v", v_pages[:, b, n, :], i * (RING * NPG) + b * NPG + n, v_loaded[b])

            for b in range(RING):
                load_values(0, b)
            with sp.Fori(1, TURNS) as i:
                for b in range(RING):
                    sp.wait_ge(k_turned, done(i, b - RING))
                    for n in range(NPG):
                        sample.load_page(sp, t_in, "cache_k", k_pages[:, b, n, :], i * (RING * NPG) + b * NPG + n, k_loaded[b])
                    sp.wait_ge(attended, done(i, b - RING))
                    load_values(i, b)
            first.load(sp, next_loaded)

        @block.gpsimd
        def _(pool):
            nc.gpsimd.memset(q_diag[:], 0.0).then_inc(cleared, 1)
            pool.wait_ge(back_taken, HP // 4)
            pool.dma_start(ps.attended[SEQ:SEQ + NS, :], o_rows[:]).then_inc(stored, 16)
            pool.wait_ge(stored, 16)

        @block.tensor
        def _(pe):
            for s in (k_turned, scored, w_turned, attended):
                pe.sem_inc(s, CR)
            for n, src in enumerate((0, 1, 3)):
                for k in range(HP):
                    last = nc.tensor.transpose(kt[:, n, k * NS:(k + 1) * NS], new_rows[:, src, k * P:(k + 1) * P], ps.ident[0:NS, 0:NS])
                last.then_inc(new_turned, 1)
            nc.tensor.matmul(out[:, 0, 0:1], sample.head_rows[:], sample.bias_col[:], start=True, stop=True).then_inc(new_turned, 1)
            pe.wait_ge(new_taken, 4)

            def turn_k(i, b):
                pe.wait_ge(k_taken, i * (4 * RING) + (b * 4 + CR))
                pe.wait_ge(k_loaded[b], i * (16 * NPG))
                for k in range(HP):
                    for n in range(NPG):
                        c0 = (k % 2) * PAST + n * P
                        last = nc.tensor.transpose(kt[:, k // 2, c0:c0 + P], k_pages[:, b, n, k * P:(k + 1) * P], ps.ident[:])
                last.then_inc(k_turned, 1)

            def score(i, b):
                pe.wait_ge(sticks, done(i, b - 2))
                pe.wait_ge(placed, i * RING + (b + 1))
                pe.wait_ge(k_taken, i * (4 * RING) + (b * 4 + 4 + CR))
                for k in range(HP):
                    last = nc.tensor.matmul(z[:, b % 2, 0:NK], q_diag[:, b % 2, k, :], k_t[:, b % 2, k, :], start=k == 0, stop=k == HP - 1)
                last.then_inc(scored, 1)

            def turn_w(i, b):
                pe.wait_ge(weighed, done(i, b))
                pe.wait_ge(w_taken, done(i, b - 1))
                for n in range(NPG):
                    nc.tensor.transpose(wt[:, 0, n * P:(n + 1) * P], w[:, b % 2, n * P:(n + 1) * P], ps.ident[:])
                nc.tensor.transpose(wt[0:NS, 0, NPG * P:(NPG + 1) * P], w[:, b % 2, PAST:NK], ps.ident[:]).then_inc(w_turned, 1)

            def attend(i, b):
                pe.wait_ge(w_taken, done(i, b))
                pe.wait_ge(gated, done(i, b - 1))
                pe.wait_ge(v_loaded[b], i * (16 * NPG) + 16 * NPG)
                for k in range(HP):
                    dst = out[:, 0, k * 2 * DS:(k + 1) * 2 * DS]
                    cols = slice(k * 2 * DS, (k + 1) * 2 * DS)
                    for n in range(NPG):
                        nc.tensor.matmul(dst, v_pages[:, b, n, k * P:(k + 1) * P], w_t[:, b % 2, n, cols], start=n == 0, stop=False)
                    last = nc.tensor.matmul(dst, new_rows[:, 2, k * P:(k + 1) * P], w_t[0:NS, b % 2, NPG, cols], start=False, stop=True)
                last.then_inc(attended, 1)

            def step(i, b, last):
                turn_w(i, b)
                if not (last and b + 1 >= RING):
                    score(*ahead(i, b, 1))
                if not (last and b + 2 >= RING):
                    turn_k(*ahead(i, b, 2))
                attend(i, b)

            turn_k(0, 0)
            score(0, 0)
            turn_k(0, 1)
            with pe.Fori(0, TURNS - 1) as i:
                for b in range(RING):
                    step(i, b, False)
            for b in range(RING):
                step(TURNS - 1, b, True)
            pe.wait_ge(gated, DB + CR)
            for k in range(HP):
                last = nc.tensor.transpose(kt[0:NS, k // 4, (k % 4) * P:(k % 4 + 1) * P], o_t[:, k, :], ps.ident[:])
            last.then_inc(back, 1)

        @block.scalar
        def _(act):
            act.sem_inc(sticks, CR)
            act.sem_inc(k_taken, CR)
            act.wait_ge(cleared, 2)
            act.wait_ge(new_turned, 3)
            nc.scalar.copy(q_t[:].rearrange("p k c -> p (k c)"), kt[:, 0, :]).then_inc(new_taken, 1)
            for n in range(2):
                nc.scalar.copy(k_t[:, n, :, PAST:NK], kt[:, 1, :].rearrange("p (k c) -> p k c", k=HP)).then_inc(new_taken, 1)
            nc.scalar.copy(g_t[:].rearrange("p k c -> p (k c)"), kt[:, 2, :]).then_inc(new_taken, 1)

            def take_k(i, b):
                act.wait_ge(k_turned, done(i, b))
                act.wait_ge(scored, done(i, b - 2))
                for q in range(4):
                    nc.scalar.copy(k_t[:, b % 2, 2 * q:2 * q + 2, 0:PAST], kt[:, q, :].rearrange("p (k c) -> p k c", k=2)).then_inc(k_taken, 1)

            def stick(i, b):
                act.wait_ge(scored, done(i, b))
                act.wait_ge(weighed, done(i, b - 2))
                nc.scalar.activation(keep[:, b % 2], z[:, b % 2, 0:NK], ACT.Sigmoid, scale=-(DH ** -0.5), bias=bias[:, 1:2])
                nc.scalar.activation(take[:, b % 2], z[:, b % 2, 0:NK], ACT.Sigmoid, scale=DH ** -0.5, bias=bias[:, 0:1]).then_inc(sticks, 1)

            def step(i, b, last):
                if not (last and b + 1 >= RING):
                    stick(*ahead(i, b, 1))
                if not (last and b + 2 >= RING):
                    take_k(*ahead(i, b, 2))

            take_k(0, 0)
            stick(0, 0)
            take_k(0, 1)
            with act.Fori(0, TURNS - 1) as i:
                for b in range(RING):
                    step(i, b, False)
            for b in range(RING):
                step(TURNS - 1, b, True)
            act.wait_ge(back, 1)
            for n in range(2):
                nc.scalar.copy(o_rows[:, n * NB:(n + 1) * NB], kt[0:NS, n, :]).then_inc(back_taken, 1)

        @block.vector
        def _(dve):
            for s in (weighed, w_taken, gated):
                dve.sem_inc(s, CR)
            nc.vector.memset(after_key[:], 1.0)
            dve.wait_ge(new_turned, 4)
            nc.vector.tensor_copy(bias[:, 0:1], out[:, 0, 0:1])
            nc.vector.tensor_scalar(bias[:, 1:2], out[:, 0, 0:1], -1.0, None, ALU.mult).then_inc(cleared, 1)
            dve.wait_ge(cleared, 2)
            dve.wait_ge(new_taken, 4)

            def place(i, b):
                dve.wait_ge(scored, done(i, b - 2))
                for hh in range(2):
                    part = slice(hh * DH, (hh + 1) * DH)
                    flat = q_diag[part, b % 2].rearrange("p k c -> p (k c)")[:, hh * DS:]
                    dst = bass.AP(flat.tensor, flat.offset, [list(flat.ap[0]), [P + 2 * DS, HP], [1, DS]])
                    last = nc.vector.tensor_scalar(dst, q_t[part, :, bass.ds(i * (RING * DS) + b * DS, DS)], 1.0, None, ALU.mult)
                last.then_inc(placed, 1)

            def weigh(i, b):
                dve.wait_ge(sticks, done(i, b))
                dve.wait_ge(scanned, i * (2 * RING) + (2 * b + 1))
                seq = bass.ds(i * RING + b, 1)
                for buf, n, op in ((keep, 0, ALU.max), (take, 1, ALU.mult)):
                    last = nc.vector.tensor_tensor(buf[:, b % 2, PAST:NK], buf[:, b % 2, PAST:NK],
                                                   hidden[:, n, seq, :].rearrange("p o c -> p (o c)"), op)
                last.then_inc(scanned, 1)
                dve.wait_ge(scanned, i * (2 * RING) + (2 * b + 2))
                k = keep[:, b % 2]
                nc.vector.tensor_tensor_scan(after_key[:, b % 2, 0:NK][:, ::-1], k[:, ::-1], k[:, ::-1], 1.0, ALU.mult, ALU.bypass).then_inc(scanned, 1)
                dve.wait_ge(scanned, i * (2 * RING) + (2 * b + 3))
                dve.wait_ge(w_turned, done(i, b - 2))
                nc.vector.tensor_tensor(w[:, b % 2], take[:, b % 2], after_key[:, b % 2, 1:NK + 1], ALU.mult).then_inc(weighed, 1)

            def take_w(i, b):
                dve.wait_ge(w_turned, done(i, b))
                dve.wait_ge(attended, done(i, b - 2))
                nc.vector.tensor_copy(w_t[:, b % 2, 0:NPG], wt[:, 0, 0:NPG * P].rearrange("p (n c) -> p n c", n=NPG))
                nc.vector.tensor_copy(w_t[0:NS, b % 2, NPG], wt[0:NS, 0, NPG * P:(NPG + 1) * P]).then_inc(w_taken, 1)

            def gate(i, b):
                dve.wait_ge(attended, done(i, b))
                for hh in range(2):
                    part = slice(hh * DH, (hh + 1) * DH)
                    src = out[part, 0, 0:HP * 2 * DS].rearrange("p (k a i) -> p k a i", k=HP, a=2)[:, :, hh, :]
                    cols = bass.ds(i * (RING * DS) + b * DS, DS)
                    last = nc.vector.tensor_tensor(o_t[part, :, cols], src, g_t[part, :, cols], ALU.mult)
                last.then_inc(gated, 1)

            dve.sem_inc(scanned, 1)
            place(0, 0)
            place(0, 1)
            weigh(0, 0)

            def step(i, b, last):
                take_w(i, b)
                if not (last and b + 2 >= RING):
                    place(*ahead(i, b, 2))
                if not (last and b + 1 >= RING):
                    weigh(*ahead(i, b, 1))
                gate(i, b)

            with dve.Fori(0, TURNS - 1) as i:
                for b in range(RING):
                    step(i, b, False)
            for b in range(RING):
                step(TURNS - 1, b, True)


def outward(nc, t_in, ps, tag, rows_in, first, w_gain, layer, x, finish):
    w_rows, KT = first.w, first.KT
    ctx = ExitStack()
    with ctx:
        def sb(name, shape, dt=F32):
            return ctx.enter_context(nc.sbuf_tensor(f"{tag}_{name}", shape, dt))

        sem = semaphores(nc, ctx, tag)

        NH = D // NB
        AHEAD = 4
        GR = KT // 4
        SPLITS = 4
        KS = KT // SPLITS
        SLOTS_W = KT + AHEAD
        w_hi = sb("w_hi", [P, SLOTS_W, NB], F32R)
        second_lo, second_raw = overlaid(nc, ctx, f"{tag}_w_lo1", f"{tag}_w_raw1", [P, KT, NB])
        w_lo, w_raw = [first.lo, second_lo], [first.raw, second_raw]
        selector = sb("selector", [NC, P + NS])
        gate_p = sb("gate_p", [P, D])
        gate_s = sb("gate_s", [NS, D])
        a = sb("a", [P, KT * P])
        a_hi = sb("a_hi", [P, 2, KT, P], F32R)
        a_lo = sb("a_lo", [P, 2, KT, P], F32R)
        scaled = sb("scaled", [P, 2, NB])
        tr = ctx.enter_context(nc.psum_tensor(f"{tag}_tr", [P, 4, NB], F32))
        acc = ctx.enter_context(nc.psum_tensor(f"{tag}_acc", [P, 2, NB], F32))
        spread = ctx.enter_context(nc.psum_tensor(f"{tag}_spread", [P, 2, NB], F32))
        x_loaded, a_loaded = [sem("x_loaded0"), sem("x_loaded1")], sem("a_loaded")
        w_loaded = [sem(f"w_loaded{q}") for q in range(SPLITS)]
        hi_s, lo_s, gate_s_s, gate_taken = sem("w_hi_s"), sem("w_lo_s"), sem("gate_spread"), sem("gate_taken")
        turned, a_hi_s, a_lo_s, made, scaled_s, added = (sem("turned"), sem("a_hi_s"), sem("a_lo_s"), sem("made"),
                                                         sem("scaled_s"), sem("added"))
        assert nc.sbuf_base <= nc.sbuf_top - KT * NB * 4
        stored, half_added, selector_loaded = sem("stored"), sem("half_added"), sem("selector_loaded")
        block = ctx.enter_context(nc.Block())
        CR = 2

        def slot(n, k):
            return (n * KT + k) % SLOTS_W

        @block.sync
        def _(sp):
            w = w_rows.rearrange("(k p) n -> p k n", p=P)

            def load_second():
                for q in range(SPLITS):
                    part = slice(KS * q, KS * (q + 1))
                    sp.dma_start(w_raw[1][:, part, :], w[:, part, NB:2 * NB]).then_inc(w_loaded[q], 16)

            def load_rows(n, first, end):
                with sp.Fori(first, end) as t:
                    sp.wait_ge(turned, t + (n * NT + CR))
                    sp.dma_start(a[:], rows_in[bass.ds(t * P, P), :]).then_inc(a_loaded, 16)

            sp.dma_start(selector[:], t_in["selector"]).then_inc(selector_loaded, 16)
            sp.dma_start(a[:], rows_in[0:P, :]).then_inc(a_loaded, 16)
            for n in range(NH):
                if finish.load is not None:
                    finish.load(sp, x[:, :, n * NB:(n + 1) * NB], n, x_loaded[n])
                load_rows(n, 1 - n, 3)
                if n == 0:
                    load_second()
                load_rows(n, 3, NPT)
                sp.wait_ge(turned, NPT + n * NT + CR)
                sp.dma_start(a[0:NS, :], rows_in[SEQ:SEQ + NS, :]).then_inc(a_loaded, 16)

        @block.tensor
        def _(pe):
            pe.sem_inc(turned, CR)
            pe.sem_inc(made, CR)
            pe.wait_ge(selector_loaded, 16)
            for n in range(NH):
                nc.tensor.matmul(spread[:, n, :], selector[:, 0:P], ps.gate[:, layer, n * NB:(n + 1) * NB],
                                 start=True, stop=True).then_inc(gate_s_s, 1)
            pe.wait_ge(gate_taken, 2)
            for n in range(NH):
                nc.tensor.matmul(spread[0:NS, n, :], selector[:, P:P + NS], ps.gate[:, layer, n * NB:(n + 1) * NB],
                                 start=True, stop=True).then_inc(gate_s_s, 1)

            def turn(n, j):
                pe.wait_ge(a_loaded, (j + (n * NT + 1)) * 16)
                pe.wait_ge(a_lo_s, (j + (n * NT)) * GR + CR)
                for k in range(KT):
                    last = nc.tensor.transpose(tr[:, k // 4, (k % 4) * P:(k % 4 + 1) * P], a[:, k * P:(k + 1) * P], ps.ident[:])
                last.then_inc(turned, 1)

            def multiply(n, b, j, first=False, sample=False):
                pe.wait_ge(a_lo_s, (j + (n * NT + 1)) * GR + CR)
                pe.wait_ge(added, j + (n * NT + CR - 1))
                for k in range(KT):
                    if first and k % KS == 0:
                        pe.wait_ge(lo_s, n * SPLITS + k // KS + 1)
                    hi = w_hi[:, slot(n, k), :]
                    nc.tensor.matmul(acc[:, b, :], a_hi[:, b, k, :], hi, start=k == 0, stop=False)
                    last = nc.tensor.matmul(acc[:, b, :], a_hi[:, b, k, :], w_lo[n][:, k, :], start=False,
                                            stop=sample and k == KT - 1)
                    if not sample:
                        last = nc.tensor.matmul(acc[:, b, :], a_lo[:, b, k, :], hi, start=False, stop=k == KT - 1)
                last.then_inc(made, 1)

            def pair(n, i, first=False):
                turn(n, i * 2 + 1)
                multiply(n, 0, i * 2, first)
                turn(n, i * 2 + 2)
                multiply(n, 1, i * 2 + 1)

            for n in range(NH):
                turn(n, 0)
                pair(n, 0, True)
                with pe.Fori(1, NPT // 2) as i:
                    pair(n, i)
                multiply(n, 0, NPT, sample=True)

        @block.scalar
        def _(act):
            act.wait_ge(gate_s_s, 2)
            nc.scalar.copy(gate_p[:], spread[:].rearrange("p a b -> p (a b)")).then_inc(gate_taken, 2)
            act.wait_ge(gate_s_s, 4)
            nc.scalar.copy(gate_s[:], spread[0:NS].rearrange("p a b -> p (a b)")).then_inc(gate_taken, 1)

            def take(n, b, j, r=P):
                act.wait_ge(turned, j + (n * NT + CR + 1))
                act.wait_ge(made, j + (n * NT + CR - 1))
                for q in range(GR):
                    nc.scalar.copy(a_hi[:, b, 4 * q:4 * q + 4, 0:r], tr[:, q, :].rearrange("p (k c) -> p k c", k=4)[:, :, 0:r]).then_inc(a_hi_s, 1)

            def split(n, q):
                if n:
                    act.wait_ge(w_loaded[q], 16)
                for k in range(KS * q, KS * (q + 1)):
                    scale = ps.ret_g[:, k:k + 1] if w_gain else 1.0
                    last = nc.scalar.activation(w_hi[:, slot(n, k), :], w_raw[n][:, k, :], ACT.Copy, scale=scale)
                last.then_inc(hi_s, 1)

            for n in range(NH):
                if n:
                    act.wait_ge(made, n * NT + CR)
                for q in range(AHEAD // KS if n else 0, SPLITS):
                    if q == SPLITS - 2:
                        take(n, 0, 0)
                    split(n, q)
                with act.Fori(0, NPT // 2 - 1) as i:
                    take(n, 1, i * 2 + 1)
                    take(n, 0, i * 2 + 2)
                take(n, 1, NPT - 1)
                take(n, 0, NPT, NS)
                if n == 0:
                    for q in range(AHEAD // KS):
                        split(1, q)

        @block.vector
        def _(dve):
            dve.sem_inc(a_lo_s, CR)
            dve.sem_inc(added, CR)
            dve.wait_ge(gate_taken, 3)

            def take(n, b, j, sample=False):
                for q in range(GR):
                    dve.wait_ge(a_hi_s, (j + n * NT) * GR + (q + 1))
                    r = NS if sample else P
                    hi = a_hi[:, b, 4 * q:4 * q + 4, 0:r]
                    dst = a_hi[:, b, 4 * q:4 * q + 4, NS:P] if sample else a_lo[:, b, 4 * q:4 * q + 4, :]
                    nc.vector.tensor_tensor(dst, tr[:, q, :].rearrange("p (k c) -> p k c", k=4)[:, :, 0:r], hi.bitcast(F32),
                                            ALU.subtract).then_inc(a_lo_s, 1)

            def add(n, b, j):
                xs = x[:, j, n * NB:(n + 1) * NB] if isinstance(j, int) else x[:, bass.ds(j, 1), n * NB:(n + 1) * NB].rearrange("p o c -> p (o c)")
                dve.wait_ge(made, j + (n * NT + CR + 1))
                nc.vector.tensor_tensor(scaled[:, b, :], acc[:, b, :], gate_p[:, n * NB:(n + 1) * NB], ALU.mult).then_inc(scaled_s, 1)
                dve.wait_ge(scaled_s, j + (n * NT + 1))
                nc.vector.tensor_tensor(xs, xs, scaled[:, b, :], ALU.add).then_inc(added, 1)

            def add_sample(n):
                xs = x[0:NS, NPT, n * NB:(n + 1) * NB]
                dve.wait_ge(made, (n + 1) * NT + CR)
                dve.wait_ge(added, n * NT + NPT + CR)
                for part in range(2):
                    last = nc.vector.tensor_tensor(scaled[0:NS, part, :], acc[part * NS:(part + 1) * NS, 0, :],
                                                   gate_s[:, n * NB:(n + 1) * NB], ALU.mult)
                last.then_inc(scaled_s, 1)
                dve.wait_ge(scaled_s, (n + 1) * NT)
                nc.vector.tensor_tensor(xs, xs, scaled[0:NS, 0, :], ALU.add).then_inc(half_added, 1)
                dve.wait_ge(half_added, n + 1)
                nc.vector.tensor_tensor(xs, xs, scaled[0:NS, 1, :], ALU.add).then_inc(added, 1)

            def split(n, q):
                dve.wait_ge(hi_s, n * SPLITS + q + 1)
                for k in range(KS * q, KS * (q + 1)):
                    hi = w_hi[:, slot(n, k), :].bitcast(F32)
                    if w_gain:
                        last = nc.vector.scalar_tensor_tensor(w_lo[n][:, k, :], w_raw[n][:, k, :], ps.ret_g[:, k:k + 1], hi,
                                                              ALU.mult, ALU.subtract)
                    else:
                        last = nc.vector.tensor_tensor(w_lo[n][:, k, :], w_raw[n][:, k, :], hi, ALU.subtract)
                last.then_inc(lo_s, 1)

            for n in range(NH):
                for q in range(AHEAD // KS if n else 0, SPLITS):
                    if q == SPLITS - 2:
                        take(n, 0, 0)
                    split(n, q)
                if finish.load is not None:
                    dve.wait_ge(x_loaded[n], 32)
                with dve.Fori(0, NPT // 2 - 1) as i:
                    take(n, 1, i * 2 + 1)
                    add(n, 0, i * 2)
                    take(n, 0, i * 2 + 2)
                    add(n, 1, i * 2 + 1)
                take(n, 1, NPT - 1)
                add(n, 0, NPT - 2)
                take(n, 0, NPT, True)
                if n == 0:
                    for q in range(AHEAD // KS):
                        split(1, q)
                add(n, 1, NPT - 1)
                add_sample(n)

        if finish.store is not None:
            @block.gpsimd
            def _(pool):
                finish.store(pool, x, added, stored, CR)


class Finish:
    def __init__(self, load=None, store=None):
        self.load, self.store = load, store


def reload_x(t_in):
    def load(sp, x_cols, n, sem):
        cols = slice(n * NB, (n + 1) * NB)
        sp.dma_start(x_cols[:, 0:NPT, :], t_in["x_prompt"][0].rearrange("(t p) d -> p t d", p=P)[:, :, cols]).then_inc(sem, 16)
        sp.dma_start(x_cols[0:NS, NPT, :], t_in["x_sample"].rearrange("b i d -> (b i) d")[:, cols]).then_inc(sem, 16)
    return load


def store_y(t_out):
    def store(pool, x, added, stored, CR):
        with pool.Fori(0, NPT) as t:
            pool.wait_ge(added, t + (NT + CR + 1))
            pool.dma_start(t_out["y_prompt"][0][bass.ds(t * P, P), :], x[:, bass.ds(t, 1), :].rearrange("p o d -> p (o d)")).then_inc(stored, 16)
        pool.wait_ge(added, 2 * NT + CR)
        pool.dma_start(t_out["y_sample"].rearrange("b i d -> (b i) d"), x[0:NS, NPT, :]).then_inc(stored, 16)
        pool.wait_ge(stored, 16 * NT)
    return store


def shared_kv_and_queries(nc, t_in, t_out, ps, x):
    ctx = ExitStack()
    with ctx:
        def sb(name, shape, dt=F32):
            return ctx.enter_context(nc.sbuf_tensor(f"kq_{name}", shape, dt))

        sem = semaphores(nc, ctx, "kq")

        def out_rows(name):
            return (t_out[name + "_prompt"][0].rearrange("s h d -> s (h d)"),
                    t_out[name + "_sample"].rearrange("b i h d -> (b i) (h d)"))

        def scratch(ap):
            return ap[0:SEQ, :], ap[SEQ:SEQ + NS, :]

        h_hi = sb("h_hi", [P, KD, SEQ + 2 * NS], F32R)
        h_lo = sb("h_lo", [P, KD, SEQ], F32R)
        w_hi = sb("w_hi", [P, 2, KD, NB], F32R)
        pairs = [overlaid(nc, ctx, f"kq_w_lo{n}", f"kq_w_raw{n}", [P, KD, NB]) for n in range(2)]
        w_lo, w_raw = [p[0] for p in pairs], [p[1] for p in pairs]
        HC = NB // DH
        y = sb("y", [P, 2, NB])
        squares = sb("squares", [P, 2, NB])
        ss = sb("ss", [P, 2, HC])
        root = sb("root", [P, 2, HC])
        rstd = sb("rstd", [P, 2, HC])
        out = sb("out", [P, 2, NB])
        xn = sb("xn", [P, 2, D])
        full = sb("full", [P, 2, KD, P])
        small = sb("small", [P, 3, NT])
        acc = ctx.enter_context(nc.psum_tensor("kq_acc", [P, 4, NB], F32))
        tr = ctx.enter_context(nc.psum_tensor("kq_tr", [P, 4, NB], F32))
        w_loaded = [sem("w_loaded0"), sem("w_loaded1")]
        hi_s, lo_s, made = sem("w_hi_s"), sem("w_lo_s"), sem("made")
        taken, squared, summed, rooted, normed, ready = (sem("taken"), sem("squared"), sem("summed"), sem("rooted"),
                                                         sem("normed"), sem("ready"))
        own, upper, merged = sem("own"), sem("upper"), sem("merged")
        stored = [sem("stored0"), sem("stored1")]
        ada_loaded, ada_used = [sem("ada_loaded0"), sem("ada_loaded1")], sem("ada_used")
        bias_loaded, mod_added, mod_turned, mod_ready = sem("bias_loaded"), sem("mod_added"), sem("mod_turned"), sem("mod_ready")

        k_out, v_out, q_out, g_out = out_rows("k"), out_rows("v"), scratch(ps.q_rows), scratch(ps.g_rows)
        w_kv, w_qg = t_in["w_kv"], t_in["sb_w_in"][0]
        chunks = [(w_kv, 2, None, ACT.Copy, v_out), (w_kv, 0, ps.k_gain, None, k_out),
                  (w_kv, 1, ps.k_gain, None, k_out), (w_kv, 3, None, ACT.Copy, v_out),
                  (w_qg, 2, None, ACT.Silu, g_out), (w_qg, 0, ps.q_gain, None, q_out),
                  (w_qg, 1, ps.q_gain, None, q_out), (w_qg, 3, None, ACT.Silu, g_out)]
        SWITCH = 4
        steps = [(c, t) for c in range(len(chunks)) for t in range(NT)]
        SPLITS = 4
        KS = KD // SPLITS
        LEAD = 4

        def normed_before(s):
            return len([1 for c, t in steps[:s] if chunks[c][2] is not None])

        def last_use(s):
            return 16 * (s // 2)

        def h_free(act, n, t):
            if n == 1:
                act.wait_ge(made, (SWITCH - 1) * NT + t + 1)

        def xn_free(act, n, t):
            if n == 1:
                act.wait_ge(mod_turned, 1)

        def slots_at(s):
            found = []
            if s + LEAD < SLOTS:
                found.append((0, s + LEAD))
            if (SWITCH - 1) * NT <= s < (SWITCH - 1) * NT + SLOTS:
                found.append((1, s - (SWITCH - 1) * NT))
            return found

        CG = 3
        ADA_FIRST, ADA_STEPS = NT, 2 * KD
        ADA_ADD = ADA_FIRST + ADA_STEPS
        xn_flat = xn[:].rearrange("p a b -> p (a b)")
        full_flat = full[:].rearrange("p a k c -> p (a k c)")

        def ada_tile(j):
            return (xn_flat, full_flat)[j % 2][:, 0:CG * NB]

        act_slot, pe_slot, dve_slot, rest_slot, _, h_ready = tile_preparation(
            nc, ps, sem, [1, 2], lambda t: x[0:rows(t), t, :], xn, full, squares[:].rearrange("p a b -> p (a b)"), small,
            lambda q: tr[:, 2 * (q % 2):2 * (q % 2) + 2, :].rearrange("p a (k c) -> p (a k) c", c=P), h_hi, h_lo,
            lambda act, t: None, xn_free, h_free)
        block = ctx.enter_context(nc.Block())

        @block.sync
        def _(sp):
            def load_ada(j):
                if j >= 2:
                    sp.wait_ge(ada_used, j - 1)
                k, c0 = j % KD, (j // KD) * CG * NB
                sp.dma_start(ada_tile(j), t_in["ada_w"][1][k * P:(k + 1) * P, c0:c0 + CG * NB]).then_inc(ada_loaded[j % 2], 16)

            for c, (w, n, _, _, _) in enumerate(chunks):
                if c >= 2:
                    sp.wait_ge(made, (c - 1) * NT)
                sp.dma_start(w_raw[c % 2][:], w.rearrange("(k p) n -> p k n", p=P)[:, :, n * NB:(n + 1) * NB]).then_inc(w_loaded[c % 2], 16)
                if c == 1:
                    sp.wait_ge(h_ready, NT)
                    load_ada(0)
                    load_ada(1)
                elif c == 2:
                    for j in range(2, KD + 2):
                        load_ada(j)
                elif c == 3:
                    for j in range(KD + 2, ADA_STEPS):
                        load_ada(j)
                    sp.wait_ge(ada_used, ADA_STEPS)
                    sp.dma_start(full_flat[0:NC, 0:2 * D], t_in["ada_b"][1:2, 0:2 * D].to_broadcast([NC, 2 * D])).then_inc(bias_loaded, 16)

        @block.tensor
        def _(pe):
            for i in range(LEAD):
                pe_slot(pe, 0, i)
            for s, (c, t) in enumerate(steps):
                if t == 0:
                    pe.wait_ge(lo_s, SPLITS * (c + 1))
                if c in (0, SWITCH):
                    pe.wait_ge(h_ready, (c // SWITCH) * NT + t + 1)
                if s >= 4:
                    pe.wait_ge(taken, s - 3)
                product(nc, acc[:, s % 4, :], h_hi, h_lo, w_hi[:, c % 2], w_lo[c % 2], t).then_inc(made, 1)
                if s == ADA_ADD + 3:
                    pe.wait_ge(mod_ready, 1)
                for n, i in slots_at(s):
                    pe_slot(pe, n, i)
                j = s - ADA_FIRST
                if 0 <= j < ADA_STEPS:
                    pe.wait_ge(ada_loaded[j % 2], 16 * (j // 2 + 1))
                    for g in range(CG):
                        last = nc.tensor.matmul(tr[32 * g:32 * g + NC, j // KD, :], ps.cond_t[:, j % KD, :],
                                                ada_tile(j)[:, g * NB:(g + 1) * NB], start=j % KD == 0, stop=j % KD == KD - 1,
                                                tile_position=(0, 32 * g))
                    last.then_inc(ada_used, 1)
                if s == ADA_ADD + 2:
                    pe.wait_ge(mod_added, 1)
                    for k in range(2 * KD):
                        last = nc.tensor.transpose(tr[:, 2, k * NC:(k + 1) * NC], xn_flat[0:NC, k * P:(k + 1) * P], ps.ident[0:NC, 0:NC])
                    last.then_inc(mod_turned, 1)

        @block.scalar
        def _(act):
            def split(c, q):
                act.wait_ge(w_loaded[c % 2], 16 * (c // 2 + 1))
                part = slice(KS * q, KS * (q + 1))
                nc.scalar.copy(w_hi[:, c % 2, part, :], w_raw[c % 2][:, part, :]).then_inc(hi_s, 1)

            for i in range(LEAD):
                act_slot(act, 0, i)
                if i >= 2:
                    split(0, 2 * i - 4)
                    split(0, 2 * i - 3)
            for s, (c, t) in enumerate(steps):
                for n, i in slots_at(s):
                    act_slot(act, n, i)
                r = rows(t)
                act.wait_ge(made, s + 1)
                if chunks[c][2] is not None:
                    m = normed_before(s)
                    if m >= 2:
                        act.wait_ge(normed, m - 1)
                        act.wait_ge(summed, m - 1)
                    if t < NPT:
                        nc.scalar.activation(squares[:, m % 2, :], acc[:, s % 4, :], ACT.Square).then_inc(squared, 1)
                        nc.scalar.copy(y[:, m % 2, :], acc[:, s % 4, :]).then_inc(taken, 1)
                    else:
                        act.wait_ge(merged, c + 1)
                        nc.scalar.activation(squares[0:r, m % 2, :], y[0:r, m % 2, :], ACT.Square).then_inc(squared, 1)
                        act.sem_inc(taken, 1)
                    act.wait_ge(summed, m + 1)
                    nc.scalar.activation(root[0:r, m % 2, :], ss[0:r, m % 2, :], ACT.Sqrt, scale=1.0 / DH,
                                         bias=ps.eps[0:r]).then_inc(rooted, 1)
                else:
                    if s >= 2:
                        act.wait_ge(stored[s % 2], last_use(s))
                    if t < NPT:
                        src = acc[:, s % 4, :]
                    else:
                        act.wait_ge(merged, c + 1)
                        src = out[0:r, s % 2, :]
                    nc.scalar.activation(out[0:r, s % 2, :], src, chunks[c][3]).then_inc(taken, 1)
                if 3 <= t < 3 + SPLITS and c + 1 < len(chunks):
                    split(c + 1, t - 3)

        @block.vector
        def _(dve):
            def split(c, q):
                dve.wait_ge(hi_s, SPLITS * c + q + 1)
                part = slice(KS * q, KS * (q + 1))
                nc.vector.tensor_tensor(w_lo[c % 2][:, part, :], w_raw[c % 2][:, part, :], w_hi[:, c % 2, part, :].bitcast(F32),
                                        ALU.subtract).then_inc(lo_s, 1)

            for i in range(LEAD):
                dve_slot(dve, 0, i)
                rest_slot(dve, 0, i)
                if i >= 2:
                    split(0, 2 * i - 4)
                    split(0, 2 * i - 3)
            for s, (c, t) in enumerate(steps):
                for n, i in slots_at(s):
                    dve_slot(dve, n, i)
                    rest_slot(dve, n, i)
                r = rows(t)
                if t == NPT:
                    dve.wait_ge(made, s + 1)
                    if chunks[c][2] is not None:
                        dve.wait_ge(normed, normed_before(s) - 1)
                        dst = y[0:r, normed_before(s) % 2, :]
                    else:
                        dve.wait_ge(stored[s % 2], last_use(s))
                        dst = out[0:r, s % 2, :]
                    nc.vector.tensor_copy(dst, acc[0:NS, s % 4, :]).then_inc(upper, 1)
                    dve.wait_ge(upper, c + 1)
                    nc.vector.tensor_tensor(dst, dst, acc[NS:P, s % 4, :], ALU.add).then_inc(merged, 1)
                if chunks[c][2] is not None:
                    m, head_gain = normed_before(s), chunks[c][2]

                    def heads(buf, i):
                        return buf[0:r, i % 2, :].rearrange("p (h d) -> p h d", h=HC)

                    dve.wait_ge(squared, m + 1)
                    nc.vector.tensor_reduce(ss[0:r, m % 2, :], heads(squares, m), AX.X, ALU.add).then_inc(summed, 1)
                    dve.wait_ge(rooted, m + 1)
                    nc.vector.reciprocal(rstd[0:r, m % 2, :], root[0:r, m % 2, :]).then_inc(own, 1)
                    dve.wait_ge(own, 2 * m + 1)
                    nc.vector.tensor_tensor(heads(squares, m), heads(y, m), rstd[0:r, m % 2, :].unsqueeze(2).to_broadcast([r, HC, DH]),
                                            ALU.mult).then_inc(own, 1)
                    dve.wait_ge(own, 2 * m + 2)
                    if s >= 2:
                        dve.wait_ge(stored[s % 2], last_use(s))
                    nc.vector.tensor_tensor(heads(out, s), heads(squares, m), head_gain[0:r].unsqueeze(1).to_broadcast([r, HC, DH]),
                                            ALU.mult).then_inc(ready, 1)
                    dve.sem_inc(normed, 1)
                if s == ADA_ADD:
                    dve.wait_ge(ada_used, ADA_STEPS)
                    dve.wait_ge(bias_loaded, 16)
                    for n in range(2 * CG):
                        src = tr[32 * (n % CG):32 * (n % CG) + NC, n // CG, :]
                        cols = slice(n * NB, (n + 1) * NB)
                        if n < 2 * D // NB:
                            last = nc.vector.tensor_tensor(xn_flat[0:NC, cols], src, full_flat[0:NC, cols], ALU.add)
                        else:
                            gate = ps.gate[:, 1, n * NB - 2 * D:(n + 1) * NB - 2 * D]
                            last = nc.vector.tensor_tensor(gate, src, gate, ALU.add)
                    last.then_inc(mod_added, 1)
                if s == ADA_ADD + 2:
                    dve.wait_ge(mod_turned, 1)
                    m = tr[:, 2, 0:2 * KD * NC].rearrange("p (s k c) -> p s k c", s=2, k=KD)
                    nc.vector.tensor_copy(ps.shift[:, 2, :, :], m[:, 0])
                    nc.vector.scalar_tensor_tensor(ps.gain[:, 2, :, :], m[:, 1], 1.0, ps.norm_g[:].unsqueeze(2).to_broadcast([P, KD, NC]),
                                                   ALU.add, ALU.mult).then_inc(mod_ready, 1)
                    dve.wait_ge(mod_ready, 1)
                if 3 <= t < 3 + SPLITS and c + 1 < len(chunks):
                    split(c + 1, t - 3)

        @block.gpsimd
        def _(pool):
            for s, (c, t) in enumerate(steps):
                r = rows(t)
                _, n, head_gain, _, dst = chunks[c]
                c0 = (n % 2) * NB
                if head_gain is not None:
                    pool.wait_ge(ready, normed_before(s + 1))
                else:
                    pool.wait_ge(taken, s + 1)
                r0 = t * P if t < NPT else 0
                pool.dma_start(dst[0 if t < NPT else 1][r0:r0 + r, c0:c0 + NB], out[0:r, s % 2, :]).then_inc(stored[s % 2], 16)
            for n in range(2):
                pool.wait_ge(stored[n], 16 * len([s for s in range(len(steps)) if s % 2 == n]))


def diagonal(buf, blocks, width, n):
    flat = buf[:].rearrange("p b c -> p (b c)")
    return bass.AP(flat.tensor, flat.offset, [list(flat.ap[0]), [width + n, blocks], [1, n]])


def at_top(nc, size):
    assert nc.sbuf_base <= nc.sbuf_top - size
    return nc.sbuf_top - size


def input_rows(t_in, t):
    return t_in["x_prompt"][0, t * P:(t + 1) * P, :] if t < NPT else t_in["x_sample"].rearrange("b i d -> (b i) d")


class FirstTiles:
    XR = 3

    def __init__(self, nc):
        at = at_top(nc, 2 * KD * (2 * DK + 2 * DV) * 4)
        self.x_ring = nc.alloc_sbuf_tensor_at("x_ring", [P, self.XR, D], F32, offset=at)

    def load(self, sp, t_in, loaded):
        for t in range(self.XR):
            sp.dma_start(self.x_ring[:, t, :], input_rows(t_in, t)).then_inc(loaded, 16)
        sp.wait_ge(loaded, 16 * self.XR)


class FirstWeights:

    def __init__(self, nc, tag, w_rows, KT):
        self.w, self.KT = w_rows, KT
        at = at_top(nc, KT * NB * 4)
        self.lo = nc.alloc_sbuf_tensor_at(f"{tag}_w_lo0", [P, KT, NB], F32R, offset=at)
        self.raw = nc.alloc_sbuf_tensor_at(f"{tag}_w_raw0", [P, KT, NB], F32, offset=at)

    def load(self, sp, loaded):
        sp.dma_start(self.raw[:], self.w.rearrange("(k p) n -> p k n", p=P)[:, :, 0:NB]).then_inc(loaded, 16)
        sp.wait_ge(loaded, 16)


def overlaid(nc, ctx, name, raw_name, shape):
    at = nc.sbuf_base
    lo = ctx.enter_context(nc.sbuf_tensor(name, shape, F32R))
    return lo, nc.alloc_sbuf_tensor_at(raw_name, shape, F32, offset=at)


def shape_constants():
    import numpy as np

    f = np.float32
    half = DK // 2
    inv_freq = 10000.0 ** (-np.arange(half, dtype=f) / f(half))
    pos = np.zeros((P, NT), f)
    pos[:, :NPT] = np.arange(SEQ).reshape(NPT, P).T
    pos[:, NPT] = PAST + np.arange(P) % DS
    ang = (pos[:, :, None] * inv_freq.astype(f)).astype(f)
    cos, sin = np.cos(ang), np.sin(ang)
    log_gamma = np.log1p(-np.exp2(-5.0 - np.arange(H)))
    decays = np.zeros((P, 2, 3, H))
    for kind, chunk in ((0, P), (1, DS)):
        i = (np.arange(P) % chunk)[:, None]
        decays[:, kind, 0] = np.exp(log_gamma * (i + 1.0))
        decays[:, kind, 1] = np.exp(-log_gamma * (i + 1.0)) * DK ** -0.5
        decays[:, kind, 2] = np.exp(log_gamma * chunk)
    j, i = np.arange(P)[:, None], np.arange(P)[None]
    causal = np.zeros((P, P + NS))
    causal[:, :P] = j <= i
    js, is_ = np.arange(NS)[:, None], np.arange(NS)[None]
    causal[:NS, P:] = (js <= is_) & (js // DS == is_ // DS)
    selector = np.zeros((NC, P + NS))
    selector[0, :P] = 1
    for b in range(DB):
        selector[1 + b, P + b * DS:P + (b + 1) * DS] = 1
    own_rows = (np.arange(NS)[:, None] // DS == np.arange(DB)[None])
    q, s = np.arange(P)[:, None], np.arange(P)[None]
    hidden = (s >= q)
    hq = np.arange(P) % DS
    tok = np.arange(NS)
    hidden_s = np.ones((P, DB, NS))
    for b in range(DB):
        hidden_s[:, b] = ~((tok[None] // DS == b) & (tok[None] % DS < hq[:, None]))
    out = {
        "ident": np.eye(P), "selector": selector, "own_rows": own_rows, "causal": causal, "decays": decays,
        "rope_cos": np.concatenate([cos, cos], -1), "rope_sin": np.concatenate([-sin, sin], -1),
        "head_rows": np.arange(AH)[:, None] == np.arange(P)[None] // DS, "far_below": hidden * FAR, "hidden_s": np.stack([hidden_s, 1 - hidden_s], 1),
    }
    return {k: np.ascontiguousarray(x, dtype=f) for k, x in out.items()}


INPUTS = ["x_prompt", "x_sample", "state_ret", "cache_k", "cache_v", "page_table", "c_prompt", "c_sample", "ada_w",
          "ada_b", "norm_g", "ret_w_in", "ret_norm_g", "ret_w_out", "kv_norm_g", "w_kv", "sb_q_g", "sb_k_g",
          "sb_w_in", "sb_w_out", "sb_bias"]
OUTPUTS = {"y_prompt": (1, SEQ, D), "y_sample": (DB, DS, D), "st_prompt": (1, 1, H, DK, DV),
           "st_sample": (1, DB, H, DK, DV), "k_prompt": (1, SEQ, AH, DH), "v_prompt": (1, SEQ, AH, DH),
           "k_sample": (DB, DS, AH, DH), "v_sample": (DB, DS, AH, DH)}


def kernel(**inputs):
    import numpy as np
    import concourse.bacc as bacc
    from concourse.bass_utils import run_bass_kernel_spmd

    nc = bacc.Bacc("TRN2", target_bir_lowering=False, num_devices=1)
    arrays = {name: np.ascontiguousarray(inputs[name]) for name in INPUTS}
    arrays.update(shape_constants())
    t_in = {name: nc.dram_tensor("in_" + name, a.shape, mybir.dt.from_np(a.dtype), kind="ExternalInput").ap()
            for name, a in arrays.items()}
    t_out = {name: nc.dram_tensor("out_" + name, shape, F32, kind="ExternalOutput").ap() for name, shape in OUTPUTS.items()}
    build_program(nc, t_in, t_out)
    results = run_bass_kernel_spmd(nc, [{"in_" + n: a for n, a in arrays.items()}], core_ids=[0]).results[0]
    return tuple(results["out_" + name] for name in OUTPUTS)
```
